# Optimizing a Trainium2 kernel written in Bass

```python
import jax
import jax.numpy as jnp
from jax import lax
import numpy as np
import jax, jax.numpy as jnp

D_MODEL = 1024
BATCH = 1
SEQ = 256
DEPTH = 2

HEAD_DIM = 64
BLOCK = 128
A_HEADS = 8
A_KV_HEADS = 2
WINDOW = 128
B_HEADS = 8
FOX_BIAS_INIT = 3.0
C_HEADS = 8
IDX_HEADS = 4
IDX_DIM = 64
DSA_TOPK_MAX = 256
D_HEADS = 8
MLA_Q_RANK = 256
MLA_KV_RANK = 128
MLA_NOPE = 64
MLA_ROPE = 32
MLA_V = 64
ROPE_THETA = 10000.0
N_EXPERTS = 16
N_GROUPS = 4
EXPERTS_PER_GROUP = N_EXPERTS // N_GROUPS
TOPK_GROUPS = 1
TOPK_EXPERTS = 2
D_FF_EXPERT = 512
LN_EPS = 1e-5
RMS_EPS = 1e-6
ALPHA = (2 * DEPTH) ** 0.25
BETA = (8 * DEPTH) ** -0.25
N_EVEN = (DEPTH + 1) // 2
N_ODD = DEPTH // 2
MIX_WIDTH = A_HEADS * HEAD_DIM + B_HEADS * HEAD_DIM
EVEN_SIZES = (A_HEADS * HEAD_DIM, A_KV_HEADS * HEAD_DIM, A_KV_HEADS * HEAD_DIM,
              B_HEADS * HEAD_DIM, B_HEADS * HEAD_DIM, B_HEADS * HEAD_DIM, B_HEADS)
EVEN_VALUE_SLOTS = (2, 5)
ODD_SIZES = (C_HEADS * HEAD_DIM, HEAD_DIM, HEAD_DIM, IDX_HEADS * IDX_DIM, IDX_DIM, IDX_HEADS,
             MLA_Q_RANK, MLA_KV_RANK, MLA_ROPE)
ODD_VALUE_SLOTS = (2,)


def split_cols(h, sizes):
    out, start = [], 0
    for n in sizes:
        out.append(h[..., start:start + n])
        start += n
    return out

def layer_norm(x, g, b):
    xf = x.astype(jnp.float32)
    mu = jnp.mean(xf, -1, keepdims=True)
    var = jnp.mean(jnp.square(xf - mu), -1, keepdims=True)
    return ((xf - mu) * lax.rsqrt(var + LN_EPS)).astype(x.dtype) * g + b

def rms_norm(x, g):
    xf = x.astype(jnp.float32)
    return (xf * lax.rsqrt(jnp.mean(jnp.square(xf), -1, keepdims=True) + RMS_EPS)).astype(x.dtype) * g

def alibi_slopes(n):
    return 2.0 ** (-8.0 * jnp.arange(1, n + 1, dtype=jnp.float32) / n)

def rope(x, pos):
    half = x.shape[-1] // 2
    inv = ROPE_THETA ** (-jnp.arange(half, dtype=jnp.float32) / half)
    ang = pos.astype(jnp.float32)[:, None] * inv[None, :]
    shape = (1, x.shape[1]) + (1,) * (x.ndim - 3) + (half,)
    cos = jnp.cos(ang).reshape(shape).astype(x.dtype)
    sin = jnp.sin(ang).reshape(shape).astype(x.dtype)
    x1, x2 = x[..., :half], x[..., half:]
    return jnp.concatenate([x1 * cos - x2 * sin, x1 * sin + x2 * cos], axis=-1)

def sliding_window_sink_attention(q, k, v, sinks):
    B, S, Hq, d = q.shape
    Hkv = k.shape[2]
    G = Hq // Hkv
    nb = S // BLOCK
    qb = q.reshape(B, nb, BLOCK, Hkv, G, d)

    def band(a):
        a = a.reshape(B, nb, BLOCK, Hkv, d)
        prev = jnp.concatenate([jnp.zeros_like(a[:, :1]), a[:, :-1]], axis=1)
        return jnp.concatenate([prev, a], axis=2)

    k_band, v_band = band(k), band(v)
    logits = jnp.einsum('bnqkgd,bnskd->bnkgqs', qb, k_band,
                        preferred_element_type=jnp.float32) * d ** -0.5
    blk = jnp.arange(nb)[:, None, None]
    t = blk * BLOCK + jnp.arange(BLOCK)[None, :, None]
    s = (blk - 1) * BLOCK + jnp.arange(2 * BLOCK)[None, None, :]
    dist = t - s
    valid = (dist >= 0) & (dist < WINDOW) & (s >= 0)
    slopes = alibi_slopes(Hq).reshape(Hkv, G)
    logits = logits - slopes[:, :, None, None] * dist[:, None, None].astype(jnp.float32)
    logits = jnp.where(valid[:, None, None], logits, -jnp.inf)
    sink = jnp.broadcast_to(sinks.astype(jnp.float32).reshape(Hkv, G, 1, 1), logits.shape[:-1] + (1,))
    p = jax.nn.softmax(jnp.concatenate([logits, sink], axis=-1), axis=-1)[..., :-1].astype(v.dtype)
    out = jnp.einsum('bnkgqs,bnskd->bnqkgd', p, v_band)
    return out.reshape(B, S, Hq * d)

def causal_block_attention(q, k, v, log_forget=None):
    B, S, H, dk = q.shape
    dv = v.shape[-1]
    nb = S // BLOCK
    scale = dk ** -0.5
    pos = jnp.arange(S)
    cum = None if log_forget is None else jnp.cumsum(log_forget, axis=1).swapaxes(1, 2)

    def one_block(i):
        q_i = lax.dynamic_slice_in_dim(q, i * BLOCK, BLOCK, axis=1)
        t = i * BLOCK + jnp.arange(BLOCK)
        logits = jnp.einsum('bqhd,bshd->bhqs', q_i, k, preferred_element_type=jnp.float32) * scale
        if cum is not None:
            c_i = lax.dynamic_slice_in_dim(cum, i * BLOCK, BLOCK, axis=2)
            logits = logits + c_i[..., :, None] - cum[:, :, None, :]
        logits = jnp.where(pos[None, :] <= t[:, None], logits, -jnp.inf)
        p = jax.nn.softmax(logits, axis=-1).astype(v.dtype)
        return jnp.einsum('bhqs,bshd->bqhd', p, v)

    out = lax.map(one_block, jnp.arange(nb))
    return out.swapaxes(0, 1).reshape(B, S, H * dv)

def dsa_attention(q, k, v, q_idx, k_idx, w_idx):
    B, S, H, d = q.shape
    nb = S // BLOCK
    top_k = min(DSA_TOPK_MAX, S // 4)
    slopes = alibi_slopes(H)
    kv = jnp.concatenate([k, v], axis=-1)
    pos = jnp.arange(S)
    w_idx = w_idx.astype(jnp.float32) * IDX_HEADS ** -0.5

    def one_block(i):
        sl = lambda a: lax.dynamic_slice_in_dim(a, i * BLOCK, BLOCK, axis=1)
        q_i, qi_i, w_i = sl(q), sl(q_idx), sl(w_idx)
        t = i * BLOCK + jnp.arange(BLOCK)
        dots = jnp.einsum('bqhe,bse->bqhs', qi_i, k_idx,
                          preferred_element_type=jnp.float32) * IDX_DIM ** -0.5
        score = jnp.einsum('bqh,bqhs->bqs', w_i, jax.nn.relu(dots))
        score = jnp.where(pos[None, None, :] <= t[None, :, None], score, -jnp.inf)
        _, idx = lax.top_k(score, top_k)
        kv_sel = jax.vmap(lambda a, j: a[j])(kv, idx)
        k_sel, v_sel = kv_sel[..., :d], kv_sel[..., d:]
        dist = (t[None, :, None] - idx).astype(jnp.float32)
        logits = jnp.einsum('bqhd,bqkd->bhqk', q_i, k_sel,
                            preferred_element_type=jnp.float32) * d ** -0.5
        logits = logits - slopes[None, :, None, None] * dist[:, None]
        logits = jnp.where(dist[:, None] >= 0, logits, -jnp.inf)
        p = jax.nn.softmax(logits, axis=-1).astype(v.dtype)
        return jnp.einsum('bhqk,bqkd->bqhd', p, v_sel)

    out = lax.map(one_block, jnp.arange(nb))
    return out.swapaxes(0, 1).reshape(B, S, H * d)

def even_mixer(x, w_in, b_f, sinks, w_o):
    B, S, _ = x.shape
    qa, ka, va, qb, kb, vb, fg = split_cols(x @ w_in, EVEN_SIZES)
    qa = qa.reshape(B, S, A_HEADS, HEAD_DIM)
    ka = ka.reshape(B, S, A_KV_HEADS, HEAD_DIM)
    va = va.reshape(B, S, A_KV_HEADS, HEAD_DIM)
    qb = qb.reshape(B, S, B_HEADS, HEAD_DIM)
    kb = kb.reshape(B, S, B_HEADS, HEAD_DIM)
    vb = vb.reshape(B, S, B_HEADS, HEAD_DIM)
    log_f = jax.nn.log_sigmoid((fg + b_f).astype(jnp.float32))
    out_a = sliding_window_sink_attention(qa, ka, va, sinks)
    out_b = causal_block_attention(qb, kb, vb, log_f)
    return jnp.concatenate([out_a, out_b], axis=-1) @ w_o

def odd_mixer(x, w_in, q_norm_g, kv_norm_g, w_uq, w_ukv, w_o):
    B, S, _ = x.shape
    qc, kc, vc, qi, ki, wi, cq, ckv, kr = split_cols(x @ w_in, ODD_SIZES)
    out_c = dsa_attention(qc.reshape(B, S, C_HEADS, HEAD_DIM), kc, vc,
                          qi.reshape(B, S, IDX_HEADS, IDX_DIM), ki, wi)
    pos = jnp.arange(S)
    q = (rms_norm(cq, q_norm_g) @ w_uq).reshape(B, S, D_HEADS, MLA_NOPE + MLA_ROPE)
    kv = (rms_norm(ckv, kv_norm_g) @ w_ukv).reshape(B, S, D_HEADS, MLA_NOPE + MLA_V)
    q = jnp.concatenate([q[..., :MLA_NOPE], rope(q[..., MLA_NOPE:], pos)], axis=-1)
    k_rope = jnp.broadcast_to(rope(kr, pos)[:, :, None, :], (B, S, D_HEADS, MLA_ROPE))
    k = jnp.concatenate([kv[..., :MLA_NOPE], k_rope], axis=-1)
    out_d = causal_block_attention(q, k, kv[..., MLA_NOPE:])
    return jnp.concatenate([out_c, out_d], axis=-1) @ w_o

def routed_moe(x, router_w, router_b, w_gate, w_up, w_down):
    B, S, D = x.shape
    xt = x.reshape(B * S, D)
    aff = jax.nn.sigmoid((xt @ router_w).astype(jnp.float32))
    sel = aff + router_b.astype(jnp.float32)
    grp_score = lax.top_k(sel.reshape(-1, N_GROUPS, EXPERTS_PER_GROUP), 2)[0].sum(-1)
    _, g_idx = lax.top_k(grp_score, TOPK_GROUPS)
    g_mask = jax.nn.one_hot(g_idx, N_GROUPS, dtype=jnp.float32).sum(1) > 0
    e_mask = jnp.repeat(g_mask, EXPERTS_PER_GROUP, axis=1)
    _, e_idx = lax.top_k(jnp.where(e_mask, sel, -jnp.inf), TOPK_EXPERTS)
    w = jnp.take_along_axis(aff, e_idx, axis=1)
    w = w / jnp.sum(w, axis=-1, keepdims=True)
    gates = jnp.einsum('nk,nke->ne', w, jax.nn.one_hot(e_idx, N_EXPERTS, dtype=jnp.float32)).astype(x.dtype)
    y = jnp.zeros_like(xt)
    for e in range(N_EXPERTS):
        h = jax.nn.silu(xt @ w_gate[e]) * (xt @ w_up[e])
        y = y + gates[:, e:e + 1] * (h @ w_down[e])
    return y.reshape(B, S, D)

def _col_scale(sizes, value_slots):
    return jnp.concatenate([jnp.full((n,), BETA if i in value_slots else 1.0, jnp.float32)
                            for i, n in enumerate(sizes)])

def first_inputs(seed: int = 0) -> dict:
    key = jax.random.key(seed)
    ks = jax.random.split(key, 20)
    nrm = lambda k, shape, scale: jax.random.normal(k, shape, jnp.float32) * scale
    even_in, odd_in = sum(EVEN_SIZES), sum(ODD_SIZES)
    ukv_scale = jnp.tile(jnp.concatenate([jnp.ones((MLA_NOPE,), jnp.float32),
                                          jnp.full((MLA_V,), BETA, jnp.float32)]), D_HEADS)
    return {
        'x': nrm(ks[0], (BATCH, SEQ, D_MODEL), 1.0),
        'even_w_in': nrm(ks[1], (N_EVEN, D_MODEL, even_in), D_MODEL ** -0.5) * _col_scale(EVEN_SIZES, EVEN_VALUE_SLOTS),
        'even_b_f': FOX_BIAS_INIT + nrm(ks[2], (N_EVEN, B_HEADS), 0.1),
        'even_sinks': nrm(ks[3], (N_EVEN, A_HEADS), 1.0),
        'odd_w_in': nrm(ks[4], (N_ODD, D_MODEL, odd_in), D_MODEL ** -0.5) * _col_scale(ODD_SIZES, ODD_VALUE_SLOTS),
        'odd_q_norm': 1.0 + nrm(ks[5], (N_ODD, MLA_Q_RANK), 0.02),
        'odd_kv_norm': 1.0 + nrm(ks[6], (N_ODD, MLA_KV_RANK), 0.02),
        'odd_w_uq': nrm(ks[7], (N_ODD, MLA_Q_RANK, D_HEADS * (MLA_NOPE + MLA_ROPE)), MLA_Q_RANK ** -0.5),
        'odd_w_ukv': nrm(ks[8], (N_ODD, MLA_KV_RANK, D_HEADS * (MLA_NOPE + MLA_V)), MLA_KV_RANK ** -0.5) * ukv_scale,
        'w_o': nrm(ks[9], (DEPTH, MIX_WIDTH, D_MODEL), MIX_WIDTH ** -0.5 * BETA),
        'ln_g': 1.0 + nrm(ks[10], (DEPTH, 2, D_MODEL), 0.02),
        'ln_b': nrm(ks[11], (DEPTH, 2, D_MODEL), 0.02),
        'router_w': nrm(ks[12], (D_MODEL, N_EXPERTS), D_MODEL ** -0.5),
        'router_b': nrm(ks[13], (N_EXPERTS,), 0.01),
        'moe_w_gate': nrm(ks[14], (DEPTH, N_EXPERTS, D_MODEL, D_FF_EXPERT), D_MODEL ** -0.5),
        'moe_w_up': nrm(ks[15], (DEPTH, N_EXPERTS, D_MODEL, D_FF_EXPERT), D_MODEL ** -0.5 * BETA),
        'moe_w_down': nrm(ks[16], (DEPTH, N_EXPERTS, D_FF_EXPERT, D_MODEL), D_FF_EXPERT ** -0.5 * BETA),
    }

def first_block(x, even_w_in, even_b_f, even_sinks, odd_w_in, odd_q_norm, odd_kv_norm, odd_w_uq,
              odd_w_ukv, w_o, ln_g, ln_b, router_w, router_b, moe_w_gate, moe_w_up, moe_w_down):
    for l in range(DEPTH):
        j = l // 2
        if l % 2 == 0:
            mix = even_mixer(x, even_w_in[j], even_b_f[j], even_sinks[j], w_o[l])
        else:
            mix = odd_mixer(x, odd_w_in[j], odd_q_norm[j], odd_kv_norm[j], odd_w_uq[j], odd_w_ukv[j], w_o[l])
        x = layer_norm(ALPHA * x + mix, ln_g[l, 0], ln_b[l, 0])
        ffn = routed_moe(x, router_w, router_b, moe_w_gate[l], moe_w_up[l], moe_w_down[l])
        x = layer_norm(ALPHA * x + ffn, ln_g[l, 1], ln_b[l, 1])
    return x


N_SUB = 3
HALF_STEP = 0.5
D_FF = 2816
CONV_WIDTH = 4
EPS = 1e-6
LRU_WIDTH = D_MODEL
LRU_HEADS = 8
LRU_BLOCK = LRU_WIDTH // LRU_HEADS
LRU_C = 8.0
SSD_WIDTH = D_MODEL
SSD_HEADDIM = 64
SSD_HEADS = SSD_WIDTH // SSD_HEADDIM
SSD_GROUPS = 2
SSD_STATE = 128
SSD_CHUNK = 128
SSD_CONV_DIM = SSD_WIDTH + 2 * SSD_GROUPS * SSD_STATE
HYB_SPLITS = (LRU_WIDTH, 2 * LRU_WIDTH, 2 * LRU_WIDTH + SSD_WIDTH, 2 * LRU_WIDTH + SSD_WIDTH + SSD_CONV_DIM)
HYB_IN = HYB_SPLITS[-1] + SSD_HEADS
HYB_OUT = LRU_WIDTH + SSD_WIDTH
MLSTM_WIDTH = 2 * D_MODEL
MLSTM_HEADS = 4
MLSTM_HEADDIM = MLSTM_WIDTH // MLSTM_HEADS
MLSTM_QKV_BLOCK = 4
MLSTM_CHUNK = 64
N_EVEN_2 = (DEPTH + 1) // 2
N_ODD_2 = DEPTH // 2


def rms_norm_2(x, g):
    xf = x.astype(jnp.float32)
    y = xf * lax.rsqrt(jnp.mean(xf * xf, axis=-1, keepdims=True) + EPS)
    return (y * g.astype(jnp.float32)).astype(x.dtype)

def head_layer_norm(h, g):
    mu = jnp.mean(h, axis=-1, keepdims=True)
    hc = h - mu
    var = jnp.mean(hc * hc, axis=-1, keepdims=True)
    return hc * lax.rsqrt(var + EPS) * g.astype(jnp.float32)

def causal_conv(x, w, b):
    width, ch = w.shape
    y = lax.conv_general_dilated(x, w[:, None, :].astype(x.dtype), window_strides=(1,),
                                 padding=((width - 1, 0),), dimension_numbers=('NWC', 'WIO', 'NWC'),
                                 feature_group_count=ch)
    return y + b

def block_diag_linear(x, w):
    nb, bi, bo = w.shape
    xb = x.reshape(x.shape[:-1] + (nb, bi))
    return jnp.einsum('...ni,nio->...no', xb, w).reshape(x.shape[:-1] + (nb * bo,))

def swiglu(h, w_gate, w_up, w_down):
    return (jax.nn.silu(h @ w_gate) * (h @ w_up)) @ w_down

def rg_lru(x, w_a, b_a, w_x, b_x, lam):
    xf = x.astype(jnp.float32)
    r = jax.nn.sigmoid(block_diag_linear(xf, w_a.astype(jnp.float32)) + b_a.astype(jnp.float32))
    i = jax.nn.sigmoid(block_diag_linear(xf, w_x.astype(jnp.float32)) + b_x.astype(jnp.float32))
    log_a = -LRU_C * r * jax.nn.softplus(-lam.astype(jnp.float32))
    a = jnp.exp(log_a)
    u = jnp.sqrt(-jnp.expm1(2.0 * log_a)) * (i * xf)

    def combine(left, right):
        a_l, u_l = left
        a_r, u_r = right
        return a_l * a_r, a_r * u_l + u_r

    _, h = lax.associative_scan(combine, (a, u), axis=1)
    return h

def segsum(x):
    t = x.shape[-1]
    cs = jnp.cumsum(x, axis=-1)
    diff = cs[..., :, None] - cs[..., None, :]
    mask = jnp.tril(jnp.ones((t, t), dtype=bool))
    return jnp.where(mask, diff, -jnp.inf)

def ssd_chunked(x, dt, a, bm, cm):
    bsz, seq, nh, hp = x.shape
    ng, ns = bm.shape[-2:]
    ne = nh // ng
    nc = seq // SSD_CHUNK
    ln = SSD_CHUNK
    xc = (x * dt[..., None]).reshape(bsz, nc, ln, ng, ne, hp)
    bc = bm.reshape(bsz, nc, ln, ng, ns)
    cc = cm.reshape(bsz, nc, ln, ng, ns)
    ac = (dt * a).reshape(bsz, nc, ln, ng, ne).transpose(0, 3, 4, 1, 2)
    acs = jnp.cumsum(ac, axis=-1)
    decay_in = jnp.exp(segsum(ac))
    cb = jnp.einsum('bclgn,bcsgn->bgcls', cc, bc)
    y_diag = jnp.einsum('bgecls,bcsgep->bclgep', cb[:, :, None] * decay_in, xc)
    decay_states = jnp.exp(acs[..., -1:] - acs).transpose(0, 3, 4, 1, 2)
    states = jnp.einsum('bclgn,bclgep->bcgepn', bc, xc * decay_states[..., None])
    chunk_tot = jnp.pad(acs[..., -1], ((0, 0), (0, 0), (0, 0), (1, 0)))
    decay_chunk = jnp.exp(segsum(chunk_tot))
    states = jnp.pad(states, ((0, 0), (1, 0), (0, 0), (0, 0), (0, 0), (0, 0)))
    prev_states = jnp.einsum('bgezj,bjgepn->bzgepn', decay_chunk, states)[:, :-1]
    decay_out = jnp.exp(acs).transpose(0, 3, 4, 1, 2)
    y_off = jnp.einsum('bclgn,bcgepn->bclgep', cc, prev_states) * decay_out[..., None]
    return (y_diag + y_off).reshape(bsz, seq, nh, hp)

def mlstm_chunkwise(q, k, v, i_pre, f_pre):
    bsz, nh, seq, dh = q.shape
    nc = seq // MLSTM_CHUNK
    ln = MLSTM_CHUNK
    k = k * (dh ** -0.5)
    log_f = jax.nn.log_sigmoid(f_pre)

    def to_chunks(t):
        return jnp.moveaxis(t.reshape((bsz, nh, nc, ln) + t.shape[3:]), 2, 0)

    causal = jnp.tril(jnp.ones((ln, ln), dtype=bool))

    def step(carry, inp):
        c_st, n_st, m_st = carry
        q_c, k_c, v_c, i_c, lf_c = inp
        bcum = jnp.cumsum(lf_c, axis=-1)
        log_d = jnp.where(causal, bcum[..., :, None] - bcum[..., None, :] + i_c[..., None, :], -jnp.inf)
        g = bcum + m_st[..., None]
        m = jnp.maximum(g, jnp.max(log_d, axis=-1))
        w_inter = jnp.exp(g - m)
        s_mat = jnp.einsum('bhtd,bhsd->bhts', q_c, k_c) * jnp.exp(log_d - m[..., None])
        num = w_inter[..., None] * jnp.einsum('bhtd,bhdv->bhtv', q_c, c_st) + jnp.einsum('bhts,bhsv->bhtv', s_mat, v_c)
        den = w_inter * jnp.einsum('bhtd,bhd->bht', q_c, n_st) + jnp.sum(s_mat, axis=-1)
        h_out = num / jnp.maximum(jnp.abs(den), jnp.exp(-m))[..., None]
        b_last = bcum[..., -1]
        log_w = b_last[..., None] - bcum + i_c
        m_new = jnp.maximum(b_last + m_st, jnp.max(log_w, axis=-1))
        w_s = jnp.exp(log_w - m_new[..., None])
        decay = jnp.exp(b_last + m_st - m_new)
        c_new = decay[..., None, None] * c_st + jnp.einsum('bhs,bhsd,bhsv->bhdv', w_s, k_c, v_c)
        n_new = decay[..., None] * n_st + jnp.einsum('bhs,bhsd->bhd', w_s, k_c)
        return (c_new, n_new, m_new), h_out

    init = (jnp.zeros((bsz, nh, dh, dh), jnp.float32), jnp.zeros((bsz, nh, dh), jnp.float32),
            jnp.zeros((bsz, nh), jnp.float32))
    _, hc = lax.scan(step, init, (to_chunks(q), to_chunks(k), to_chunks(v), to_chunks(i_pre), to_chunks(log_f)))
    return jnp.moveaxis(hc, 0, 2).reshape(bsz, nh, seq, dh)

def hybrid_mixer(h, w_in, w_out, lru_conv_w, lru_conv_b, lru_wa, lru_ba, lru_wx, lru_bx, lru_lambda,
                 ssd_conv_w, ssd_conv_b, ssd_dt_bias, ssd_a_log, ssd_d, ssd_norm_g):
    bsz, seq, _ = h.shape
    f32 = jnp.float32
    gate_lru, x_lru, z_ssd, xbc, dt_raw = jnp.split(h @ w_in, HYB_SPLITS, axis=-1)
    x_lru = causal_conv(x_lru, lru_conv_w, lru_conv_b)
    y_lru = rg_lru(x_lru, lru_wa, lru_ba, lru_wx, lru_bx, lru_lambda) * jax.nn.gelu(gate_lru.astype(f32))
    xbc = jax.nn.silu(causal_conv(xbc, ssd_conv_w, ssd_conv_b)).astype(f32)
    gn = SSD_GROUPS * SSD_STATE
    xs = xbc[..., :SSD_WIDTH].reshape(bsz, seq, SSD_HEADS, SSD_HEADDIM)
    bm = xbc[..., SSD_WIDTH:SSD_WIDTH + gn].reshape(bsz, seq, SSD_GROUPS, SSD_STATE)
    cm = xbc[..., SSD_WIDTH + gn:].reshape(bsz, seq, SSD_GROUPS, SSD_STATE)
    dt = jax.nn.softplus(dt_raw.astype(f32) + ssd_dt_bias.astype(f32))
    a = -jnp.exp(ssd_a_log.astype(f32))
    y = ssd_chunked(xs, dt, a, bm, cm) + ssd_d.astype(f32)[:, None] * xs
    y = y.reshape(bsz, seq, SSD_WIDTH) * jax.nn.silu(z_ssd.astype(f32))
    y = rms_norm_2(y.reshape(bsz, seq, SSD_GROUPS, SSD_WIDTH // SSD_GROUPS),
                 ssd_norm_g.reshape(SSD_GROUPS, SSD_WIDTH // SSD_GROUPS)).reshape(bsz, seq, SSD_WIDTH)
    y_cat = jnp.concatenate([y_lru, y], axis=-1).astype(h.dtype)
    return y_cat @ w_out

def mlstm_block(h, w_up, conv_w, conv_b, wq, wk, wv, w_gates, b_gates, norm_g, skip, w_down):
    bsz, seq, _ = h.shape
    f32 = jnp.float32
    xm, z = jnp.split(h @ w_up, 2, axis=-1)
    xc = jax.nn.silu(causal_conv(xm, conv_w, conv_b))
    q = block_diag_linear(xc, wq)
    k = block_diag_linear(xc, wk)
    v = block_diag_linear(xm, wv)
    gates = (q @ w_gates[:MLSTM_WIDTH] + k @ w_gates[MLSTM_WIDTH:2 * MLSTM_WIDTH]
             + v @ w_gates[2 * MLSTM_WIDTH:] + b_gates).astype(f32).transpose(0, 2, 1)
    i_pre = gates[:, :MLSTM_HEADS]
    f_pre = gates[:, MLSTM_HEADS:]

    def heads(t):
        return t.astype(f32).reshape(bsz, seq, MLSTM_HEADS, MLSTM_HEADDIM).transpose(0, 2, 1, 3)

    hh = mlstm_chunkwise(heads(q), heads(k), heads(v), i_pre, f_pre)
    hh = head_layer_norm(hh.transpose(0, 2, 1, 3), norm_g.reshape(MLSTM_HEADS, MLSTM_HEADDIM))
    hh = hh.reshape(bsz, seq, MLSTM_WIDTH) + skip.astype(f32) * xc.astype(f32)
    return (hh * jax.nn.silu(z.astype(f32))).astype(h.dtype) @ w_down

def second_inputs(seed: int = 0) -> dict:
    key = jax.random.key(seed)
    ks = iter(jax.random.split(key, 64))
    f32 = jnp.float32

    def nrm(shape, fan_in, scale=1.0):
        return jax.random.normal(next(ks), shape, f32) * (scale * fan_in ** -0.5)

    def small(shape, s=0.02):
        return jax.random.normal(next(ks), shape, f32) * s

    def gain(shape):
        return 1.0 + small(shape, 0.05)

    x = jax.random.normal(next(ks), (BATCH, SEQ, D_MODEL), f32)
    c = jax.random.normal(next(ks), (BATCH, D_MODEL), f32)
    ada_w = nrm((DEPTH, D_MODEL, N_SUB * 3 * D_MODEL), D_MODEL, 0.5)
    ada_b = small((DEPTH, N_SUB * 3 * D_MODEL))
    norm_g = gain((DEPTH, N_SUB, D_MODEL))
    ffn_w_gate = nrm((DEPTH, 2, D_MODEL, D_FF), D_MODEL)
    ffn_w_up = nrm((DEPTH, 2, D_MODEL, D_FF), D_MODEL)
    ffn_w_down = nrm((DEPTH, 2, D_FF, D_MODEL), D_FF)
    hyb_w_in = nrm((N_EVEN_2, D_MODEL, HYB_IN), D_MODEL)
    hyb_w_out = nrm((N_EVEN_2, HYB_OUT, D_MODEL), HYB_OUT)
    lru_conv_w = nrm((N_EVEN_2, CONV_WIDTH, LRU_WIDTH), CONV_WIDTH)
    lru_conv_b = small((N_EVEN_2, LRU_WIDTH))
    lru_wa = nrm((N_EVEN_2, LRU_HEADS, LRU_BLOCK, LRU_BLOCK), LRU_BLOCK)
    lru_ba = small((N_EVEN_2, LRU_WIDTH))
    lru_wx = nrm((N_EVEN_2, LRU_HEADS, LRU_BLOCK, LRU_BLOCK), LRU_BLOCK)
    lru_bx = small((N_EVEN_2, LRU_WIDTH))
    a_pow = jax.random.uniform(next(ks), (N_EVEN_2, LRU_WIDTH), f32, minval=0.9, maxval=0.999)
    s_a = a_pow ** (1.0 / LRU_C)
    lru_lambda = jnp.log(s_a) - jnp.log1p(-s_a)
    ssd_conv_w = nrm((N_EVEN_2, CONV_WIDTH, SSD_CONV_DIM), CONV_WIDTH)
    ssd_conv_b = small((N_EVEN_2, SSD_CONV_DIM))
    dt0 = jnp.exp(jax.random.uniform(next(ks), (N_EVEN_2, SSD_HEADS), f32,
                                     minval=float(np.log(1e-3)), maxval=float(np.log(1e-1))))
    ssd_dt_bias = dt0 + jnp.log(-jnp.expm1(-dt0))
    ssd_a_log = jnp.log(jax.random.uniform(next(ks), (N_EVEN_2, SSD_HEADS), f32, minval=1.0, maxval=16.0))
    ssd_d = gain((N_EVEN_2, SSD_HEADS))
    ssd_norm_g = gain((N_EVEN_2, SSD_WIDTH))
    mlstm_w_up = nrm((N_ODD_2, D_MODEL, 2 * MLSTM_WIDTH), D_MODEL)
    mlstm_conv_w = nrm((N_ODD_2, CONV_WIDTH, MLSTM_WIDTH), CONV_WIDTH)
    mlstm_conv_b = small((N_ODD_2, MLSTM_WIDTH))
    nblk = MLSTM_WIDTH // MLSTM_QKV_BLOCK
    mlstm_wq = nrm((N_ODD_2, nblk, MLSTM_QKV_BLOCK, MLSTM_QKV_BLOCK), MLSTM_QKV_BLOCK)
    mlstm_wk = nrm((N_ODD_2, nblk, MLSTM_QKV_BLOCK, MLSTM_QKV_BLOCK), MLSTM_QKV_BLOCK)
    mlstm_wv = nrm((N_ODD_2, nblk, MLSTM_QKV_BLOCK, MLSTM_QKV_BLOCK), MLSTM_QKV_BLOCK)
    mlstm_w_gates = nrm((N_ODD_2, 3 * MLSTM_WIDTH, 2 * MLSTM_HEADS), 3 * MLSTM_WIDTH, 0.5)
    f_bias = jnp.broadcast_to(jnp.linspace(3.0, 6.0, MLSTM_HEADS, dtype=f32), (N_ODD_2, MLSTM_HEADS))
    mlstm_b_gates = jnp.concatenate([small((N_ODD_2, MLSTM_HEADS), 0.1),
                                     f_bias + small((N_ODD_2, MLSTM_HEADS), 0.02)], axis=-1)
    mlstm_norm_g = gain((N_ODD_2, MLSTM_WIDTH))
    mlstm_skip = gain((N_ODD_2, MLSTM_WIDTH))
    mlstm_w_down = nrm((N_ODD_2, MLSTM_WIDTH, D_MODEL), MLSTM_WIDTH)
    final_norm_g = gain((D_MODEL,))
    return {'x': x, 'c': c, 'ada_w': ada_w, 'ada_b': ada_b, 'norm_g': norm_g,
            'ffn_w_gate': ffn_w_gate, 'ffn_w_up': ffn_w_up, 'ffn_w_down': ffn_w_down,
            'hyb_w_in': hyb_w_in, 'hyb_w_out': hyb_w_out,
            'lru_conv_w': lru_conv_w, 'lru_conv_b': lru_conv_b, 'lru_wa': lru_wa, 'lru_ba': lru_ba,
            'lru_wx': lru_wx, 'lru_bx': lru_bx, 'lru_lambda': lru_lambda,
            'ssd_conv_w': ssd_conv_w, 'ssd_conv_b': ssd_conv_b, 'ssd_dt_bias': ssd_dt_bias,
            'ssd_a_log': ssd_a_log, 'ssd_d': ssd_d, 'ssd_norm_g': ssd_norm_g,
            'mlstm_w_up': mlstm_w_up, 'mlstm_conv_w': mlstm_conv_w, 'mlstm_conv_b': mlstm_conv_b,
            'mlstm_wq': mlstm_wq, 'mlstm_wk': mlstm_wk, 'mlstm_wv': mlstm_wv,
            'mlstm_w_gates': mlstm_w_gates, 'mlstm_b_gates': mlstm_b_gates,
            'mlstm_norm_g': mlstm_norm_g, 'mlstm_skip': mlstm_skip, 'mlstm_w_down': mlstm_w_down,
            'final_norm_g': final_norm_g}

def second_block(x, c, ada_w, ada_b, norm_g, ffn_w_gate, ffn_w_up, ffn_w_down, hyb_w_in, hyb_w_out,
              lru_conv_w, lru_conv_b, lru_wa, lru_ba, lru_wx, lru_bx, lru_lambda,
              ssd_conv_w, ssd_conv_b, ssd_dt_bias, ssd_a_log, ssd_d, ssd_norm_g,
              mlstm_w_up, mlstm_conv_w, mlstm_conv_b, mlstm_wq, mlstm_wk, mlstm_wv,
              mlstm_w_gates, mlstm_b_gates, mlstm_norm_g, mlstm_skip, mlstm_w_down, final_norm_g):
    bsz = x.shape[0]
    c_act = jax.nn.silu(c)
    for layer in range(DEPTH):
        mod = (c_act @ ada_w[layer] + ada_b[layer]).reshape(bsz, N_SUB, 3, D_MODEL)[:, :, :, None, :]

        def modulate(t, sub):
            return rms_norm_2(t, norm_g[layer, sub]) * (1.0 + mod[:, sub, 1]) + mod[:, sub, 0]

        h = modulate(x, 0)
        x = x + HALF_STEP * (1.0 + mod[:, 0, 2]) * swiglu(h, ffn_w_gate[layer, 0], ffn_w_up[layer, 0], ffn_w_down[layer, 0])
        h = modulate(x, 1)
        if layer % 2 == 0:
            e = layer // 2
            y = hybrid_mixer(h, hyb_w_in[e], hyb_w_out[e], lru_conv_w[e], lru_conv_b[e], lru_wa[e], lru_ba[e],
                             lru_wx[e], lru_bx[e], lru_lambda[e], ssd_conv_w[e], ssd_conv_b[e],
                             ssd_dt_bias[e], ssd_a_log[e], ssd_d[e], ssd_norm_g[e])
        else:
            o = layer // 2
            y = mlstm_block(h, mlstm_w_up[o], mlstm_conv_w[o], mlstm_conv_b[o], mlstm_wq[o], mlstm_wk[o],
                            mlstm_wv[o], mlstm_w_gates[o], mlstm_b_gates[o], mlstm_norm_g[o],
                            mlstm_skip[o], mlstm_w_down[o])
        x = x + (1.0 + mod[:, 1, 2]) * y.astype(x.dtype)
        h = modulate(x, 2)
        x = x + HALF_STEP * (1.0 + mod[:, 2, 2]) * swiglu(h, ffn_w_gate[layer, 1], ffn_w_up[layer, 1], ffn_w_down[layer, 1])
    return rms_norm_2(x, final_norm_g)


def setup_inputs(seed=0):
    out = dict(first_inputs(seed))
    for name, value in second_inputs(seed + 1).items():
        if name != "x":
            out[name + "_2"] = value
    return out


def reference(
    x, even_w_in, even_b_f, even_sinks, odd_w_in, odd_q_norm, odd_kv_norm, odd_w_uq, odd_w_ukv,
    w_o, ln_g, ln_b, router_w, router_b, moe_w_gate, moe_w_up, moe_w_down, c_2, ada_w_2,
    ada_b_2, norm_g_2, ffn_w_gate_2, ffn_w_up_2, ffn_w_down_2, hyb_w_in_2, hyb_w_out_2,
    lru_conv_w_2, lru_conv_b_2, lru_wa_2, lru_ba_2, lru_wx_2, lru_bx_2, lru_lambda_2,
    ssd_conv_w_2, ssd_conv_b_2, ssd_dt_bias_2, ssd_a_log_2, ssd_d_2, ssd_norm_g_2, mlstm_w_up_2,
    mlstm_conv_w_2, mlstm_conv_b_2, mlstm_wq_2, mlstm_wk_2, mlstm_wv_2, mlstm_w_gates_2,
    mlstm_b_gates_2, mlstm_norm_g_2, mlstm_skip_2, mlstm_w_down_2, final_norm_g_2,
):
    x = first_block(
        x, even_w_in, even_b_f, even_sinks, odd_w_in, odd_q_norm, odd_kv_norm, odd_w_uq,
        odd_w_ukv, w_o, ln_g, ln_b, router_w, router_b, moe_w_gate, moe_w_up, moe_w_down,
    )
    return second_block(
        x, c_2, ada_w_2, ada_b_2, norm_g_2, ffn_w_gate_2, ffn_w_up_2, ffn_w_down_2, hyb_w_in_2,
        hyb_w_out_2, lru_conv_w_2, lru_conv_b_2, lru_wa_2, lru_ba_2, lru_wx_2, lru_bx_2,
        lru_lambda_2, ssd_conv_w_2, ssd_conv_b_2, ssd_dt_bias_2, ssd_a_log_2, ssd_d_2,
        ssd_norm_g_2, mlstm_w_up_2, mlstm_conv_w_2, mlstm_conv_b_2, mlstm_wq_2, mlstm_wk_2,
        mlstm_wv_2, mlstm_w_gates_2, mlstm_b_gates_2, mlstm_norm_g_2, mlstm_skip_2,
        mlstm_w_down_2, final_norm_g_2,
    )


_drawn_inputs = setup_inputs


def setup_inputs(seed=0):
    import zlib

    import numpy as np

    out = dict(_drawn_inputs(seed))
    spreads = {}
    factors = {'even_b_f': 40.008,
     'even_sinks': 2.713,
     'odd_q_norm': 8.0,
     'odd_kv_norm': 8.0,
     'lru_ba_2': 8.0,
     'lru_bx_2': 8.0,
     'ssd_conv_b_2': 3.327,
     'ssd_d_2': 3.231,
     'mlstm_conv_b_2': 2.97,
     'mlstm_norm_g_2': 2.886,
     'mlstm_skip_2': 4.309}
    for name, (base, spread) in spreads.items():
        noise = np.random.default_rng([zlib.crc32(name.encode()), seed]).standard_normal(out[name].shape)
        drawn = base * np.exp(spread * noise) if base else spread * noise
        out[name] = jnp.asarray(drawn.astype(out[name].dtype))
    for name, factor in factors.items():
        out[name] = (out[name] * factor).astype(out[name].dtype)
    return out
```

```python
from contextlib import ExitStack

import numpy as np

import concourse.bass as bass
from concourse import mybir

ALU = mybir.AluOpType
ACT = mybir.ActivationFunctionType
F32 = mybir.dt.float32
AX = mybir.AxisListType

P = 128
T = 256
TT = T // P
D = 1024
KD = D // P
HD = 64
MW = P + T
NEG = -1.0e30
SLOTS = 4
SLOT = 6 * D
FG = 256
CH = FG // P
NE, DFE = 16, 512
DFF = 2816
MOE_G = NE * DFE // FG
FFN_G = DFF // FG
ALPHA = 4.0 ** 0.25
LN_EPS, EPS = 1e-5, 1e-6
STAGES = ("even", "moe0", "odd", "moe1", "ada", "ffn00", "hyb", "ffn01", "ffn10", "mlstm", "ffn11")
FINAL = True

EVEN_IN, ODD_IN, HYB_IN = 2312, 1380, 4624
PW = 768

C_ID, C_NEGW, C_NEGC, C_CAUS, C_TRIT, C_BD, C_COS, C_SIN, C_TIE, NCONST = np.cumsum(
    [0, 128, MW, MW, MW, MW, 128, 32, 32, 16]).tolist()


class Stage:

    def __init__(self, name, kind, n, u, cb, ub, v2, me):
        self.name, self.kind, self.n, self.u, self.cb, self.ub, self.v2, self.me = name, kind, n, u, cb, ub, v2, me
        self.layer = self.i = self.sub = 0
        self.end = n


class Head:

    def __init__(self, kind, h, dk, scale, at, q, k, v):
        self.kind, self.h, self.dk, self.scale, self.at, self.q, self.k, self.v = kind, h, dk, scale, at, q, k, v


def constants():
    c = np.zeros((P, NCONST), np.float32)
    p = np.arange(P)
    c[:, C_ID:C_ID + 128] = np.eye(P)
    t = np.concatenate([np.repeat(p[:, None], P, 1), np.repeat(p[:, None] + P, T, 1)], 1)
    s = np.concatenate([np.arange(P), np.arange(T)])[None, :]
    dist = (t - s).astype(np.float32)
    c[:, C_NEGW:C_NEGW + MW] = np.where((dist >= 0) & (dist < 128), -dist, NEG)
    c[:, C_NEGC:C_NEGC + MW] = np.where(dist >= 0, -dist, NEG)
    c[:, C_CAUS:C_CAUS + MW] = np.where(dist >= 0, 0.0, NEG)
    tq = np.concatenate([np.arange(T), np.arange(P) + P])[None, :]
    sk = np.concatenate([np.repeat(p[:, None], T, 1), np.repeat(p[:, None] + P, P, 1)], 1)
    c[:, C_TRIT:C_TRIT + MW] = (sk <= tq)
    c[:, C_BD:C_BD + 128] = (p[:, None] // 4 == p[None, :] // 4)
    inv = np.float32(10000.0) ** (-np.arange(16, dtype=np.float32) / np.float32(16))
    ang = np.arange(T, dtype=np.float32)[:, None] * inv[None, :]
    c[:, C_COS:C_COS + 32] = np.cos(ang).reshape(TT, P, 16).transpose(1, 0, 2).reshape(P, 32)
    c[:, C_SIN:C_SIN + 32] = np.sin(ang).reshape(TT, P, 16).transpose(1, 0, 2).reshape(P, 32)
    c[:, C_TIE:C_TIE + 16] = 16 - np.arange(16)
    return c


def vector_rows():
    sizes = [("ada_b_2", 144), ("norm_g_2", 48), ("lru_conv_w_2", 32), ("lru_conv_b_2", 8), ("lru_ba_2", 8),
             ("lru_bx_2", 8), ("lru_lambda_2", 8), ("ssd_conv_w_2", 48), ("ssd_conv_b_2", 12),
             ("ssd_norm_g_2", 8), ("mlstm_conv_w_2", 64), ("mlstm_conv_b_2", 16), ("mlstm_norm_g_2", 16),
             ("mlstm_skip_2", 16), ("odd_q_norm", 2), ("odd_kv_norm", 1), ("c_2", 8)]
    at, out = 0, {}
    for name, n in sizes:
        out[name] = (at, n)
        at += n
    return out, at


ROWS, NROWS = vector_rows()
ROW_TILES = -(-NROWS // P)


def flat(ap):
    names = "abcdefg"[:len(ap.shape)]
    return ap.rearrange(f"{' '.join(names)} -> ({' '.join(names)})") if len(names) > 1 else ap


def make_plan(a):
    items, plan = [], []

    def project(w):
        src = w.rearrange("(k p) n -> p k n", p=P)
        for lo in range(0, w.shape[1], PW):
            hi = min(lo + PW, w.shape[1])
            n = hi - lo
            items.append([(k0 * n, (k1 - k0, n), src[:, k0:k1, lo:hi]) for k0, k1 in ((0, 3), (3, 6), (6, 8))])

    def output(w):
        src = w.rearrange("(k p) n -> p k n", p=P)
        for k in range(0, w.shape[0] // P, 4):
            items.append([(a0 * D, (a1 - a0, D), src[:, k + a0:k + a1, :]) for a0, a1 in ((0, 2), (2, 3), (3, 4))])

    def hidden(wg, wu, wd):
        for g in range(FFN_G):
            items.append([
                (0, (KD, FG), wg.rearrange("(k p) n -> p k n", p=P)[:, :, g * FG:(g + 1) * FG]),
                (KD * FG, (KD, FG), wu.rearrange("(k p) n -> p k n", p=P)[:, :, g * FG:(g + 1) * FG]),
                (2 * KD * FG, (CH, D), wd.rearrange("(c p) n -> p c n", p=P)[:, g * CH:(g + 1) * CH, :])])

    u = chunks = units = v2 = moes = 0
    for name in STAGES:
        r = Stage(name=name, kind=name.rstrip("01"), n=len(items), u=u, cb=chunks, ub=units, v2=v2, me=moes)
        if name == "even":
            project(a["even_w_in"][0])
            output(a["w_o"][0])
            u, units = u + 2, units + 16
        elif name == "odd":
            project(a["odd_w_in"][0])
            output(a["w_o"][1])
            u, units = u + 2, units + 16
        elif r.kind == "moe":
            r.layer = int(name[-1])
            items.extend([("moe", r.layer)] * MOE_G)
            u, chunks, moes = u + 1, chunks + CH * MOE_G, moes + 1
        elif name == "ada":
            project(a["ada_w_2"][0])
            project(a["ada_w_2"][1])
        elif r.kind == "ffn":
            r.layer, r.i, r.sub = int(name[3]), int(name[4]), 2 * int(name[4])
            hidden(a["ffn_w_gate_2"][r.layer, r.i], a["ffn_w_up_2"][r.layer, r.i], a["ffn_w_down_2"][r.layer, r.i])
            u, chunks, v2 = u + 1, chunks + CH * FFN_G, v2 + 1
        elif name == "hyb":
            r.layer, r.sub = 0, 1
            project(a["hyb_w_in_2"][0])
            output(a["hyb_w_out_2"][0])
            u, v2 = u + 1, v2 + 1
        elif name == "mlstm":
            r.layer, r.sub = 1, 1
            project(a["mlstm_w_up_2"][0])
            output(a["mlstm_w_down_2"][0])
            u, v2 = u + 1, v2 + 1
        r.end = len(items)
        plan.append(r)
    return items, plan, v2


def program(nc, a, out):
    items, plan, v2_end = make_plan(a)
    with ExitStack() as ctx:
        sems = {}

        def S(name):
            if name not in sems:
                sems[name] = ctx.enter_context(nc.semaphore(name))
            return sems[name]

        def sb(name, shape):
            return ctx.enter_context(nc.sbuf_tensor(name, shape, F32))

        ring = sb("ring", [P, SLOTS, SLOT])
        X = sb("X", [P, TT, D])
        XN = sb("XN", [P, TT, D])
        XT = sb("XT", [P, KD, T])
        ROWB = sb("ROWB", [P, 2, D])
        CON = sb("CON", [P, NCONST])
        COL = sb("COL", [P, ROW_TILES * P])
        MOD = sb("MOD", [P, 2, 72])
        MODA = sb("MODA", [P, 6, KD])
        MODG = sb("MODG", [P, 6, KD])
        ONES = sb("ONES", [P, T])
        RW = sb("RW", [P, KD, NE])
        RB = sb("RB", [P, NE])
        SINK = sb("SINK", [P, 8])
        SSDD = sb("SSDD", [P, 8])
        MARKS = sb("MARKS", [1, 128])
        BF = sb("BF", [16, 8])
        WQKV = sb("WQKV", [P, 3, 16, 4])
        WGT = sb("WGT", [P, 48, 8])
        ST = sb("ST", [P, 192])
        NAR = 16256
        AR = sb("AR", [P, NAR])
        PS = ctx.enter_context(nc.psum_tensor("PS", [P, 8, 512], F32))
        PSY = PS[:, 0:4, :].rearrange("p (t h) n -> p t (h n)", t=TT)

        ID = CON[:, C_ID:C_ID + P]

        def carve(at, *shape):
            n = int(np.prod(shape))
            assert at + n <= NAR, (at, n)
            v = AR[:, at:at + n]
            if len(shape) > 1:
                names = "abcd"[:len(shape)]
                v = v.rearrange(f"p ({' '.join(names)}) -> p {' '.join(names)}",
                                **{k: s for k, s in zip(names, shape)})
            return v

        def col(name, i=0, n=1):
            c = ROWS[name][0] + i
            return COL[:, c:c + n]

        class Lane:

            def __init__(self, eng, name):
                self.e, self.name, self.n = eng, name + "_step", 0

            def c(self, ins):
                self.n += 1
                ins.then_inc(S(self.name), 1)
                self.e.wait_ge(S(self.name), self.n)

        def bc(ap, shape):
            return ap.to_broadcast(shape)

        TM = carve(0, TT, PW * 3)
        A0 = TT * PW * 3
        QK = carve(A0, 2, 512)
        LG = carve(A0 + 1024, 2, MW)
        PB = carve(A0 + 1024 + 2 * MW, 2, MW)
        PT = carve(A0 + 1024 + 4 * MW, 2, MW)
        A1 = A0 + 1024 + 6 * MW
        CT = carve(A1, T)
        NCT = carve(A1 + T, T)
        SPW = carve(A1 + 2 * T, 6, T)
        CTOK = carve(A1 + 8 * T, TT, 8)
        TMO = carve(0, TT, ODD_IN)
        WUQ = carve(TT * ODD_IN, 2, 768)
        DQ = carve(A1, TT, 8, 96)
        DKV = carve(A1 + 1536, TT, 8, 128)
        DK = carve(A1 + 3584, TT, 8, 96)
        SELM = carve(A1 + 5120, MW)
        SCR = carve(A1 + 5120 + MW, MW)
        TMPS = carve(A1 + 5120 + 2 * MW, MW)
        CQT = carve(A1 + 6272, 3, T)
        WUKV = carve(A1 + 6272 + 768, 1024)
        CQN = DKV[:, :, 0:3, :]
        QIT = DQ.rearrange("p t h d -> p (t h d)")[:, 0:5 * T].rearrange("p (h t) -> p h t", t=T)
        GB = carve(0, NE, T)
        SG = carve(4096, 2, T)
        HT = carve(4608, 2, T)
        RT = carve(5120, 12, TT * NE)
        RP = carve(5504, TT, 4, 6)
        GT = carve(5600, T)
        DG = carve(6144, KD, P)
        GA = carve(0, 8, T)
        XL = carve(2048, 8, T)
        ZH = carve(4096, 8, T)
        XBC = carve(6144, 12, T)
        RAW = carve(9216, 2, T + 3)
        HWA = carve(9216 + 520, 8, P)
        HWX = carve(9216 + 520 + 1024, 8, P)
        H1 = carve(11784, 8, T)
        H2 = carve(11784 + 2048, 8, T)
        RG = XN[:, :, :].rearrange("p t (k d) -> p (t k) d", d=T)
        IG = XT
        AC = carve(11784, T)
        DTR = carve(11784 + T, T)
        SPH = carve(11784 + 2 * T, 6, T)
        CBM = carve(11784 + 2048, 2, MW)
        EH = carve(11784 + 2048 + 2 * MW, 2, MW)
        ACD = carve(11784 + 2048 + 4 * MW, 64)
        H2_RS = carve(11784, 2, T)
        XM = carve(0, 16, T + 3)
        ZM = carve(4144, 16, T)
        XC = carve(8240, 16, T)
        BD = carve(12336, 3, 4, P)
        EM = carve(13872, MW)
        PM = carve(13872 + MW, MW)
        MR = carve(13872 + 2 * MW, 4, T)
        SPX = XN[:, :, :].rearrange("p t (k d) -> p (t k) d", d=T)
        NQ = XT
        VM = XN[:, 0, :].rearrange("p (t d) -> p t d", t=TT)
        HN = XN[:, 1, :].rearrange("p (t d) -> p t d", t=TT)
        block = ctx.enter_context(nc.Block())

        def units_of(name):
            out_ = []
            if name == "even":
                for h in range(8):
                    out_.append(Head(kind="window", h=h, dk=HD, scale=HD ** -0.5, at=HD * h,
                                                q=TM[:, :, HD * h:HD * h + HD],
                                                k=TM[:, :, 512 + HD * (h // 4):512 + HD * (h // 4) + HD],
                                                v=TM[:, :, 640 + HD * (h // 4):640 + HD * (h // 4) + HD]))
                for h in range(8):
                    out_.append(Head(kind="fox", h=h, dk=HD, scale=HD ** -0.5, at=512 + HD * h,
                                                q=TM[:, :, 768 + HD * h:768 + HD * h + HD],
                                                k=TM[:, :, 1280 + HD * h:1280 + HD * h + HD],
                                                v=TM[:, :, 1792 + HD * h:1792 + HD * h + HD]))
            else:
                for h in range(8):
                    out_.append(Head(kind="dsa", h=h, dk=HD, scale=HD ** -0.5, at=HD * h,
                                                q=TMO[:, :, HD * h:HD * h + HD], k=TMO[:, :, 512:576],
                                                v=TMO[:, :, 576:640]))
                for h in range(8):
                    out_.append(Head(kind="mla", h=h, dk=96, scale=96 ** -0.5, at=512 + HD * h,
                                                q=DQ[:, :, h, :], k=DK[:, :, h, :], v=DKV[:, :, h, HD:2 * HD]))
            return out_

        BLK = [(0, P), (P, MW)]

        def feature_tiles(width):
            return [(c // PW, (c % PW) // P) for c in range(0, width - width % P, P)]

        def tile_done(eng, r, tiles, f):
            i, j = tiles[f]
            if f + 1 == len(tiles) or tiles[f + 1][0] != i:
                eng.wait_ge(S("w_used"), 2 * (r.n + i + 1))
            else:
                eng.wait_ge(S("tile_ps"), TILE_BASE[r.name] + sum(
                    1 for g in range(f + 1) if g + 1 < len(tiles) and tiles[g + 1][0] == tiles[g][0]))

        HT_TILES, MT_TILES = feature_tiles(HYB_IN), feature_tiles(4096)
        n_h = NT_H_TILES = len(HT_TILES)
        TILE_BASE = {"hyb": 0, "mlstm": 30 if any(r.name == "hyb" for r in plan) else 0}
        EV_BASE = {"hyb": 0, "mlstm": n_h if any(r.name == "hyb" for r in plan) else 0}
        NT_H = n_h
        RG_XD = XN

        @block.sync
        def _(sp):
            def load(slot, n, parts):
                if not isinstance(n, int) or n >= SLOTS:
                    sp.wait_ge(S("w_used"), n * 2 - (SLOTS - 1) * 2)
                for o, (k, w), src in parts:
                    sp.dma_start(ring[:, slot, o:o + k * w].rearrange("p (k w) -> p k w", k=k), src)\
                      .then_inc(S(f"w_land{slot}"), 16)

            for r in plan:
                if r.kind != "moe":
                    for n in range(r.n, r.end):
                        load(n % SLOTS, n, items[n])
                    continue

                def experts(i):
                    for j in range(SLOTS):
                        e = bass.ds(i * 2 + j // 2, 1)
                        f0 = (j % 2) * FG
                        w_g = a["moe_w_gate"][r.layer, e].rearrange("a (k p) n -> p (a k) n", p=P)
                        w_u = a["moe_w_up"][r.layer, e].rearrange("a (k p) n -> p (a k) n", p=P)
                        w_d = a["moe_w_down"][r.layer, e].rearrange("a (c p) n -> p (a c) n", p=P)
                        load((r.n + j) % SLOTS, i * SLOTS + (r.n + j),
                             [(0, (KD, FG), w_g[:, :, f0:f0 + FG]), (KD * FG, (KD, FG), w_u[:, :, f0:f0 + FG]),
                              (2 * KD * FG, (CH, D), w_d[:, (j % 2) * CH:(j % 2 + 1) * CH, :])])

                experts(0)
                with sp.Fori(1, MOE_G // SLOTS, 1) as i:
                    experts(i)
            sp.wait_ge(S("final"), 1)
            sp.dma_start(out[0].rearrange("(t p) d -> p t d", p=P), XN[:, :, :]).then_inc(S("stored"), 16)
            sp.wait_ge(S("stored"), 16)

        N_SMALL, N_ROWS = 14, [0]

        @block.gpsimd
        def _(pool):
            def ld(dst, src, name):
                pool.dma_start(dst, src, allow_slow_non_contiguous=True).then_inc(S(name), 16)

            ld(X[:, :, :], a["x"][0].rearrange("(t p) d -> p t d", p=P), "x_load")
            ld(CON[:, :], a["const"], "con_load")
            ld(BF[0:8, 0:1], a["even_b_f"].rearrange("a h -> h a"), "small_load")
            ld(BF[0:16, 1:2], a["ssd_dt_bias_2"].rearrange("a h -> h a"), "small_load")
            ld(BF[0:16, 2:3], a["ssd_a_log_2"].rearrange("a h -> h a"), "small_load")
            ld(BF[0:4, 3:4], a["mlstm_b_gates_2"][:, 0:4].rearrange("a h -> h a"), "small_load")
            ld(BF[0:4, 4:5], a["mlstm_b_gates_2"][:, 4:8].rearrange("a h -> h a"), "small_load")
            ld(SINK[:, :], a["even_sinks"][0].partition_broadcast(P), "small_load")
            ld(RB[:, :], a["router_b"].partition_broadcast(P), "small_load")
            ld(RW[:, :, :], a["router_w"].rearrange("(k p) e -> p k e", p=P), "small_load")
            for half in range(2):
                ld(SSDD[64 * half:64 * half + 64, :],
                   a["ssd_d_2"][0].rearrange("(t h) -> h t", h=2)[half].partition_broadcast(64), "small_load")
            for i, w in enumerate(("mlstm_wq_2", "mlstm_wk_2", "mlstm_wv_2")):
                ld(WQKV[:, i, :, :], a[w][0].rearrange("(t n) i o -> (n i) t o", t=16), "small_load")
            ld(WGT[:, :, :], a["mlstm_w_gates_2"][0].rearrange("(k p) e -> p k e", p=P), "small_load")
            for name, (at, n) in ROWS.items():
                shape = a[name].shape
                names = "abcde"[:len(shape)]
                src = a[name].rearrange(f"{' '.join(names)} -> ({' '.join(names)})").rearrange("(r c) -> r c", c=P)
                done = 0
                while done < n:
                    t, q = divmod(at + done, P)
                    m = min(n - done, P - q)
                    ld(AR[q:q + m, t * P:(t + 1) * P], src[done:done + m, :], "rows_load")
                    N_ROWS[0] += 1
                    done += m
            n_ln = 0
            for r in plan:
                if r.kind in ("even", "moe", "odd"):
                    if n_ln > 0:
                        pool.wait_ge(S("ln_done"), n_ln)
                    w = {"even": (0, 0), "moe0": (0, 1), "odd": (1, 0), "moe1": (1, 1)}[r.name]
                    ld(ROWB[:, 0, :], a["ln_g"][w[0], w[1]].partition_broadcast(P), "ln_load")
                    ld(ROWB[:, 1, :], a["ln_b"][w[0], w[1]].partition_broadcast(P), "ln_load")
                    n_ln += 1
                if r.name == "odd":
                    pool.wait_ge(S("cols_done"), 1)
                    if r.n:
                        pool.wait_ge(S("w_used"), 2 * r.n)
                    ld(WUQ, a["odd_w_uq"][0].rearrange("(k p) n -> p k n", p=P), "rank_load")
                    ld(WUKV, a["odd_w_ukv"][0], "rank_load")
                if r.name == "hyb":
                    pool.wait_ge(S("cols_done"), 1)
                    if r.n:
                        pool.wait_ge(S("w_used"), 2 * r.n)
                    ld(HWA, a["lru_wa_2"][0].rearrange("h i o -> i h o"), "lru_load")
                    ld(HWX, a["lru_wx_2"][0].rearrange("h i o -> i h o"), "lru_load")
            if n_ln:
                pool.wait_ge(S("ln_done"), n_ln)
            if FINAL:
                ld(ROWB[:, 1, :], a["final_norm_g_2"].partition_broadcast(P), "fin_load")

        @block.tensor
        def _(pe):
            mm = nc.tensor.matmul

            def landed(n):
                pe.wait_ge(S(f"w_land{n % SLOTS}"), 48 * (n // SLOTS + 1))

            def slot(n, k, w):
                return ring[:, n % SLOTS, 0:k * w].rearrange("p (k w) -> p k w", k=k)

            def columns():
                pe.wait_ge(S("con_load"), 16)
                pe.wait_ge(S("rows_load"), 16 * N_ROWS[0])
                for t in range(ROW_TILES):
                    m = min(P, NROWS - t * P)
                    nc.tensor.transpose(PS[:, t, 0:m], AR[0:m, t * P:(t + 1) * P], ID[0:m, 0:m])\
                      .then_inc(S("cols_ps"), 1)

            def trn(u, src):
                pe.wait_ge(S("xn"), u + 1)
                for j in range(4):
                    for i in range(2):
                        for t in range(TT):
                            ins = nc.tensor.transpose(PS[:, 4 + j, i * T + t * P:i * T + (t + 1) * P],
                                                      src[:, t, (2 * j + i) * P:(2 * j + i + 1) * P], ID)
                    ins.then_inc(S("xt_ps"), 1)

            def out_rows(r, n0, n1, tiles):
                kt = 4 * (n1 - n0)
                for k in range(kt):
                    n = n0 + k // 4
                    if k % 4 == 0:
                        landed(n)
                    w = slot(n, 4, D)
                    for t in range(TT):
                        for h in range(2):
                            ins = mm(PSY[:, t, 512 * h:512 * h + 512], tiles[k][:, t * P:(t + 1) * P],
                                     w[:, k % 4, 512 * h:512 * h + 512], start=k == 0, stop=k == kt - 1)
                    if k % 4 == 3:
                        ins.then_inc(S("w_used"), 2)

            def project(r, widths, evac):
                for i, w in enumerate(widths):
                    n, b0 = r.n + i, 4 * (i % 2)
                    landed(n)
                    if i >= 2:
                        pe.wait_ge(S(evac), i - 1)
                    wt = slot(n, KD, w)
                    for t in range(TT):
                        for c0 in range(0, w, 512):
                            c1 = min(w, c0 + 512)
                            for k in range(KD):
                                ins = mm(PS[:, b0 + 2 * t + c0 // 512, 0:c1 - c0], XT[:, k, t * P:(t + 1) * P],
                                         wt[:, k, c0:c1], start=k == 0, stop=k == KD - 1)
                    ins.then_inc(S("w_used"), 2)

            def project_tiles(r, tiles, wd):
                for f, (i, j) in enumerate(tiles):
                    n = r.n + i
                    w = min(PW, wd - i * PW)
                    if j == 0:
                        landed(n)
                    if f >= 8:
                        pe.wait_ge(S("tile_out"), EV_BASE[r.name] + f - 7)
                    wt = slot(n, KD, w)
                    for k in range(KD):
                        ins = mm(PS[:, f % 8, 0:T], wt[:, k, j * P:(j + 1) * P], XT[:, k, :],
                                 start=k == 0, stop=k == KD - 1)
                    if f + 1 == len(tiles) or tiles[f + 1][0] != i:
                        ins.then_inc(S("w_used"), 2)
                    else:
                        ins.then_inc(S("tile_ps"), 1)

            def attention(r, units):
                def transposed(i):
                    u, w, b = r.ub + i, units[i], i % 2
                    if u >= 2:
                        pe.wait_ge(S("qk"), 2 * (u - 1))
                    for t in range(TT):
                        nc.tensor.transpose(PS[0:w.dk, b, t * P:(t + 1) * P], w.q[:, t, :], ID)
                        ins = nc.tensor.transpose(PS[0:w.dk, b, T + t * P:T + (t + 1) * P], w.k[:, t, :], ID)
                    ins.then_inc(S("qk_ps"), 1)

                def scores(i):
                    u, w, b = r.ub + i, units[i], i % 2
                    pe.wait_ge(S("qk"), 2 * (u + 1))
                    if u >= 2:
                        pe.wait_ge(S("logits"), u - 1)
                    fox = w.kind == "fox"
                    for t, (c0, c1) in enumerate(BLK):
                        ins = mm(PS[:, 2 + b, c0:c1], QK[0:w.dk, b, t * P:(t + 1) * P], QK[0:w.dk, b, T:T + c1 - c0],
                                 start=True, stop=not fox)
                        if fox:
                            ins = mm(PS[:, 2 + b, c0:c1], bc(ID[0:8, w.h:w.h + 1], (8, P)), NCT[0:8, 0:c1 - c0],
                                     start=False, stop=True)
                    ins.then_inc(S("scores"), 1)

                def probs(i):
                    u, b = r.ub + i, i % 2
                    pe.wait_ge(S("p"), 2 * (u + 1))
                    if u >= 2:
                        pe.wait_ge(S("pt"), u - 1)
                    for c in range(3):
                        ins = nc.tensor.transpose(PS[:, 4 + b, c * P:(c + 1) * P], PB[:, b, c * P:(c + 1) * P], ID)
                    ins.then_inc(S("pt_ps"), 1)

                def values(i):
                    u, w, b = r.ub + i, units[i], i % 2
                    pe.wait_ge(S("pt"), u + 1)
                    if u >= 2:
                        pe.wait_ge(S("o"), u - 1)
                    mm(PS[:, 6 + b, 0:HD], PT[:, b, 0:P], w.v[:, 0, :], start=True, stop=True)
                    mm(PS[:, 6 + b, HD:2 * HD], PT[:, b, P:2 * P], w.v[:, 0, :], start=True, stop=False)
                    mm(PS[:, 6 + b, HD:2 * HD], PT[:, b, 2 * P:3 * P], w.v[:, 1, :], start=False, stop=True)\
                        .then_inc(S("o_ps"), 1)

                n = len(units)
                for i in range(n + 3):
                    if i < n:
                        transposed(i)
                    if 0 <= i - 1 < n:
                        scores(i - 1)
                    if 0 <= i - 2 < n:
                        probs(i - 2)
                    if 0 <= i - 3 < n:
                        values(i - 3)

            def even(r):
                trn(r.u, X)
                pe.wait_ge(S("xt"), 8 * (r.u + 1))
                project(r, [PW] * 3, "tm_even")
                n = r.n + 3
                landed(n)
                pe.wait_ge(S("tm_even"), 3)
                wt = slot(n, KD, 8)
                for k in range(KD):
                    ins = mm(PS[0:8, 0, 0:T], wt[:, k, :], XT[:, k, :], start=k == 0, stop=k == KD - 1)
                ins.then_inc(S("w_used"), 2)
                pe.wait_ge(S("ct"), 1)
                for t in range(TT):
                    ins = nc.tensor.transpose(PS[:, 1, 8 * t:8 * t + 8], CT[0:8, t * P:(t + 1) * P], ID[0:8, 0:8])
                ins.then_inc(S("ct_ps"), 1)
                pe.wait_ge(S("ctok"), 1)
                attention(r, units_of("even"))
                trn(r.u + 1, XN)
                pe.wait_ge(S("xt"), 8 * (r.u + 2))
                out_rows(r, r.n + 4, r.end, [XT[:, k, :] for k in range(KD)])

            def odd(r):
                trn(r.u, X)
                pe.wait_ge(S("xt"), 8 * (r.u + 1))
                project(r, [PW, ODD_IN - PW], "tm_odd")
                pe.wait_ge(S("tm_odd"), 2)
                for h in range(5):
                    for t in range(TT):
                        ins = nc.tensor.transpose(PS[0:HD, h // 2, (h % 2) * T + t * P:(h % 2) * T + (t + 1) * P],
                                                  TMO[:, t, 640 + HD * h:640 + HD * (h + 1)], ID)
                ins.then_inc(S("qi_ps"), 1)
                pe.wait_ge(S("qit"), 3)
                for h in range(4):
                    for t, (c0, c1) in enumerate(BLK):
                        ins = mm(PS[:, 4 + h, c0:c1], QIT[0:HD, h, t * P:(t + 1) * P], QIT[0:HD, 4, 0:c1 - c0],
                                 start=True, stop=True)
                    ins.then_inc(S("dots"), 1)
                pe.wait_ge(S("cqn"), 1)
                for c in range(3):
                    for t in range(TT):
                        ins = nc.tensor.transpose(PS[:, c, t * P:(t + 1) * P], CQN[:, t, c, :], ID)
                ins.then_inc(S("cqt_ps"), 1)
                pe.wait_ge(S("cqt"), 3)
                pe.wait_ge(S("rank_load"), 32)
                pe.wait_ge(S("dsa"), 1)
                for t in range(TT):
                    for c0, c1 in ((0, 512), (512, 768)):
                        for k in range(2):
                            ins = mm(PS[:, 4 + 2 * t + c0 // 512, 0:c1 - c0], CQT[:, k, t * P:(t + 1) * P],
                                     WUQ[:, k, c0:c1], start=k == 0, stop=k == 1)
                ins.then_inc(S("dq_ps"), 1)
                for t in range(TT):
                    for h in range(2):
                        ins = mm(PS[:, 2 * t + h, :], CQT[:, 2, t * P:(t + 1) * P], WUKV[:, 512 * h:512 * h + 512],
                                 start=True, stop=True)
                ins.then_inc(S("dkv_ps"), 1)
                pe.wait_ge(S("mla_ready"), 1)
                attention(r, units_of("odd"))
                trn(r.u + 1, XN)
                pe.wait_ge(S("xt"), 8 * (r.u + 2))
                out_rows(r, r.n + 2, r.end, [XT[:, k, :] for k in range(KD)])

            def hidden_layer(n0, cb, groups):
                def gate_up(i, j):
                    s = (n0 + j // CH) % SLOTS
                    if j % CH == 0:
                        pe.wait_ge(S(f"w_land{s}"), i * 48 + 48 * ((n0 + j // CH) // SLOTS + 1))
                    first = isinstance(i, int) and i == 0
                    if not first or j >= 4:
                        pe.wait_ge(S("hidden"), i * 8 + (cb + j - 3))
                    for m in range(2):
                        w = ring[:, s, m * KD * FG:(m + 1) * KD * FG].rearrange("p (k f) -> p k f", k=KD)
                        for k in range(KD):
                            ins = mm(PS[:, 4 + j % 4, m * T:(m + 1) * T], w[:, k, (j % CH) * P:(j % CH + 1) * P],
                                     XT[:, k, :], start=k == 0, stop=k == KD - 1)
                    ins.then_inc(S("gate_up"), 1)

                def down(i, j, start=False, stop=False):
                    s = (n0 + j // CH) % SLOTS
                    pe.wait_ge(S("hidden"), i * 8 + (cb + j + 1))
                    w = ring[:, s, 2 * KD * FG:2 * KD * FG + CH * D].rearrange("p (c n) -> p c n", c=CH)
                    for t in range(TT):
                        for h in range(2):
                            ins = mm(PSY[:, t, 512 * h:512 * h + 512], HT[:, j % 2, t * P:(t + 1) * P],
                                     w[:, j % CH, 512 * h:512 * h + 512], start=start, stop=stop,
                                     skip_group_check=True)
                    ins.then_inc(S("w_used"), 1)

                per = CH * SLOTS
                turns, rest = divmod(groups, SLOTS)
                last = CH * groups - 1
                gate_up(0, 0)
                for j in range(per - 1):
                    gate_up(0, j + 1)
                    down(0, j, start=j == 0)
                if turns > 2:
                    with pe.Fori(1, turns, 1) as i:
                        gate_up(i, 0)
                        w_prev = i - 1
                        down_open(w_prev, down)
                        for j in range(per - 1):
                            gate_up(i, j + 1)
                            down(i, j)
                    down(turns - 1, per - 1, stop=True)
                    return
                for c in range(per - 1, last + 1):
                    if c < last:
                        gate_up((c + 1) // per, (c + 1) % per)
                    down(c // per, c % per, stop=c == last)

            def down_open(i, down):
                down(i, CH * SLOTS - 1)

            def gate_row(r):
                pe.wait_ge(S("xt"), 8 * (r.u + 1))
                pe.wait_ge(S("diag"), r.v2 + 1)
                for j in range(2):
                    ins = mm(PS[:, 6 + j, :], ONES[:, 0:P],
                             DG[:, 4 * j:4 * j + 4, :].rearrange("p k d -> p (k d)"), start=True, stop=True)
                ins.then_inc(S("row_ps"), 1)
                pe.wait_ge(S("row"), r.v2 + 1)

            def moe(r):
                trn(r.u, X)
                pe.wait_ge(S("xt"), 8 * (r.u + 1))
                pe.wait_ge(S("small_load"), 16 * N_SMALL)
                for t in range(TT):
                    for k in range(KD):
                        ins = mm(PS[:, 4, NE * t:NE * t + NE], XT[:, k, t * P:(t + 1) * P], RW[:, k, :],
                                 start=k == 0, stop=k == KD - 1)
                ins.then_inc(S("route_ps"), 1)
                pe.wait_ge(S("gates"), r.me + 1)
                for t in range(TT):
                    ins = nc.tensor.transpose(PS[0:NE, 5, t * P:(t + 1) * P], RT[:, 11, NE * t:NE * t + NE], ID)
                ins.then_inc(S("gates_ps"), 1)
                pe.wait_ge(S("gates_t"), r.me + 1)
                for e in range(NE):
                    if e >= 8 and e % 2 == 0:
                        pe.wait_ge(S("gate_rows"), 8 * r.me + e // 2 - 3)
                    ins = mm(PS[:, 4 + (e // 2) % 4, (e % 2) * T:(e % 2 + 1) * T], bc(ID[0:NE, e:e + 1], (NE, P)),
                             GT[0:NE, :], start=True, stop=True)
                    if e % 2 == 1:
                        ins.then_inc(S("rows_ps"), 1)
                pe.wait_ge(S("gate_rows"), 8 * (r.me + 1))
                hidden_layer(r.n, r.cb, MOE_G)

            def ffn(r):
                trn(r.u, XN)
                gate_row(r)
                hidden_layer(r.n, r.cb, FFN_G)

            def ada(r):
                pe.wait_ge(S("c_act"), 1)
                for i in range(24):
                    n, l = r.n + i, i // 12
                    landed(n)
                    wt = slot(n, KD, PW)
                    for j in range(6):
                        m = (i % 12) * 6 + j
                        for k in range(KD):
                            ins = mm(PS[:, 4 + l, m:m + 1], wt[:, k, j * P:(j + 1) * P], ST[:, 56 + k:57 + k],
                                     start=k == 0, stop=k == KD - 1)
                    ins.then_inc(S("w_used"), 2)

            def hyb(r):
                trn(r.u, XN)
                gate_row(r)
                project_tiles(r, HT_TILES, HYB_IN)
                n = r.n + 6
                landed(n)
                pe.wait_ge(S("tile_out"), EV_BASE["hyb"] + NT_H)
                wt = slot(n, KD, 16)
                for k in range(KD):
                    ins = mm(PS[0:16, 0, 0:T], wt[:, k, :], XT[:, k, :], start=k == 0, stop=k == KD - 1)
                ins.then_inc(S("w_used"), 2)
                pe.wait_ge(S("lru_load"), 32)
                pe.wait_ge(S("conv"), 20)
                for i in range(8):
                    b = 2 + i % 2
                    if i >= 2:
                        pe.wait_ge(S("lru_gates"), 2 * (i - 1))
                    mm(PS[:, b, 0:T], HWA[:, i, :], XL[:, i, :], start=True, stop=True)
                    mm(PS[:, b, T:2 * T], HWX[:, i, :], XL[:, i, :], start=True, stop=True)\
                        .then_inc(S("lru_ps"), 1)
                pe.wait_ge(S("ssd_rows"), 1)
                for m, src in enumerate((AC, DTR)):
                    for t in range(TT):
                        ins = nc.tensor.transpose(PS[:, 1, 32 * m + 16 * t:32 * m + 16 * t + 16],
                                                  src[0:16, t * P:(t + 1) * P], ID[0:16, 0:16])
                ins.then_inc(S("acd_ps"), 1)
                pe.wait_ge(S("xbc"), 1)
                for t in range(TT):
                    for j in range(2):
                        for c in range(4):
                            ins = nc.tensor.transpose(PS[:, 4 + 2 * t + j, c * P:(c + 1) * P],
                                                      XBC[:, 4 * j + c, t * P:(t + 1) * P], ID)
                        ins.then_inc(S("xs_ps"), 1)
                for g in range(2):
                    mm(PS[:, 2 + g, 0:T], XBC[:, 8 + g, 0:P], XBC[:, 10 + g, :], start=True, stop=True)
                    mm(PS[:, 2 + g, T:MW], XBC[:, 8 + g, P:T], XBC[:, 10 + g, P:T], start=True, stop=True)\
                        .then_inc(S("cb_ps"), 1)
                pe.wait_ge(S("cbm"), 2)
                pe.wait_ge(S("xd"), 4)
                pe.wait_ge(S("acd"), 1)

                def spread(h):
                    if h >= 2:
                        pe.wait_ge(S("decay"), h - 1)
                    mm(PS[:, 4 + h % 2, 0:T], bc(ID[0:16, h:h + 1], (16, P)), AC[0:16, :], start=True, stop=True)\
                        .then_inc(S("spread"), 1)

                def head(h):
                    pe.wait_ge(S("mt"), h + 1)
                    if h % 2 == 0 and h >= 4:
                        pe.wait_ge(S("ys"), h // 2 - 1)
                    o = 64 * (h % 2)
                    b = 6 + (h // 2) % 2
                    mm(PS[o:o + 64, b, 0:T], RG_XD[:, 0, 64 * h:64 * h + 64], EH[:, h % 2, 0:T],
                       start=True, stop=False)
                    mm(PS[o:o + 64, b, P:T], RG_XD[:, 1, 64 * h:64 * h + 64], EH[:, h % 2, T:MW],
                       start=False, stop=True).then_inc(S("head_ps"), 1)

                for h in range(17):
                    if h < 16:
                        spread(h)
                    if h >= 1:
                        head(h - 1)
                pe.wait_ge(S("sq"), 1)
                for g in range(2):
                    for j in range(4):
                        ins = mm(PS[:, 4 + g, 0:T], ONES[:, 0:P], XBC[:, 4 * g + j, :], start=j == 0, stop=j == 3)
                    ins.then_inc(S("sq_ps"), 1)
                pe.wait_ge(S("y_hyb"), 1)
                out_rows(r, r.n + 7, r.end, [GA[:, k, :] for k in range(8)] + [ZH[:, k, :] for k in range(8)])

            def mlstm(r):
                trn(r.u, XN)
                gate_row(r)
                project_tiles(r, MT_TILES, 4096)
                pe.wait_ge(S("xc"), 1)
                for h in range(4):
                    pe.wait_ge(S("bd"), h + 1)
                    for w in range(3):
                        for j in range(4):
                            q = (h * 3 + w) * 4 + j
                            b = 2 + q % 4
                            if q >= 4:
                                pe.wait_ge(S("qkv1"), q - 3)
                            src = XM[:, 4 * h + j, 3:] if w == 2 else XC[:, 4 * h + j, :]
                            mm(PS[:, b, 0:T], BD[:, w, j, :], src, start=True, stop=True).then_inc(S("qkv1_ps"), 1)
                            if q >= 1:
                                gates_add(q - 1)
                gates_add(47)
                pe.wait_ge(S("gtok_in"), 1)
                for m in range(2):
                    for t in range(TT):
                        ins = nc.tensor.transpose(PS[:, 2, 8 * m + 4 * t:8 * m + 4 * t + 4],
                                                  MR[0:4, 2 + m, t * P:(t + 1) * P], ID[0:4, 0:4])
                ins.then_inc(S("gtok_ps"), 1)
                pe.wait_ge(S("gtok"), 1)
                for h in range(4):
                    pe.wait_ge(S("bd"), 4 + h + 1)
                    for w in range(2):
                        for j in range(4):
                            q = w * 4 + j
                            if q >= 2:
                                pe.wait_ge(S("qk2"), 8 * h + q - 1)
                            mm(PS[:, q % 2, 0:T], BD[:, w, j, :], XC[:, 4 * h + j, :], start=True, stop=True)\
                                .then_inc(S("qk2_ps"), 1)
                    for t in range(TT):
                        for j in range(4):
                            ins = mm(PS[:, 2 + t, j * P:(j + 1) * P], XM[:, 4 * h + j, 3 + t * P:3 + (t + 1) * P],
                                     BD[:, 2, j, :], start=True, stop=True)
                        ins.then_inc(S("v2_ps"), 1)
                    mm(PS[:, 4, 0:T], bc(ID[0:4, h:h + 1], (4, P)), MR[0:4, 1, :], start=True, stop=True)\
                        .then_inc(S("mspread"), 1)
                    pe.wait_ge(S("qk2"), 8 * (h + 1))
                    for c, (s0, t0, t1) in enumerate(((0, 0, T), (P, P, T))):
                        for j in range(4):
                            ins = mm(PS[:, 5, 0 + c * T:c * T + t1 - t0], NQ[:, 4 + j, s0:s0 + P], NQ[:, j, t0:t1],
                                     start=j == 0, stop=j == 3)
                    ins.then_inc(S("kq_ps"), 1)
                    pe.wait_ge(S("pm"), h + 1)
                    pe.wait_ge(S("v2"), 2 * (h + 1))
                    for t in range(TT):
                        for s in range(t + 1):
                            c0 = s * T if t == s else P
                            lhs = PM[:, c0:c0 + P]
                            mm(PS[:, 6 + t, :], lhs, VM[:, s, :], start=s == 0, stop=s == t)
                    for t in range(TT):
                        for s in range(t + 1):
                            c0 = s * T if t == s else P
                            ins = mm(PS[:, 4, t:t + 1], PM[:, c0:c0 + P], ONES[:, 0:1], start=s == 0, stop=s == t)
                    ins.then_inc(S("num_ps"), 1)
                    pe.wait_ge(S("hn"), h + 1)
                    for j in range(4):
                        for t in range(TT):
                            ins = nc.tensor.transpose(PS[:, 2 + j // 2, (j % 2) * T + t * P:(j % 2) * T + (t + 1) * P],
                                                      HN[:, t, j * P:(j + 1) * P], ID)
                    ins.then_inc(S("hn_ps"), 1)
                    pe.wait_ge(S("ym"), h + 1)
                out_rows(r, r.n + 6, r.end, [ZM[:, k, :] for k in range(16)])

            def gates_add(q):
                h, w, j = q // 12, q // 4 % 3, q % 4
                pe.wait_ge(S("qkv1"), q + 1)
                for m in range(2):
                    ins = mm(PS[0:4, m, 0:T], WGT[:, w * 16 + 4 * h + j, 4 * m:4 * m + 4], NQ[:, q % 8, :],
                             start=q == 0, stop=q == 47)
                ins.then_inc(S("gadd"), 1)

            columns()
            for r in plan:
                {"even": even, "odd": odd, "moe": moe, "ada": ada, "ffn": ffn, "hyb": hyb, "mlstm": mlstm}[r.kind](r)

        BN = ST[:, 0:24].rearrange("p (t h s) -> p t h s", t=TT, h=2)
        MV = ST[:, 24:28].rearrange("p (t s) -> p t s", t=TT)
        VAR, SD, RSTD, SSQ = ST[:, 28:30], ST[:, 30:32], ST[:, 32:34], ST[:, 34:36]
        NM = ST[:, 36:40].rearrange("p (b t) -> p b t", b=2)
        SM = ST[:, 40:44].rearrange("p (b t) -> p b t", b=2)
        ES = ST[:, 44:48].rearrange("p (b t) -> p b t", b=2)
        RC = ST[:, 48:52].rearrange("p (b t) -> p b t", b=2)
        SSQ4 = ST[:, 52:56]
        CACT = ST[:, 56:64]
        NSINK = ST[:, 64:72]
        WI = ST[:, 72:80].rearrange("p (t h) -> p t h", t=TT)
        VAR4, SD4, RS4 = ST[:, 80:84], ST[:, 84:88], ST[:, 88:92]
        TICK = ST[0:1, 95:96]
        SPL = ST[:, 96:104]
        NSPL = ST[:, 104:112]
        SPA = [ST[:, 112 + 8 * i:120 + 8 * i] for i in range(5)]
        ENM = ST[:, 152:160].rearrange("p (t h) -> p t h", t=TT)
        GTOK = ST[:, 160:176].rearrange("p (m t h) -> p m t h", m=2, t=TT)
        DEN = ST[:, 176:178]
        M8 = ST[:, 178:186]

        @block.scalar
        def _(act):
            L = Lane(act, "act")
            c = L.c
            count = {"sqrt": 0, "sp": 0, "tile": 0, "ssq": 0}

            f = nc.scalar.activation

            def root(out_, in_):
                count["sqrt"] += 1
                act.wait_ge(S("var"), count["sqrt"])
                f(out_, in_, ACT.Sqrt).then_inc(S("sd"), 1)

            def softplus_exp(e, a_):
                count["sp"] += 1
                act.wait_ge(S("sp_a"), count["sp"])
                f(e, a_, ACT.Exp, scale=-1.0).then_inc(S("sp_e"), 1)

            def trn_out(r, u, mod=False):
                for k in range(KD):
                    act.wait_ge(S("xt_ps"), 4 * u + k // 2 + 1)
                    src = PS[:, 4 + k // 2, (k % 2) * T:(k % 2 + 1) * T]
                    if mod:
                        i = r.layer * 3 + r.sub
                        f(XT[:, k, :], src, ACT.Identity, scale=MODA[:, i, k:k + 1],
                          bias=MOD[:, r.layer, r.sub * 24 + k:r.sub * 24 + k + 1]).then_inc(S("xt"), 1)
                    else:
                        f(XT[:, k, :], src, ACT.Copy).then_inc(S("xt"), 1)

            def squares(r):
                act.wait_ge(S("xres"), r.v2 + 1)
                for t in range(TT):
                    f(XN[:, t, :], X[:, t, :], ACT.Square, accum_out=SSQ[:, t:t + 1]).then_inc(S("ssq"), 1)
                root(SD, VAR)

            def gate_row_out(r):
                act.wait_ge(S("row_ps"), r.v2 + 1)
                f(ROWB[:, 0, :], PS[:, 6:8, :].rearrange("p j n -> p (j n)"), ACT.Copy).then_inc(S("row"), 1)

            def attention(r, units):
                n = len(units)
                for i in range(n + 1):
                    if i < n:
                        u, w, b = r.ub + i, units[i], i % 2
                        act.wait_ge(S("qk_ps"), u + 1)
                        if u >= 2:
                            act.wait_ge(S("scores"), u - 1)
                        f(QK[0:w.dk, b, 0:T], PS[0:w.dk, b, 0:T], ACT.Copy, scale=w.scale).then_inc(S("qk"), 1)
                        f(QK[0:w.dk, b, T:2 * T], PS[0:w.dk, b, T:2 * T], ACT.Copy).then_inc(S("qk"), 1)
                    if i >= 1:
                        u, w, b = r.ub + i - 1, units[i - 1], (i - 1) % 2
                        act.wait_ge(S("nm"), u + 1)
                        if u >= 2:
                            act.wait_ge(S("pt_ps"), u - 1)
                        if w.kind == "window":
                            c(f(ES[:, b, :], NM[:, b, :], ACT.Exp, bias=SINK[:, w.h:w.h + 1]))
                        for t, (c0, c1) in enumerate(BLK):
                            f(PB[:, b, c0:c1], LG[:, b, c0:c1], ACT.Exp, bias=NM[:, b, t:t + 1],
                              accum_out=SM[:, b, t:t + 1]).then_inc(S("p"), 1)

            def even(r):
                trn_out(r, r.u)
                for i in range(3):
                    act.wait_ge(S("w_used"), 2 * (r.n + i + 1))
                    f(TM[:, :, PW * i:PW * (i + 1)],
                      PS[:, 4 * (i % 2):4 * (i % 2) + 4, :].rearrange("p (t h) n -> p t (h n)", t=TT)[:, :, 0:PW],
                      ACT.Copy).then_inc(S("tm_even"), 1)
                softplus_exp(SPW[0:8, 2, :], SPW[0:8, 1, :])
                attention(r, units_of("even"))
                trn_out(r, r.u + 1)
                root(SD, VAR)

            def odd(r):
                trn_out(r, r.u)
                for i, w in enumerate((PW, ODD_IN - PW)):
                    act.wait_ge(S("w_used"), 2 * (r.n + i + 1))
                    f(TMO[:, :, PW * i:PW * i + w],
                      PS[:, 4 * i:4 * i + 4, :].rearrange("p (t h) n -> p t (h n)", t=TT)[:, :, 0:w],
                      ACT.Copy).then_inc(S("tm_odd"), 1)
                act.wait_ge(S("tm_odd"), 2)
                for m, (c0, c1) in enumerate(((964, 1220), (1220, 1348))):
                    for t in range(TT):
                        c(f(XN[:, 0, 0:c1 - c0], TMO[:, t, c0:c1], ACT.Square,
                            accum_out=SSQ4[:, 2 * m + t:2 * m + t + 1]))
                f(ST[0:1, 94:95], SSQ4[0:1, 0:1], ACT.Copy).then_inc(S("ssq4"), 1)
                act.wait_ge(S("qi_ps"), 1)
                for b in range(3):
                    m = 2 if b < 2 else 1
                    f(QIT[0:HD, 2 * b:2 * b + m, :],
                      PS[0:HD, b, 0:m * T].rearrange("p (m t) -> p m t", m=m), ACT.Copy).then_inc(S("qit"), 1)
                root(SD4, VAR4)
                act.wait_ge(S("cqt_ps"), 1)
                for k in range(3):
                    g = col("odd_q_norm", k) if k < 2 else col("odd_kv_norm")
                    f(CQT[:, k, :], PS[:, k, 0:T], ACT.Copy, scale=g).then_inc(S("cqt"), 1)
                act.wait_ge(S("dq_ps"), 1)
                f(DQ.rearrange("p t h d -> p t (h d)"),
                  PS[:, 4:8, :].rearrange("p (t h) n -> p t (h n)", t=TT)[:, :, 0:768], ACT.Copy).then_inc(S("dq"), 1)
                act.wait_ge(S("dkv_ps"), 1)
                f(DKV.rearrange("p t h d -> p t (h d)"),
                  PS[:, 0:4, :].rearrange("p (t h) n -> p t (h n)", t=TT), ACT.Copy).then_inc(S("dkv"), 1)
                attention(r, units_of("odd"))
                trn_out(r, r.u + 1)
                root(SD, VAR)

            def silus(r, groups):
                def silu(i, j):
                    act.wait_ge(S("gate_up"), i * 8 + (r.cb + j + 1))
                    if j >= 2 or not isinstance(i, int) or i > 0:
                        act.wait_ge(S("hidden"), i * 8 + (r.cb + j - 1))
                    f(SG[:, j % 2, :], PS[:, 4 + j % 4, 0:T], ACT.Silu).then_inc(S("silu"), 1)

                turns, rest = divmod(groups, SLOTS)
                if turns <= 2:
                    for k in range(CH * groups):
                        silu(k // 8, k % 8)
                    return
                for j in range(8):
                    silu(0, j)
                with act.Fori(1, turns, 1) as i:
                    for j in range(8):
                        silu(i, j)

            def moe(r):
                trn_out(r, r.u)
                act.wait_ge(S("route_ps"), r.me + 1)
                f(RT[:, 0, :], PS[:, 4, 0:TT * NE], ACT.Sigmoid).then_inc(S("aff"), 1)
                act.wait_ge(S("gates_ps"), r.me + 1)
                f(GT[0:NE, :], PS[0:NE, 5, 0:T], ACT.Copy).then_inc(S("gates_t"), 1)
                for k in range(8):
                    act.wait_ge(S("rows_ps"), 8 * r.me + k + 1)
                    f(GB[:, 2 * k:2 * k + 2, :], PS[:, 4 + k % 4, :].rearrange("p (e t) -> p e t", e=2),
                      ACT.Copy).then_inc(S("gate_rows"), 1)
                silus(r, MOE_G)
                root(SD, VAR)

            def ffn(r):
                squares(r)
                trn_out(r, r.u, True)
                gate_row_out(r)
                silus(r, FFN_G)

            def ada(r):
                act.wait_ge(S("cols"), ROW_TILES)
                f(CACT, col("c_2", 0, KD), ACT.Silu).then_inc(S("c_act"), 1)

            def tiles_out(r, tiles, where):
                conv = 0
                for k in range(len(tiles)):
                    tile_done(act, r, tiles, k)
                    dst, is_conv = where(k)
                    if is_conv:
                        if conv >= 2:
                            act.wait_ge(S("conv"), conv - 1)
                        conv += 1
                    f(dst, PS[:, k % 8, 0:T], ACT.Copy).then_inc(S("tile_out"), 1)

            def hyb(r):
                squares(r)
                trn_out(r, r.u, True)
                gate_row_out(r)

                def where(k):
                    if k < 8:
                        return GA[:, k, :], False
                    if k < 16:
                        return RAW[:, k % 2, 3:], True
                    if k < 24:
                        return ZH[:, k - 16, :], False
                    return RAW[:, k % 2, 3:], True

                act.wait_ge(S("pads"), 1)
                tiles_out(r, HT_TILES, where)
                softplus_exp(SPA[1], SPA[0])
                for i in range(8):
                    act.wait_ge(S("lru_ps"), i + 1)
                    b = 2 + i % 2
                    f(RG[:, i, :], PS[:, b, 0:T], ACT.Sigmoid, bias=col("lru_ba_2", i)).then_inc(S("lru_gates"), 1)
                    f(IG[:, i, :], PS[:, b, T:2 * T], ACT.Sigmoid, bias=col("lru_bx_2", i)).then_inc(S("lru_gates"), 1)
                act.wait_ge(S("spl"), 1)
                act.wait_ge(S("lru_gates"), 16)
                for i in range(8):
                    f(H1[:, i, :], RG[:, i, :], ACT.Exp, scale=NSPL[:, i:i + 1])
                for i in range(8):
                    c(f(RG[:, i, :], RG[:, i, :], ACT.Tanh, scale=SPL[:, i:i + 1]))
                f(ST[0:1, 94:95], ST[0:1, 96:97], ACT.Copy).then_inc(S("lru_at"), 1)
                root(RG, RG)
                act.wait_ge(S("gelu_in"), 1)
                f(H2, H2, ACT.Tanh, scale=0.7978845608028654).then_inc(S("gelu_tanh"), 1)
                act.wait_ge(S("conv"), 20)
                f(XBC, XBC, ACT.Silu).then_inc(S("xbc"), 1)
                f(ZH, ZH, ACT.Silu).then_inc(S("zsilu"), 1)
                f(BF[0:16, 5:6], BF[0:16, 2:3], ACT.Exp).then_inc(S("a_exp"), 1)
                softplus_exp(SPH[0:16, 1, :], SPH[0:16, 0, :])
                for h in range(16):
                    act.wait_ge(S("decay"), h + 1)
                    f(EH[:, h % 2, :], EH[:, h % 2, :], ACT.Exp).then_inc(S("eh"), 1)
                root(H2_RS, H2_RS)

            def mlstm(r):
                squares(r)
                trn_out(r, r.u, True)
                gate_row_out(r)
                tiles_out(r, MT_TILES, lambda k: (XM[:, k, 3:], False) if k < 16 else (ZM[:, k - 16, :], False))
                act.wait_ge(S("mconv"), 16)
                f(XC, XC, ACT.Silu).then_inc(S("xc"), 1)
                act.wait_ge(S("tile_out"), EV_BASE["mlstm"] + 32)
                f(ZM, ZM, ACT.Silu).then_inc(S("zm"), 1)
                for q in range(48):
                    act.wait_ge(S("qkv1_ps"), q + 1)
                    if q >= 8:
                        act.wait_ge(S("gadd"), q - 7)
                    f(NQ[:, q % 8, :], PS[:, 2 + q % 4, 0:T], ACT.Copy).then_inc(S("qkv1"), 1)
                softplus_exp(SPX[0:4, 1, :], SPX[0:4, 0, :])
                act.wait_ge(S("gtok"), 1)
                f(ENM, GTOK[:, 1, :, :], ACT.Exp, scale=-1.0).then_inc(S("enm"), 1)
                for h in range(4):
                    if h == 0:
                        act.wait_ge(S("gadd"), 48)
                    else:
                        act.wait_ge(S("kq_ps"), h)
                    for q in range(8):
                        act.wait_ge(S("qk2_ps"), 8 * h + q + 1)
                        f(NQ[:, q, :], PS[:, q % 2, 0:T], ACT.Copy).then_inc(S("qk2"), 1)
                    for t in range(TT):
                        act.wait_ge(S("v2_ps"), 2 * h + t + 1)
                        if h == 0:
                            act.wait_ge(S("v_free"), 1)
                        f(VM[:, t, :], PS[:, 2 + t, :], ACT.Copy).then_inc(S("v2"), 1)
                    act.wait_ge(S("em"), h + 1)
                    f(EM, EM, ACT.Exp).then_inc(S("em_exp"), 1)
                    root(SD, VAR)

            def final():
                act.wait_ge(S("xres"), v2_end + 1)
                for t in range(TT):
                    f(XN[:, t, :], X[:, t, :], ACT.Square, accum_out=SSQ[:, t:t + 1]).then_inc(S("ssq"), 1)
                root(SD, VAR)

            for r in plan:
                {"even": even, "odd": odd, "moe": moe, "ada": ada, "ffn": ffn, "hyb": hyb, "mlstm": mlstm}[r.kind](r)
            if FINAL:
                final()

        @block.vector
        def _(dve):
            L = Lane(dve, "dve")
            c = L.c
            V = nc.vector
            count, marks = {"var": 0, "sp": 0, "ssq": 0, "ln": 0}, [0]

            def mark():
                marks[0] += 1
                return V.memset(MARKS[0:1, marks[0]:marks[0] + 1], 0.0)

            def ts(out_, in_, s1, s2=None, o1=ALU.mult, o2=None):
                return V.tensor_scalar(out_, in_, s1, s2, o1, o2) if o2 is not None else \
                    V.tensor_scalar(out_, in_, s1, s2, o1)

            def tt(out_, x_, y_, op=ALU.mult):
                return V.tensor_tensor(out_, x_, y_, op)

            def stt(out_, x_, s, y_, o1, o2):
                return V.scalar_tensor_tensor(out=out_, in0=x_, scalar=s, in1=y_, op0=o1, op1=o2)

            def root(rstd, sd):
                count["var"] += 1
                mark().then_inc(S("var"), 1)
                dve.wait_ge(S("sd"), count["var"])
                c(V.reciprocal(rstd, sd))

            def softplus(out_, x_, a_, e, d, w):
                count["sp"] += 1
                c(ts(a_, x_, -1.0))
                c(tt(a_, a_, x_, ALU.max))
                mark().then_inc(S("sp_a"), 1)
                dve.wait_ge(S("sp_e"), count["sp"])
                c(ts(d, e, 2.0, None, ALU.add))
                c(V.reciprocal(d, d))
                c(tt(e, e, d))
                c(tt(w, e, e))
                c(ts(d, w, 1.0 / 17))
                for k in range(7, 0, -1):
                    c(stt(d, d, 1.0 / (2 * k + 1), w, ALU.add, ALU.mult))
                c(stt(d, d, 1.0, e, ALU.add, ALU.mult))
                c(ts(w, x_, 0.0, None, ALU.max))
                c(stt(out_, d, 2.0, w, ALU.mult, ALU.add))

            def residual_norm(r):
                dve.wait_ge(S("w_used"), 2 * r.end)
                c(stt(X[:, :, :], X[:, :, :], ALPHA, PSY, ALU.mult, ALU.add))
                for t in range(TT):
                    for h in range(2):
                        c(V.bn_stats(BN[:, t, h, :], X[:, t, 512 * h:512 * h + 512]))
                    c(V.bn_aggr(MV[:, t, :], BN[:, t, :, :]))
                c(ts(VAR, MV[:, :, 1], LN_EPS, None, ALU.add))
                root(RSTD, SD)
                for t in range(TT):
                    c(ts(X[:, t, :], X[:, t, :], MV[:, t, 0:1], RSTD[:, t:t + 1], ALU.subtract, ALU.mult))
                count["ln"] += 1
                dve.wait_ge(S("ln_load"), 32 * count["ln"])
                for t in range(TT):
                    c(tt(X[:, t, :], X[:, t, :], ROWB[:, 0, :]))
                    c(tt(X[:, t, :], X[:, t, :], ROWB[:, 1, :], ALU.add))
                mark().then_inc(S("ln_done"), 1)

            def rms():
                mark().then_inc(S("xres"), 1)
                count["ssq"] += 2
                dve.wait_ge(S("ssq"), count["ssq"])
                c(ts(VAR, SSQ, 1.0 / D, EPS, ALU.mult, ALU.add))
                root(RSTD, SD)
                for t in range(TT):
                    c(ts(XN[:, t, :], X[:, t, :], RSTD[:, t:t + 1]))

            def begin(r):
                rms()
                mark().then_inc(S("xn"), 1)
                i = r.layer * 3 + r.sub
                c(tt(DG, bc(ID.unsqueeze(1), (P, KD, P)), bc(MODG[:, i, :].unsqueeze(2), (P, KD, P))))
                mark().then_inc(S("diag"), 1)

            def residual_gate(r):
                dve.wait_ge(S("w_used"), 2 * r.end)
                for t in range(TT):
                    c(tt(XN[:, t, :], PSY[:, t, :], ROWB[:, 0, :]))
                    c(tt(X[:, t, :], X[:, t, :], XN[:, t, :], ALU.add))

            def attention(r, units):
                n = len(units)
                for i in range(n + 2):
                    if i >= 2:
                        u, w, b = r.ub + i - 2, units[i - 2], i % 2
                        dve.wait_ge(S("p"), 2 * (u + 1))
                        if w.kind == "window":
                            c(tt(SM[:, b, :], SM[:, b, :], ES[:, b, :], ALU.add))
                        c(V.reciprocal(RC[:, b, :], SM[:, b, :]))
                        dve.wait_ge(S("o_ps"), u + 1)
                        tt(XN[:, :, w.at:w.at + HD], PS[:, 6 + b, 0:2 * HD].rearrange("p (t d) -> p t d", t=TT),
                           bc(RC[:, b, :].unsqueeze(2), (P, TT, HD))).then_inc(S("o"), 1)
                    if i < n:
                        u, w, b = r.ub + i, units[i], i % 2
                        dve.wait_ge(S("scores"), u + 1)
                        if u >= 2:
                            dve.wait_ge(S("p"), 2 * (u - 1))
                        s, lg = PS[:, 2 + b, 0:MW], LG[:, b, :]
                        slope = 2.0 ** -(w.h + 1)
                        if w.kind == "window":
                            stt(lg, CON[:, C_NEGW:C_NEGW + MW], slope, s, ALU.mult, ALU.add).then_inc(S("logits"), 1)
                        elif w.kind == "dsa":
                            stt(lg, CON[:, C_NEGC:C_NEGC + MW], slope, s, ALU.mult, ALU.add).then_inc(S("logits"), 1)
                            dve.wait_ge(S("logits"), u + 1)
                            c(tt(lg, lg, SELM, ALU.add))
                        elif w.kind == "mla":
                            tt(lg, s, CON[:, C_CAUS:C_CAUS + MW], ALU.add).then_inc(S("logits"), 1)
                        else:
                            for t, (c0, c1) in enumerate(BLK):
                                ins = stt(lg[:, c0:c1], s[:, c0:c1], CTOK[:, t, w.h:w.h + 1],
                                          CON[:, C_CAUS + c0:C_CAUS + c1], ALU.add, ALU.add)
                                if t == 0:
                                    c(ins)
                            ins.then_inc(S("logits"), 1)
                        dve.wait_ge(S("logits"), u + 1)
                        for t, (c0, c1) in enumerate(BLK):
                            ins = V.tensor_reduce(NM[:, b, t:t + 1], lg[:, c0:c1], AX.X, ALU.max, negate=True)
                            if t == 0 or w.kind == "window":
                                c(ins)
                        if w.kind == "window":
                            ins = ts(NM[:, b, :], NM[:, b, :], NSINK[:, w.h:w.h + 1], None, ALU.min)
                        ins.then_inc(S("nm"), 1)
                    if 1 <= i <= n:
                        u, b = r.ub + i - 1, (i - 1) % 2
                        dve.wait_ge(S("pt_ps"), u + 1)
                        if u >= 2:
                            dve.wait_ge(S("o_ps"), u - 1)
                        V.tensor_copy(PT[:, b, :], PS[:, 4 + b, 0:MW]).then_inc(S("pt"), 1)
                dve.wait_ge(S("o"), r.ub + n)

            def even(r):
                mark().then_inc(S("xn"), 1)
                dve.wait_ge(S("w_used"), 2 * (r.n + 4))
                dve.wait_ge(S("small_load"), 16 * N_SMALL)
                c(ts(NSINK, SINK[:, :], -1.0))
                c(ts(SPW[0:8, 0, :], PS[0:8, 0, 0:T], -1.0, BF[0:8, 0:1], ALU.mult, ALU.subtract))
                softplus(SPW[0:8, 5, :], *[SPW[0:8, k, :] for k in range(5)])
                c(V.tensor_tensor_scan(NCT[0:8, :], ONES[0:8, :], SPW[0:8, 5, :], 0.0, ALU.mult, ALU.add))
                ts(CT[0:8, :], NCT[0:8, :], -1.0).then_inc(S("ct"), 1)
                dve.wait_ge(S("ct_ps"), 1)
                V.tensor_copy(CTOK.rearrange("p t h -> p (t h)"), PS[:, 1, 0:16]).then_inc(S("ctok"), 1)
                dve.wait_ge(S("ctok"), 1)
                attention(r, units_of("even"))
                mark().then_inc(S("xn"), 1)
                residual_norm(r)

            def rope(dst1, dst2, x1, x2, cos, sin, s4):
                for s_, (x_, y_) in zip(s4, ((x1, cos), (x2, sin), (x1, sin), (x2, cos))):
                    c(tt(s_, x_, y_))
                c(tt(dst1, s4[0], s4[1], ALU.subtract))
                c(tt(dst2, s4[2], s4[3], ALU.add))

            def odd(r):
                mark().then_inc(S("xn"), 1)
                dve.wait_ge(S("ssq4"), 1)
                c(ts(VAR4[:, 0:2], SSQ4[:, 0:2], 1.0 / 256, EPS, ALU.mult, ALU.add))
                c(ts(VAR4[:, 2:4], SSQ4[:, 2:4], 1.0 / 128, EPS, ALU.mult, ALU.add))
                root(RS4, SD4)
                for t in range(TT):
                    c(ts(CQN[:, t, 0:2, :].rearrange("p k d -> p (k d)"), TMO[:, t, 964:1220], RS4[:, t:t + 1]))
                    c(ts(CQN[:, t, 2, :], TMO[:, t, 1220:1348], RS4[:, 2 + t:3 + t]))
                mark().then_inc(S("cqn"), 1)
                c(ts(WI, TMO[:, :, 960:964], 1.0 / 16))
                for h in range(4):
                    dve.wait_ge(S("dots"), h + 1)
                    for t, (c0, c1) in enumerate(BLK):
                        dst = SCR if h == 0 else TMPS
                        c(ts(dst[:, c0:c1], PS[:, 4 + h, c0:c1], 0.0, WI[:, t, h:h + 1], ALU.max, ALU.mult))
                    if h:
                        c(tt(SCR, SCR, TMPS, ALU.add))
                c(tt(SCR, SCR, CON[:, C_CAUS:C_CAUS + MW], ALU.add))
                for c0, c1 in BLK:
                    for _k in range(8):
                        c(V.max(M8, SCR[:, c0:c1]))
                        c(V.match_replace(SCR[:, c0:c1], M8, SCR[:, c0:c1], -3.0e38))
                c(ts(SELM, SCR, -2.0e38, None, ALU.is_le))
                c(ts(SELM, SELM, 1.0, -NEG, ALU.subtract, ALU.mult))
                mark().then_inc(S("dsa"), 1)
                dve.wait_ge(S("dq"), 1)
                s4 = [SCR[:, 128 * i:128 * i + 128] for i in range(3)] + [TMPS[:, 0:128]]
                for t in range(TT):
                    cos = CON[:, C_COS + 16 * t:C_COS + 16 * t + 16]
                    sin = CON[:, C_SIN + 16 * t:C_SIN + 16 * t + 16]
                    rope(DQ[:, t, :, 64:80], DQ[:, t, :, 80:96], DQ[:, t, :, 64:80], DQ[:, t, :, 80:96],
                         bc(cos.unsqueeze(1), (P, 8, 16)), bc(sin.unsqueeze(1), (P, 8, 16)),
                         [s_.rearrange("p (h d) -> p h d", h=8) for s_ in s4])
                    rope(TMPS[:, 128:144], TMPS[:, 144:160], TMO[:, t, 1348:1364], TMO[:, t, 1364:1380], cos, sin,
                         [s_[:, 0:16] for s_ in s4])
                    c(V.tensor_copy(DK[:, t, :, 64:96], bc(TMPS[:, 128:160].unsqueeze(1), (P, 8, 32))))
                dve.wait_ge(S("dkv"), 1)
                c(V.tensor_copy(DK[:, 0, :, 0:64], DKV[:, 0, :, 0:64]))
                c(V.tensor_copy(DK[:, 1, :, 0:64], DKV[:, 1, :, 0:64]))
                mark().then_inc(S("mla_ready"), 1)
                attention(r, units_of("odd"))
                mark().then_inc(S("xn"), 1)
                residual_norm(r)

            def first_of(dst, x_, m, tie, n, tmp):
                c(V.tensor_reduce(m, x_, AX.X, ALU.max))
                c(tt(tmp, x_, bc(m.unsqueeze(2), (P, TT, n)), ALU.is_equal))
                c(tt(tmp, tmp, bc(tie.unsqueeze(1), (P, TT, n))))
                c(V.tensor_reduce(m, tmp, AX.X, ALU.max))
                c(tt(dst, tmp, bc(m.unsqueeze(2), (P, TT, n)), ALU.is_equal))

            def route(r):
                v = [RT[:, k, :].rearrange("p (t e) -> p t e", t=TT) for k in range(12)]
                aff, sel, one1, one2, tmp, w = v[0], v[1], v[2], v[3], v[4], v[5]
                grp, gone, gtmp = v[6][:, :, 0:4], v[7][:, :, 0:4], v[8][:, :, 0:4]
                m = RT[:, 9, 0:2]
                dve.wait_ge(S("aff"), r.me + 1)
                dve.wait_ge(S("small_load"), 16 * N_SMALL)
                c(tt(sel, aff, bc(RB[:, :].unsqueeze(1), (P, TT, NE)), ALU.add))
                q = sel.rearrange("p t (g e) -> p t g e", g=4)
                for k, (i, j) in enumerate(((0, 1), (0, 2), (0, 3), (1, 2), (1, 3), (2, 3))):
                    c(tt(RP[:, :, :, k], q[:, :, :, i], q[:, :, :, j], ALU.add))
                c(V.tensor_reduce(grp, RP, AX.X, ALU.max))
                first_of(gone, grp, m, CON[:, C_TIE:C_TIE + 4], 4, gtmp)
                c(ts(gone, gone, 1.0, -NEG, ALU.subtract, ALU.mult))
                for t in range(TT):
                    c(tt(sel[:, t, :].rearrange("p (g e) -> p g e", g=4), sel[:, t, :].rearrange("p (g e) -> p g e", g=4),
                         bc(gone[:, t, :].unsqueeze(2), (P, 4, 4)), ALU.add))
                first_of(one1, sel, m, CON[:, C_TIE:C_TIE + NE], NE, tmp)
                c(stt(sel, one1, 10 * NEG, sel, ALU.mult, ALU.add))
                first_of(one2, sel, m, CON[:, C_TIE:C_TIE + NE], NE, tmp)
                c(tt(one1, one1, one2, ALU.add))
                c(tt(w, one1, aff))
                c(V.tensor_reduce(m, w, AX.X, ALU.add))
                c(V.reciprocal(m, m))
                c(tt(v[11], w, bc(m.unsqueeze(2), (P, TT, NE))))
                mark().then_inc(S("gates"), 1)

            def hiddens(r, groups, gated):
                def hid(i, j):
                    dve.wait_ge(S("silu"), i * 8 + (r.cb + j + 1))
                    if j >= 2 or not isinstance(i, int) or i > 0:
                        dve.wait_ge(S("w_used"), i * 8 + (2 * r.n + j - 1))
                    sg = SG[:, j % 2, :]
                    if gated:
                        g = GB[:, bass.ds(i * 2 + j // 4, 1), :].rearrange("p a t -> p (a t)")
                        tt(sg, sg, g).then_inc(S("gated"), 1)
                        dve.wait_ge(S("gated"), i * 8 + (r.me * CH * MOE_G + j + 1))
                    tt(HT[:, j % 2, :], sg, PS[:, 4 + j % 4, T:2 * T]).then_inc(S("hidden"), 1)

                turns, rest = divmod(groups, SLOTS)
                if turns <= 2:
                    for k in range(CH * groups):
                        hid(k // 8, k % 8)
                    return
                for j in range(8):
                    hid(0, j)
                with dve.Fori(1, turns, 1) as i:
                    for j in range(8):
                        hid(i, j)

            def moe(r):
                mark().then_inc(S("xn"), 1)
                route(r)
                dve.wait_ge(S("gate_rows"), 8 * (r.me + 1))
                hiddens(r, MOE_G, True)
                residual_norm(r)

            def ffn(r):
                begin(r)
                hiddens(r, FFN_G, False)
                residual_gate(r)

            def ada(r):
                dve.wait_ge(S("w_used"), 2 * r.end)
                for l in range(2):
                    c(tt(MOD[:, l, :], PS[:, 4 + l, 0:72], col("ada_b_2", 72 * l, 72), ALU.add))
                    for s in range(3):
                        i = 3 * l + s
                        c(stt(MODA[:, i, :], MOD[:, l, 24 * s + 8:24 * s + 16], 1.0, col("norm_g_2", 8 * i, 8),
                              ALU.add, ALU.mult))
                        c(ts(MODG[:, i, :], MOD[:, l, 24 * s + 16:24 * s + 24], 1.0, 1.0 if s == 1 else 0.5,
                             ALU.add, ALU.mult))

            def conv4(dst, x_, w, b, n, i, sem):
                c(ts(dst, x_[:, 3:3 + T], col(w, 3 * n + i), col(b, i), ALU.mult, ALU.add))
                for k in (2, 1):
                    c(stt(dst, x_[:, k:k + T], col(w, k * n + i), dst, ALU.mult, ALU.add))
                stt(dst, x_[:, 0:T], col(w, i), dst, ALU.mult, ALU.add).then_inc(S(sem), 1)

            def hyb(r):
                begin(r)
                c(V.memset(RAW[:, :, 0:3], 0.0))
                mark().then_inc(S("pads"), 1)
                q = 0
                for k in list(range(8, 16)) + list(range(24, 36)):
                    dve.wait_ge(S("tile_out"), EV_BASE["hyb"] + k + 1)
                    if k < 16:
                        conv4(XL[:, k - 8, :], RAW[:, k % 2, :], "lru_conv_w_2", "lru_conv_b_2", 8, k - 8, "conv")
                    else:
                        conv4(XBC[:, k - 24, :], RAW[:, k % 2, :], "ssd_conv_w_2", "ssd_conv_b_2", 12, k - 24, "conv")
                c(ts(SPA[4], col("lru_lambda_2", 0, 8), -1.0))
                softplus(SPL, SPA[4], SPA[0], SPA[1], SPA[2], SPA[3])
                c(ts(SPL, SPL, 8.0))
                c(ts(NSPL, SPL, -1.0))
                mark().then_inc(S("spl"), 1)
                dve.wait_ge(S("lru_at"), 1)
                c(ts(H2, RG, 1.0, None, ALU.add))
                c(V.reciprocal(H2, H2))
                c(stt(RG, RG, 2.0, H2, ALU.mult, ALU.mult))
                count["var"] += 1
                mark().then_inc(S("var"), 1)
                c(tt(IG[:, :, :], IG[:, :, :], XL))
                dve.wait_ge(S("sd"), count["var"])
                c(tt(IG[:, :, :], IG[:, :, :], RG))
                for i in range(8):
                    c(V.tensor_tensor_scan(XL[:, i, :], H1[:, i, :], IG[:, i, :], 0.0, ALU.mult, ALU.add))
                c(tt(H2, GA, GA))
                c(ts(H2, H2, 0.044715, 1.0, ALU.mult, ALU.add))
                c(tt(H2, H2, GA))
                mark().then_inc(S("gelu_in"), 1)
                dve.wait_ge(S("gelu_tanh"), 1)
                c(stt(H2, H2, 1.0, GA, ALU.add, ALU.mult))
                c(stt(GA, H2, 0.5, XL, ALU.mult, ALU.mult))
                dve.wait_ge(S("w_used"), 2 * (r.n + 7))
                dve.wait_ge(S("a_exp"), 1)
                c(ts(BF[0:16, 5:6], BF[0:16, 5:6], -1.0))
                c(ts(SPH[0:16, 4, :], PS[0:16, 0, 0:T], BF[0:16, 1:2], None, ALU.add))
                softplus(DTR[0:16, :], SPH[0:16, 4, :], *[SPH[0:16, k, :] for k in range(4)])
                c(ts(SPH[0:16, 4, :], DTR[0:16, :], BF[0:16, 5:6]))
                c(V.tensor_tensor_scan(AC[0:16, :], ONES[0:16, :], SPH[0:16, 4, :], 0.0, ALU.mult, ALU.add))
                mark().then_inc(S("ssd_rows"), 1)
                dve.wait_ge(S("acd_ps"), 1)
                V.tensor_copy(ACD, PS[:, 1, 0:64]).then_inc(S("acd"), 1)
                dve.wait_ge(S("acd"), 1)
                for t in range(TT):
                    for j in range(2):
                        dve.wait_ge(S("xs_ps"), 2 * t + j + 1)
                        tt(XN[:, t, 512 * j:512 * j + 512].rearrange("p (h d) -> p h d", h=8),
                           PS[:, 4 + 2 * t + j, :].rearrange("p (h d) -> p h d", h=8),
                           bc(ACD[:, 32 + 16 * t + 8 * j:32 + 16 * t + 8 * j + 8].unsqueeze(2), (P, 8, 64)))\
                            .then_inc(S("xd"), 1)
                for g in range(2):
                    dve.wait_ge(S("cb_ps"), g + 1)
                    tt(CBM[:, g, :], PS[:, 2 + g, 0:MW], CON[:, C_TRIT:C_TRIT + MW]).then_inc(S("cbm"), 1)
                dve.wait_ge(S("cbm"), 2)

                def ys(k):
                    dve.wait_ge(S("head_ps"), 2 * k + 2)
                    stt(XBC[:, k, :], XBC[:, k, :], SSDD[:, k:k + 1], PS[:, 6 + k % 2, 0:T], ALU.mult, ALU.add)\
                        .then_inc(S("ys"), 1)

                for h in range(17):
                    if h < 16:
                        dve.wait_ge(S("spread"), h + 1)
                        if h >= 2:
                            dve.wait_ge(S("head_ps"), h - 1)
                        b = 4 + h % 2
                        c(ts(EH[:, h % 2, 0:T], PS[:, b, 0:T], ACD[:, h:h + 1], 0.0, ALU.subtract, ALU.min))
                        ts(EH[:, h % 2, T:MW], PS[:, b, P:T], ACD[:, 16 + h:17 + h], 0.0, ALU.subtract, ALU.min)\
                            .then_inc(S("decay"), 1)
                    if h >= 1:
                        dve.wait_ge(S("eh"), h)
                        tt(EH[:, (h - 1) % 2, :], EH[:, (h - 1) % 2, :], CBM[:, (h - 1) // 8, :]).then_inc(S("mt"), 1)
                    if h >= 3 and h % 2 == 1:
                        ys((h - 3) // 2)
                ys(7)
                dve.wait_ge(S("ys"), 8)
                dve.wait_ge(S("zsilu"), 1)
                c(tt(ZH, ZH, XBC[:, 0:8, :]))
                c(tt(XBC[:, 0:8, :], ZH, ZH))
                mark().then_inc(S("sq"), 1)
                for g in range(2):
                    dve.wait_ge(S("sq_ps"), g + 1)
                    c(ts(H2_RS[:, g, :], PS[:, 4 + g, 0:T], 1.0 / 512, EPS, ALU.mult, ALU.add))
                root(H2_RS, H2_RS)
                for k in range(8):
                    c(stt(ZH[:, k, :], ZH[:, k, :], col("ssd_norm_g_2", k), H2_RS[:, k // 4, :], ALU.mult, ALU.mult))
                mark().then_inc(S("y_hyb"), 1)
                residual_gate(r)

            def mlstm(r):
                begin(r)
                c(V.memset(XM[:, :, 0:3], 0.0))
                for k in range(16):
                    dve.wait_ge(S("tile_out"), EV_BASE["mlstm"] + k + 1)
                    conv4(XC[:, k, :], XM[:, k, :], "mlstm_conv_w_2", "mlstm_conv_b_2", 16, k, "mconv")
                dve.wait_ge(S("mconv"), 16)

                def diag(n):
                    h = n % 4
                    dve.wait_ge(S("small_load"), 16 * N_SMALL)
                    if n >= 1:
                        dve.wait_ge(S("qkv1_ps"), 12 * min(n, 4))
                    if n >= 5:
                        dve.wait_ge(S("v2_ps"), 2 * (n - 4))
                    for w in range(3):
                        for j in range(4):
                            ins = tt(BD[:, w, j, :].rearrange("p (n o) -> p n o", o=4),
                                     bc(WQKV[:, w, 4 * h + j, :].unsqueeze(1), (P, 32, 4)),
                                     CON[:, C_BD:C_BD + 128].rearrange("p (n o) -> p n o", o=4))
                            if (w, j) != (2, 3):
                                c(ins)
                    ins.then_inc(S("bd"), 1)

                for h in range(4):
                    diag(h)
                dve.wait_ge(S("gadd"), 48)
                F_, NMR, G_, MR_ = (MR[0:4, k, :] for k in range(4))
                x_ = SPX[0:4, 4, :]
                c(ts(x_, PS[0:4, 1, 0:T], -1.0, BF[0:4, 4:5], ALU.mult, ALU.subtract))
                softplus(SPX[0:4, 5, :], x_, *[SPX[0:4, k, :] for k in range(4)])
                c(ts(SPX[0:4, 5, :], SPX[0:4, 5, :], -1.0))
                c(V.tensor_tensor_scan(F_, ONES[0:4, :], SPX[0:4, 5, :], 0.0, ALU.mult, ALU.add))
                c(stt(G_, PS[0:4, 0, 0:T], BF[0:4, 3:4], F_, ALU.add, ALU.subtract))
                c(V.tensor_tensor_scan(x_, ONES[0:4, :], G_, 0.0, ALU.mult, ALU.max))
                c(tt(MR_, F_, x_, ALU.add))
                c(ts(NMR, x_, -1.0))
                mark().then_inc(S("gtok_in"), 1)
                mark().then_inc(S("v_free"), 1)
                dve.wait_ge(S("gtok_ps"), 1)
                V.tensor_copy(GTOK.rearrange("p m t h -> p (m t h)"), PS[:, 2, 0:16]).then_inc(S("gtok"), 1)
                dve.wait_ge(S("gtok"), 1)
                for h in range(4):
                    diag(4 + h)
                    dve.wait_ge(S("mspread"), h + 1)
                    if h:
                        dve.wait_ge(S("num_ps"), h)
                    c(ts(EM[:, 0:T], PS[:, 4, 0:T], GTOK[:, 0, 0, h:h + 1], 0.0, ALU.add, ALU.min))
                    c(ts(EM[:, T:MW], PS[:, 4, P:T], GTOK[:, 0, 1, h:h + 1], 0.0, ALU.add, ALU.min))
                    mark().then_inc(S("em"), 1)
                    dve.wait_ge(S("em_exp"), h + 1)
                    c(tt(EM, EM, CON[:, C_TRIT:C_TRIT + MW]))
                    dve.wait_ge(S("kq_ps"), h + 1)
                    stt(PM, PS[:, 5, 0:MW], 512 ** -0.5, EM, ALU.mult, ALU.mult).then_inc(S("pm"), 1)
                    dve.wait_ge(S("num_ps"), h + 1)
                    dve.wait_ge(S("enm"), 1)
                    c(ts(DEN, PS[:, 4, 0:2], -1.0))
                    c(tt(DEN, DEN, PS[:, 4, 0:2], ALU.max))
                    c(tt(DEN, DEN, ENM[:, :, h], ALU.max))
                    c(V.reciprocal(DEN, DEN))
                    for t in range(TT):
                        c(ts(HN[:, t, :], PS[:, 6 + t, :], DEN[:, t:t + 1]))
                        c(V.bn_stats(BN[:, t, 0, :], HN[:, t, :]))
                        c(V.bn_aggr(MV[:, t, :], BN[:, t, 0, :]))
                    c(ts(VAR, MV[:, :, 1], EPS, None, ALU.add))
                    root(RSTD, SD)
                    for t in range(TT):
                        c(ts(HN[:, t, :], HN[:, t, :], MV[:, t, 0:1], RSTD[:, t:t + 1], ALU.subtract, ALU.mult))
                    mark().then_inc(S("hn"), 1)
                    dve.wait_ge(S("hn_ps"), h + 1)
                    dve.wait_ge(S("zm"), 1)
                    for j in range(4):
                        k = 4 * h + j
                        c(ts(XC[:, k, :], XC[:, k, :], col("mlstm_skip_2", k)))
                        c(stt(XC[:, k, :], PS[:, 2 + j // 2, (j % 2) * T:(j % 2 + 1) * T], col("mlstm_norm_g_2", k),
                              XC[:, k, :], ALU.mult, ALU.add))
                        c(tt(ZM[:, k, :], ZM[:, k, :], XC[:, k, :]))
                    mark().then_inc(S("ym"), 1)
                residual_gate(r)

            def final():
                rms()
                dve.wait_ge(S("fin_load"), 16)
                for t in range(TT):
                    c(tt(XN[:, t, :], XN[:, t, :], ROWB[:, 1, :]))
                mark().then_inc(S("final"), 1)

            c(V.memset(ONES[:, :], 1.0))
            dve.wait_ge(S("x_load"), 16)
            dve.wait_ge(S("con_load"), 16)
            for t in range(ROW_TILES):
                m = min(P, NROWS - t * P)
                dve.wait_ge(S("cols_ps"), t + 1)
                V.tensor_copy(COL[:, t * P:t * P + m], PS[:, t, 0:m]).then_inc(S("cols"), 1)
            dve.wait_ge(S("cols"), ROW_TILES)
            mark().then_inc(S("cols_done"), 1)
            for r in plan:
                {"even": even, "odd": odd, "moe": moe, "ada": ada, "ffn": ffn, "hyb": hyb, "mlstm": mlstm}[r.kind](r)
            if FINAL:
                final()
            else:
                for t in range(TT):
                    c(V.tensor_copy(XN[:, t, :], X[:, t, :]))
                mark().then_inc(S("final"), 1)


def kernel(**inputs):
    import concourse.bacc as bacc
    from concourse.bass_utils import run_bass_kernel_spmd

    nc = bacc.Bacc("TRN2", target_bir_lowering=False, num_devices=1)
    arrays = {name: np.ascontiguousarray(x) for name, x in inputs.items()}
    arrays["const"] = constants()
    aps = {name: nc.dram_tensor(f"in_{name}", x.shape, mybir.dt.from_np(x.dtype), kind="ExternalInput").ap()
           for name, x in arrays.items()}
    out = nc.dram_tensor("out", (1, T, D), F32, kind="ExternalOutput").ap()
    program(nc, aps, out)
    r = run_bass_kernel_spmd(nc, [{f"in_{name}": x for name, x in arrays.items()}], core_ids=[0])
    return r.results[0]["out"]
```

```python
from contextlib import ExitStack

import numpy as np

import concourse.bass as bass
from concourse import mybir

ALU = mybir.AluOpType
ACT = mybir.ActivationFunctionType
F32 = mybir.dt.float32
F32R = mybir.dt.float32r
AX = mybir.AxisListType

P = 128
T = 256
TT = T // P
D = 1024
KD = D // P
HD = 64
MW = P + T
NEG = -1.0e30
SLOTS = 2
SLOT = 6 * D
FG = 256
CH = FG // P
NE, DFE = 16, 512
DFF = 2816
MOE_G = NE * DFE // FG
TURN = 8
AW = 9 * D // (MOE_G // TURN)
FFN_G = DFF // FG
ALPHA = 4.0 ** 0.25
LN_EPS, EPS = 1e-5, 1e-6
STAGES = ("even", "moe0", "odd", "moe1", "mod", "ffn00", "hyb", "ffn01", "ffn10", "mlstm", "ffn11")
FINAL = True

EVEN_IN, ODD_IN, HYB_IN = 2312, 1380, 4624
PW = 768
PC = 256
EVEN_SPANS = [(0, 256), (256, 1024), (1024, 1792), (1792, 2304)]
HYB_SPANS = [(1024, 1792), (1792, 2560), (4096, 4624), (2560, 3328), (3328, 4096), (0, 768), (768, 1024)]

C_ID, C_NEGW, C_NEGC, C_CAUS, C_TRIT, C_BD, C_COS, C_SIN, C_TIE, NCONST = np.cumsum(
    [0, 128, MW, MW, MW, MW, 128, 32, 32, 16]).tolist()


class Stage:

    def __init__(self, name, kind, n, u, cb, ub, v2, me):
        self.name, self.kind, self.n, self.u, self.cb, self.ub, self.v2, self.me = name, kind, n, u, cb, ub, v2, me
        self.layer = self.i = self.sub = self.items = self.per = self.hs = self.sb = 0
        self.end, self.ln, self.scaled_by_pool = n, 0, False
        self.wb = self.we = self.pb = self.forget_used = 0
        self.pieces, self.used, self.n_proj, self.before = [], [], 0, None


class Head:

    def __init__(self, kind, h, dk, scale, at, q, k, v):
        self.kind, self.h, self.dk, self.scale, self.at, self.q, self.k, self.v = kind, h, dk, scale, at, q, k, v


def constants():
    c = np.zeros((P, NCONST), np.float32)
    p = np.arange(P)
    c[:, C_ID:C_ID + 128] = np.eye(P)
    t = np.concatenate([np.repeat(p[:, None], P, 1), np.repeat(p[:, None] + P, T, 1)], 1)
    s = np.concatenate([np.arange(P), np.arange(T)])[None, :]
    dist = (t - s).astype(np.float32)
    c[:, C_NEGW:C_NEGW + MW] = np.where((dist >= 0) & (dist < 128), -dist, NEG)
    c[:, C_NEGC:C_NEGC + MW] = np.where(dist >= 0, -dist, NEG)
    c[:, C_CAUS:C_CAUS + MW] = np.where(dist >= 0, 0.0, NEG)
    tq = np.concatenate([np.arange(T), np.arange(P) + P])[None, :]
    sk = np.concatenate([np.repeat(p[:, None], T, 1), np.repeat(p[:, None] + P, P, 1)], 1)
    c[:, C_TRIT:C_TRIT + MW] = (sk <= tq)
    c[:, C_BD:C_BD + 128] = (p[:, None] // 4 == p[None, :] // 4)
    inv = np.float32(10000.0) ** (-np.arange(16, dtype=np.float32) / np.float32(16))
    ang = np.arange(T, dtype=np.float32)[:, None] * inv[None, :]
    c[:, C_COS:C_COS + 32] = np.cos(ang).reshape(TT, P, 16).transpose(1, 0, 2).reshape(P, 32)
    c[:, C_SIN:C_SIN + 32] = np.sin(ang).reshape(TT, P, 16).transpose(1, 0, 2).reshape(P, 32)
    c[:, C_TIE:C_TIE + 16] = 16 - np.arange(16)
    return c


def vector_rows():
    sizes = [("ada_b_2", 144), ("norm_g_2", 48), ("lru_conv_w_2", 32), ("lru_conv_b_2", 8), ("lru_ba_2", 8),
             ("lru_bx_2", 8), ("lru_lambda_2", 8), ("ssd_conv_w_2", 48), ("ssd_conv_b_2", 12),
             ("ssd_norm_g_2", 8), ("mlstm_conv_w_2", 64), ("mlstm_conv_b_2", 16), ("mlstm_norm_g_2", 16),
             ("mlstm_skip_2", 16), ("odd_q_norm", 2), ("odd_kv_norm", 1), ("c_2", 8),
             ("ln_g", 32), ("ln_b", 32)]
    at, out = 0, {}
    for name, n in sizes:
        out[name] = (at, n)
        at += n
    return out, at


ROWS, NROWS = vector_rows()
ROW_TILES = -(-NROWS // P)


def flat(ap):
    names = "abcdefg"[:len(ap.shape)]
    return ap.rearrange(f"{' '.join(names)} -> ({' '.join(names)})") if len(names) > 1 else ap


def make_plan(a):
    items, plan = [], []

    def project(r, w, spans=None):
        src = w.rearrange("(k p) n -> p k n", p=P)
        for lo, hi in spans or [(lo, min(lo + PW, w.shape[1])) for lo in range(0, w.shape[1], PW)]:
            n = hi - lo
            r.pieces += [(len(items), n, c, min(PC, n - c), KD) for c in range(0, n, PC)]
            items.append([(k0 * n, (k1 - k0, n), src[:, k0:k1, lo:hi]) for k0, k1 in ((0, 3), (3, 6), (6, 8))])
        r.n_proj = len(r.pieces)

    def output(r, w):
        src = w.rearrange("(k p) n -> p k n", p=P)
        for k in range(0, w.shape[0] // P, 4):
            r.pieces += [(len(items), D, k2, D, 2) for k2 in (0, 2)]
            items.append([(a0 * D, (a1 - a0, D), src[:, k + a0:k + a1, :]) for a0, a1 in ((0, 2), (2, 3), (3, 4))])

    u = chunks = units = v2 = moes = steps = splits = norms = used = pieces = 0
    for name in STAGES:
        r = Stage(name=name, kind=name.rstrip("01"), n=len(items), u=u, cb=chunks, ub=units, v2=v2, me=moes)
        r.wb, r.pb, r.sb = used, pieces, splits
        if name == "even":
            project(r, a["even_w_in"][0], EVEN_SPANS)
            output(r, a["w_o"][0])
            u, units, splits = u + 2, units + 16, splits + KD
        elif name == "odd":
            project(r, a["odd_w_in"][0])
            output(r, a["w_o"][1])
            u, units, splits = u + 2, units + 16, splits + KD
        elif r.kind == "moe":
            r.layer = int(name[-1])
            r.items, r.per, r.hs = MOE_G, CH * TURN, steps
            items.extend([None] * MOE_G)
            splits += KD // 2
            u, chunks, moes, steps = u + 1, chunks + CH * MOE_G, moes + 1, steps + 3 * CH * MOE_G
        elif r.kind == "ffn":
            r.layer, r.i, r.sub = int(name[3]), int(name[4]), 2 * int(name[4])
            r.items, r.per, r.hs = FFN_G, CH * 2, steps
            items.extend([None] * FFN_G)
            splits += KD // 2
            u, chunks, v2, steps = u + 1, chunks + CH * FFN_G, v2 + 1, steps + 2 * CH * FFN_G
        elif name == "hyb":
            r.layer, r.sub = 0, 1
            project(r, a["hyb_w_in_2"][0], HYB_SPANS)
            output(r, a["hyb_w_out_2"][0])
            u, v2, splits = u + 1, v2 + 1, splits + 3 * KD // 2
        elif name == "mlstm":
            r.layer, r.sub = 1, 1
            project(r, a["mlstm_w_up_2"][0])
            output(r, a["mlstm_w_down_2"][0])
            u, v2, splits = u + 1, v2 + 1, splits + 3 * KD // 2
        r.end = len(items)
        for p in range(len(r.pieces)):
            if name == "even" and p == 6:
                used += 1
                r.forget_used = used
            used += -(-r.pieces[p][3] // P) if name in ("hyb", "mlstm") and p < r.n_proj else 1
            r.used.append(used)
        used += CH * r.items
        r.we = used
        pieces += len(r.pieces)
        r.ln = norms
        if r.kind in ("even", "moe", "odd"):
            norms += 1
        plan.append(r)
    work = [r for r in plan if r.kind != "mod"]
    for r, after in zip(work, work[1:]):
        after.before = r
    for r, after in zip(plan, plan[1:]):
        r.scaled_by_pool = r.kind in ("even", "moe", "odd") and after.kind in ("even", "moe", "odd")
    return items, plan, v2


def program(nc, a, out):
    items, plan, v2_end = make_plan(a)
    with ExitStack() as ctx:
        sems = {}

        def S(name):
            if name not in sems:
                sems[name] = ctx.enter_context(nc.semaphore(name))
            return sems[name]

        def sb(name, shape, dt=F32):
            return ctx.enter_context(nc.sbuf_tensor(name, shape, dt))

        ring = sb("ring", [P, SLOTS, SLOT])
        X = sb("X", [P, TT, D])
        XN = sb("XN", [P, TT, D])
        XT = sb("XT", [P, KD, T])
        ROWB = sb("ROWB", [P, 2, D])
        CON = sb("CON", [P, NCONST])
        COL = sb("COL", [P, ROW_TILES * P])
        MOD = sb("MOD", [P, 2, 72])
        MODA = sb("MODA", [P, 6, KD])
        MODG = sb("MODG", [P, 6, KD])
        ONES = sb("ONES", [P, T])
        RW = sb("RW", [P, KD, NE])
        WF = sb("WF", [P, KD, 8])
        RB = sb("RB", [P, NE])
        SINK = sb("SINK", [P, 8])
        SSDD = sb("SSDD", [P, 8])
        MARKS = sb("MARKS", [1, 128])
        BF = sb("BF", [16, 8])
        WQKV = sb("WQKV", [P, 3, 16, 4])
        WGT = sb("WGT", [P, 6, 2, 8, 4])
        ST = sb("ST", [P, 192])
        NAR = 16192
        WGH, WGL = (sb(n, [P, 2, 2 * KD * P], F32R) for n in ("WGH", "WGL"))
        XTH, XTL = (sb(n, [P, KD, T], F32R) for n in ("XTH", "XTL"))
        with nc.sbuf_tensor("AR", [P, NAR], F32) as AR:
            pass
        WDH, WDL = (sb(n, [P, 2, D], F32R) for n in ("WDH", "WDL"))
        HTH, HTL = (sb(n, [P, 2, T], F32R) for n in ("HTH", "HTL"))
        FA = sb("FA", [P, 4096 + 3 * AW])
        PS = ctx.enter_context(nc.psum_tensor("PS", [P, 8, 512], F32))
        PSY = PS[:, 0:4, :].rearrange("p (t h) n -> p t (h n)", t=TT)

        ID = CON[:, C_ID:C_ID + P]

        def carve(at, *shape):
            n = int(np.prod(shape))
            assert at + n <= NAR, (at, n)
            v = AR[:, at:at + n]
            if len(shape) > 1:
                names = "abcd"[:len(shape)]
                v = v.rearrange(f"p ({' '.join(names)}) -> p {' '.join(names)}",
                                **{k: s for k, s in zip(names, shape)})
            return v

        def col(name, i=0, n=1):
            c = ROWS[name][0] + i
            return COL[:, c:c + n]

        class Lane:

            def __init__(self, eng, name):
                self.e, self.name, self.n = eng, name + "_step", 0

            def c(self, ins):
                self.n += 1
                ins.then_inc(S(self.name), 1)
                self.e.wait_ge(S(self.name), self.n)

        def bc(ap, shape):
            return ap.to_broadcast(shape)

        TM = carve(0, TT, PW * 3)
        A0 = TT * PW * 3
        QK = carve(A0, 2, 512)
        LG = carve(A0 + 1024, 2, MW)
        PB = carve(A0 + 1024 + 2 * MW, 2, MW)
        PT = carve(A0 + 1024 + 4 * MW, 2, MW)
        A1 = A0 + 1024 + 6 * MW
        CT = carve(A1, T)
        NCT = carve(A1 + T, T)
        SPW = carve(A1 + 2 * T, 6, T)
        CTOK = carve(A1 + 8 * T, TT, 8)
        TMO = carve(0, TT, ODD_IN)
        WUQ = carve(TT * ODD_IN, 2, 768)
        DQ = carve(A1, TT, 8, 96)
        DKV = carve(A1 + 1536, TT, 8, 128)
        DK = carve(A1 + 3584, TT, 8, 96)
        SELM = carve(A1 + 5120, MW)
        SCR = carve(A1 + 5120 + MW, MW)
        TMPS = carve(A1 + 5120 + 2 * MW, MW)
        CQT = carve(A1 + 6272, 3, T)
        WUKV = carve(A1 + 6272 + 768, 1024)
        CQN = DKV[:, :, 0:3, :]
        QIT = DQ.rearrange("p t h d -> p (t h d)")[:, 0:5 * T].rearrange("p (h t) -> p h t", t=T)
        ROWS_IN = ROWB[:, 0, 0:ROW_TILES * P]
        XNF = XN[:, :, :].rearrange("p t d -> p (t d)")
        GB = FA[:, 0:4096].rearrange("p (e t) -> p e t", e=NE)
        ADW = FA[:, 4096:4096 + 2 * AW].rearrange("p (b n) -> p b n", b=2)
        ADC = FA[:, 4096 + 2 * AW:4096 + 3 * AW]
        SG = XNF[:, 0:512].rearrange("p (b t) -> p b t", b=2)
        HR = XNF[:, 512:1024].rearrange("p (b t) -> p b t", b=2)
        RT = XNF[:, 1024:1408].rearrange("p (k e) -> p k e", k=12)
        RP = XNF[:, 1408:1456].rearrange("p (t g k) -> p t g k", t=TT, g=4)
        GT = XNF[:, 1536:1792]
        DG = ROWB[:, 1, :].rearrange("p (k d) -> p k d", k=KD)
        GA = carve(0, 8, T)
        XL = carve(2048, 8, T)
        ZH = carve(4096, 8, T)
        XBC = carve(6144, 12, T)
        RAW = carve(9216, 2, T + 3)
        HWA = carve(9216 + 520, 8, P)
        HWX = carve(9216 + 520 + 1024, 8, P)
        H1 = carve(11784, 8, T)
        H2 = carve(11784 + 2048, 8, T)
        RG = XN[:, :, :].rearrange("p t (k d) -> p (t k) d", d=T)
        IG = XT
        AC = ROWB[:, 1, 0:T]
        DTR = ROWB[:, 1, T:2 * T]
        SPH = [XT[0:16, k, :] for k in range(4)] + [ROWB[0:16, 1, 2 * T:3 * T]]
        EH = carve(11784, 2, MW)
        CBM = carve(11784 + 2 * MW, 2, MW)
        ACD = carve(11784 + 4096, 64)
        H2_RS = carve(11784 + 2048, 2, T)
        XM = carve(0, 16, T + 3)
        ZM = carve(4144, 16, T)
        XC = carve(8240, 16, T)
        BD = carve(12336, 3, 4, P)
        BDX = XN[:, :, :].rearrange("p t d -> p (t d)")[:, 0:12 * P].rearrange("p (w j n) -> p w j n", w=3, j=4)
        BDR = ROWB[:, 1, :].rearrange("p (w j n) -> p w j n", w=2, j=4)
        BDV = carve(13872 + 2 * MW + 4 * T, 4, P)
        BD_A, BD_B = [BD[:, w, :, :] for w in range(3)], [BDX[:, w, :, :] for w in range(3)]
        BD_C = [BDR[:, 0, :, :], BDR[:, 1, :, :], BDV]
        BDS = [BD_A, BD_B, BD_A, BD_B, BD_A, BD_C, BD_A, BD_C]
        EM = carve(13872, MW)
        PM = carve(13872 + MW, MW)
        MR = carve(13872 + 2 * MW, 4, T)
        SPX = [XN[0:4, 1, i * T:(i + 1) * T] for i in range(4)] + [EM[0:4, 0:T], PM[0:4, 0:T]]
        NQ = XT
        VM = XN[:, 0, :].rearrange("p (t d) -> p t d", t=TT)
        HN = XN[:, 1, :].rearrange("p (t d) -> p t d", t=TT)
        block = ctx.enter_context(nc.Block())

        def units_of(name):
            out_ = []
            if name == "even":
                for h in range(8):
                    out_.append(Head(kind="window", h=h, dk=HD, scale=HD ** -0.5, at=HD * h,
                                                q=TM[:, :, HD * h:HD * h + HD],
                                                k=TM[:, :, 512 + HD * (h // 4):512 + HD * (h // 4) + HD],
                                                v=TM[:, :, 640 + HD * (h // 4):640 + HD * (h // 4) + HD]))
                for h in range(8):
                    out_.append(Head(kind="fox", h=h, dk=HD, scale=HD ** -0.5, at=512 + HD * h,
                                                q=TM[:, :, 768 + HD * h:768 + HD * h + HD],
                                                k=TM[:, :, 1280 + HD * h:1280 + HD * h + HD],
                                                v=TM[:, :, 1792 + HD * h:1792 + HD * h + HD]))
            else:
                for h in range(8):
                    out_.append(Head(kind="mla", h=h, dk=96, scale=96 ** -0.5, at=512 + HD * h,
                                                q=DQ[:, :, h, :], k=DK[:, :, h, :], v=DKV[:, :, h, HD:2 * HD]))
                for h in range(8):
                    out_.append(Head(kind="dsa", h=h, dk=HD, scale=HD ** -0.5, at=HD * h,
                                                q=TMO[:, :, HD * h:HD * h + HD], k=TMO[:, :, 512:576],
                                                v=TMO[:, :, 576:640]))
            return out_

        BLK = [(0, P), (P, MW)]

        work = [r for r in plan if r.kind != "mod"]
        AFTER = {r.name: after for r, after in zip(work, work[1:])}
        HYB_TILES = [k for lo, hi in HYB_SPANS for k in range(lo // P, -(-hi // P))]
        TILE_OF = {r.name: [(p, j) for p in range(r.n_proj) for j in range(-(-r.pieces[p][3] // P))]
                   for r in plan if r.name in ("hyb", "mlstm")}
        DT_AT = HYB_TILES.index(36)
        STEP_AT = HYB_TILES.index(1)
        EV_BASE = {"hyb": 0, "mlstm": 37 if any(r.name == "hyb" for r in plan) else 0}
        LRU_AT = 12
        NORMED_BANK = (2, 2, 2, 4)
        RG_XD = XN

        def run_turns(eng, total, per, body):
            n = (total - 2) // per
            for j in range(per):
                body(0, j)
            with eng.Fori(1, n, 1) as i:
                for j in range(per):
                    body(i, j)
            for c in range(n * per, total):
                body(c // per, c % per)

        def exists(r, i, j, ahead):
            return not isinstance(i, int) or 0 <= i * r.per + j + ahead < CH * r.items

        def past(i, j, back):
            return not isinstance(i, int) or i > 0 or j >= back

        def piece(r, p):
            n, width, c, w, k = r.pieces[p]
            b = (p + len(r.pieces)) % 2
            if k == KD:
                raw = ring[:, n % SLOTS, 0:KD * width].rearrange("p (k w) -> p k w", k=KD)[:, :, c:c + w]
            else:
                raw = ring[:, n % SLOTS, 0:4 * D].rearrange("p (k w) -> p k w", k=4)[:, c:c + k, :]
            hi, lo = (W[:, b, 0:k * w].rearrange("p (k w) -> p k w", k=k) for W in (WGH, WGL))
            return raw, hi, lo

        def raw_slot(r, j):
            s = (r.n + j // CH) % SLOTS
            gu = ring[:, s, 0:2 * KD * FG].rearrange("p (k f) -> p k f", f=FG)
            dn = ring[:, s, 2 * KD * FG + (j % CH) * D:2 * KD * FG + (j % CH + 1) * D]
            return gu[:, :, (j % CH) * P:(j % CH + 1) * P], dn

        def land_count(r, i, j):
            return i * (48 * r.per // CH // SLOTS) + 48 * ((r.n + j // CH) // SLOTS + 1)

        @block.sync
        def _(sp):
            def load(slot, parts):
                for o, (k, w), src in parts:
                    sp.dma_start(ring[:, slot, o:o + k * w].rearrange("p (k w) -> p k w", k=k), src)\
                      .then_inc(S(f"w_land{slot}"), 16)

            def freed(n):
                if n < 0:
                    return
                q = [r for r in plan if r.n <= n < r.end][0]
                if q.items:
                    sp.wait_ge(S("lo_dn"), q.cb + CH * (n - q.n + 1))
                else:
                    sp.wait_ge(S("piece_lo"), q.pb + sum(1 for x in q.pieces if x[0] <= n))

            for t in range(TT):
                sp.dma_start(X[:, t, :], a["x"][0][t * P:(t + 1) * P, :]).then_inc(S("x_load"), 16)
            for r in plan:
                if not r.items:
                    for n in range(r.n, r.end):
                        freed(n - SLOTS)
                        load(n % SLOTS, items[n])
                    continue

                def hidden_item(i, m):
                    if r.kind == "moe":
                        e, f0 = bass.ds(i * (TURN // 2) + m // 2, 1), (m % 2) * FG
                        w_g = a["moe_w_gate"][r.layer, e].rearrange("a (k p) n -> p (a k) n", p=P)[:, :, f0:f0 + FG]
                        w_u = a["moe_w_up"][r.layer, e].rearrange("a (k p) n -> p (a k) n", p=P)[:, :, f0:f0 + FG]
                        w_d = a["moe_w_down"][r.layer, e].rearrange("a (c p) n -> p (a c) n", p=P)
                        w_d = w_d[:, (m % 2) * CH:(m % 2 + 1) * CH, :]
                    else:
                        c0 = bass.ds(i * (2 * FG) + m * FG, FG)
                        w_g = a["ffn_w_gate_2"][r.layer, r.i].rearrange("(k p) n -> p k n", p=P)[:, :, c0]
                        w_u = a["ffn_w_up_2"][r.layer, r.i].rearrange("(k p) n -> p k n", p=P)[:, :, c0]
                        w_d = a["ffn_w_down_2"][r.layer, r.i][c0, :].rearrange("(c p) n -> p c n", p=P)
                    load((r.n + m) % SLOTS, [(0, (KD, FG), w_g), (KD * FG, (KD, FG), w_u), (2 * KD * FG, (CH, D), w_d)])

                def mod_item(i, m):
                    sp.dma_start(ADW[:, m % 2, :], a["ada_w_2"][r.layer, m * P:(m + 1) * P, bass.ds(i * AW, AW)])\
                      .then_inc(S(f"mod_land{m % 2}"), 16)

                per = r.per // CH
                for m in range(per):
                    freed(r.n + m - SLOTS)
                    hidden_item(0, m)
                    if r.kind == "moe" and m == 1:
                        if r.n:
                            sp.wait_ge(S("w_used"), r.wb)
                        mod_item(0, 0)
                        mod_item(0, 1)
                    if r.kind == "moe" and m >= 2:
                        sp.wait_ge(S("mod_acc"), r.me * MOE_G + m - 1)
                        mod_item(0, m)
                with sp.Fori(1, r.items // per, 1) as i:
                    for m in range(per):
                        sp.wait_ge(S("lo_dn"), i * r.per + (r.cb + CH * (m - SLOTS + 1)))
                        hidden_item(i, m)
                        if r.kind == "moe":
                            sp.wait_ge(S("mod_acc"), i * TURN + (r.me * MOE_G + m - 1))
                            mod_item(i, m)
                for n in range(r.items - r.items % per, r.items):
                    freed(r.n + n - SLOTS)
                    hidden_item(n // per, n % per)
            sp.wait_ge(S("final"), 1)
            sp.dma_start(out[0].rearrange("(t p) d -> p t d", p=P), XN[:, :, :]).then_inc(S("stored"), 16)
            sp.wait_ge(S("stored"), 16)

        N_SMALL, N_ROWS = 26, [0]

        @block.gpsimd
        def _(pool):
            def ld(dst, src, name):
                pool.dma_start(dst, src, allow_slow_non_contiguous=True).then_inc(S(name), 16)

            ld(WF[:, :, :], a["even_w_in"][0].rearrange("(k p) n -> p k n", p=P)[:, :, EVEN_IN - 8:EVEN_IN], "small_load")
            ld(BF[0:8, 0:1], a["even_b_f"].rearrange("a h -> h a"), "small_load")
            ld(BF[0:16, 1:2], a["ssd_dt_bias_2"].rearrange("a h -> h a"), "small_load")
            ld(BF[0:16, 2:3], a["ssd_a_log_2"].rearrange("a h -> h a"), "small_load")
            ld(BF[0:4, 3:4], a["mlstm_b_gates_2"][:, 0:4].rearrange("a h -> h a"), "small_load")
            ld(BF[0:4, 4:5], a["mlstm_b_gates_2"][:, 4:8].rearrange("a h -> h a"), "small_load")
            ld(SINK[:, :], a["even_sinks"][0].partition_broadcast(P), "small_load")
            ld(RB[:, :], a["router_b"].partition_broadcast(P), "small_load")
            ld(RW[:, :, :], a["router_w"].rearrange("(k p) e -> p k e", p=P), "small_load")
            for half in range(2):
                ld(SSDD[64 * half:64 * half + 64, :],
                   a["ssd_d_2"][0].rearrange("(t h) -> h t", h=2)[half].partition_broadcast(64), "small_load")
            for i, w in enumerate(("mlstm_wq_2", "mlstm_wk_2", "mlstm_wv_2")):
                ld(WQKV[:, i, :, :], a[w][0].rearrange("(t n) i o -> (n i) t o", t=16), "small_load")
            for g in range(6):
                for m in range(2):
                    ld(WGT[:, g, m, :, :], a["mlstm_w_gates_2"][0][8 * g * P:8 * (g + 1) * P, 4 * m:4 * m + 4]
                       .rearrange("(k p) e -> p k e", p=P), "small_load")
            for name, (at, n) in ROWS.items():
                shape = a[name].shape
                names = "abcde"[:len(shape)]
                src = a[name].rearrange(f"{' '.join(names)} -> ({' '.join(names)})").rearrange("(r c) -> r c", c=P)
                done = 0
                while done < n:
                    t, q = divmod(at + done, P)
                    m = min(n - done, P - q)
                    ld(ROWS_IN[q:q + m, t * P:(t + 1) * P], src[done:done + m, :], "rows_load")
                    N_ROWS[0] += 1
                    done += m
            pool.wait_ge(S("cols_done"), 1)
            for n, r in enumerate(plan):
                if r.kind in ("even", "moe", "odd"):
                    w = {"even": (0, 0), "moe0": (0, 1), "odd": (1, 0), "moe1": (1, 1)}[r.name]
                    if r.ln:
                        pool.wait_ge(S("x_ready"), r.ln)
                    ld(ROWB[:, 0, :], a["ln_g"][w[0], w[1]].partition_broadcast(P), "ln_load")
                    ld(ROWB[:, 1, :], a["ln_b"][w[0], w[1]].partition_broadcast(P), "ln_load")
                if r.name == "odd":
                    if r.n:
                        pool.wait_ge(S("w_used"), r.wb)
                    ld(WUQ, a["odd_w_uq"][0].rearrange("(k p) n -> p k n", p=P), "rank_load")
                    ld(WUKV, a["odd_w_ukv"][0], "rank_load")
                if r.name == "hyb":
                    if r.n:
                        pool.wait_ge(S("w_used"), r.wb)
                    ld(HWA, a["lru_wa_2"][0].rearrange("h i o -> i h o"), "lru_load")
                    ld(HWX, a["lru_wx_2"][0].rearrange("h i o -> i h o"), "lru_load")
                if r.scaled_by_pool:
                    pool.wait_ge(S("ln_load"), 32 * (r.ln + 1))
                    pool.wait_ge(S("xt_ps"), 4 * (plan[n + 1].u + 1))
                    for t in range(TT):
                        nc.gpsimd.tensor_tensor(X[:, t, :], X[:, t, :], ROWB[:, 0, :], ALU.mult)\
                            .then_inc(S("scaled"), 1)
                    pool.wait_ge(S("scaled"), TT * (r.ln + 1))
                    for t in range(TT):
                        ins = nc.gpsimd.tensor_tensor(X[:, t, :], X[:, t, :], ROWB[:, 1, :], ALU.add)
                    ins.then_inc(S("x_ready"), 1)
                if r.name == "hyb":
                    pool.wait_ge(S("lru_at"), 8)
                    nc.gpsimd.tensor_tensor(H2, H1, H1, ALU.mult).then_inc(S("a_squared"), 1)
                    nc.gpsimd.tensor_tensor(IG[:, :, :], IG[:, :, :], XL, ALU.mult).then_inc(S("gated_in"), 1)
                    pool.wait_ge(S("h2_free"), 1)
                    for q in range(4):
                        pool.wait_ge(S("tile_out"), EV_BASE["hyb"] + HYB_TILES.index(2 * q + 1) + 1)
                        g, h = GA[:, 2 * q:2 * q + 2, :], H2[:, 2 * q:2 * q + 2, :]
                        nc.gpsimd.tensor_tensor(h, g, g, ALU.mult).then_inc(S("gelu_step"), 1)
                        pool.wait_ge(S("gelu_step"), 3 * q + 1)
                        nc.gpsimd.tensor_scalar(h, h, 0.044715, 1.0, ALU.mult, ALU.add).then_inc(S("gelu_step"), 1)
                        pool.wait_ge(S("gelu_step"), 3 * q + 2)
                        nc.gpsimd.tensor_tensor(h, h, g, ALU.mult).then_inc(S("gelu_step"), 1)
                if r.name == "mlstm":
                    pool.wait_ge(S("w_used"), r.wb)
                    pool.wait_ge(S("xt_ps"), 4 * (r.u + 1))
                    pool.wait_ge(S("small_load"), 16 * N_SMALL)
                    for i in range(8):
                        if i in (2, 3):
                            pool.wait_ge(S("qkv1_ps"), 12 * (i - 1))
                        if i == 4:
                            pool.wait_ge(S("qkv1_ps"), 36)
                        if i == 5:
                            pool.wait_ge(S("row_ps"), r.v2 + 1)
                        if i >= 6:
                            pool.wait_ge(S("v2_ps"), 2 * (i - 5))
                        for w in range(3):
                            for j in range(4):
                                ins = nc.gpsimd.tensor_tensor(
                                    BDS[i][w][:, j, :].rearrange("p (n o) -> p n o", o=4),
                                    bc(WQKV[:, w, 4 * (i % 4) + j, :].unsqueeze(1), (P, 32, 4)),
                                    CON[:, C_BD:C_BD + 128].rearrange("p (n o) -> p n o", o=4), ALU.mult)
                        ins.then_inc(S("bd"), 1)
            if FINAL:
                if plan[-1].ln:
                    pool.wait_ge(S("x_ready"), plan[-1].ln)
                if v2_end:
                    pool.wait_ge(S("row_ps"), v2_end)
                ld(ROWB[:, 1, :], a["final_norm_g_2"].partition_broadcast(P), "fin_load")

        @block.tensor
        def _(pe):
            mm = nc.tensor.matmul

            def columns():
                pe.wait_ge(S("con_load"), 16)
                pe.wait_ge(S("rows_load"), 16 * N_ROWS[0])
                for t in range(ROW_TILES):
                    m = min(P, NROWS - t * P)
                    nc.tensor.transpose(PS[:, 4 + t, 0:m], ROWS_IN[0:m, t * P:(t + 1) * P], ID[0:m, 0:m])\
                      .then_inc(S("cols_ps"), 1)

            def trn(u, src):
                if u == 0:
                    pe.wait_ge(S("con_load"), 16)
                for t in range(TT):
                    pe.wait_ge(S(f"xn{t}"), u + 1)
                    for j in range(4):
                        for i in range(2):
                            ins = nc.tensor.transpose(PS[:, 4 + j, i * T + t * P:i * T + (t + 1) * P],
                                                      src[:, t, (2 * j + i) * P:(2 * j + i + 1) * P], ID)
                        if t == TT - 1:
                            ins.then_inc(S("xt_ps"), 1)

            def out_rows(r, half=0):
                for q in range(4):
                    out_piece(r, r.n_proj + 4 * half + q, 2 * q, r.sb + KD // 2 * (1 + half))

            def out_piece(r, p, k0, split):
                pe.wait_ge(S("piece_lo"), r.pb + p + 1)
                pe.wait_ge(S("x_low"), split + k0 // 2 + 1)
                _, hi, lo = piece(r, p)
                for k in range(2):
                    for t in range(TT):
                        for q, (x_, w_) in enumerate(((XTH, hi), (XTH, lo), (XTL, hi))):
                            for h in range(2):
                                if p == len(r.pieces) - 1 and k == 1 and t == 1 and q == 0 and h == 0:
                                    ins.then_inc(S("y0"), 1)
                                ins = mm(PSY[:, t, 512 * h:512 * h + 512], x_[:, k0 + k, t * P:(t + 1) * P],
                                         w_[:, k, 512 * h:512 * h + 512], start=p == r.n_proj and k == 0 and q == 0,
                                         stop=p == len(r.pieces) - 1 and k == 1 and q == 2, skip_group_check=True)
                ins.then_inc(S("w_used"), 1)

            def project(r, evac):
                for p in range(r.n_proj):
                    w, i, c0 = r.pieces[p][3], p // 3, PC * (p % 3)
                    if p == 6:
                        forget_gates(r)
                    if p == 8:
                        pe.wait_ge(S("forget"), 1)
                    if c0 == 0 and i >= 2:
                        pe.wait_ge(S(evac), i - 1)
                    pe.wait_ge(S("piece_lo"), r.pb + p + 1)
                    _, hi, lo = piece(r, p)
                    for t in range(TT):
                        for k in range(KD):
                            if p == 0 and t == 0 and k % 2 == 0:
                                pe.wait_ge(S("x_low"), r.sb + k // 2 + 1)
                            for q, (x_, w_) in enumerate(((XTH, hi), (XTH, lo), (XTL, hi))):
                                ins = mm(PS[:, 4 * (i % 2) + 2 * t + c0 // 512, c0 % 512:c0 % 512 + w],
                                         x_[:, k, t * P:(t + 1) * P], w_[:, k, :],
                                         start=k == 0 and q == 0, stop=k == KD - 1 and q == 2)
                    ins.then_inc(S("w_used"), 1)

            def project_tile(r, f, banks):
                p, j = TILE_OF[r.name][f]
                w = min(P, r.pieces[p][3] - j * P)
                if j == 0:
                    pe.wait_ge(S("piece_lo"), r.pb + p + 1)
                if f >= banks:
                    pe.wait_ge(S("tile_out"), EV_BASE[r.name] + f - banks + 1)
                _, hi, lo = piece(r, p)
                for k in range(KD):
                    if f == 0 and k % 2 == 0:
                        pe.wait_ge(S("x_low"), r.sb + k // 2 + 1)
                    for q, (w_, x_) in enumerate(((hi, XTH), (hi, XTL), (lo, XTH))):
                        ins = mm(PS[0:w, f % banks, 0:T], w_[:, k, j * P:j * P + w], x_[:, k, :],
                                 start=k == 0 and q == 0, stop=k == KD - 1 and q == 2)
                ins.then_inc(S("w_used"), 1)

            def attention(r, units):
                def transposed(i):
                    u, w, b = r.ub + i, units[i], i % 2
                    if u >= 2:
                        pe.wait_ge(S("qk"), 2 * (u - 1))
                    for t in range(TT):
                        nc.tensor.transpose(PS[0:w.dk, b, t * P:(t + 1) * P], w.q[:, t, :], ID)
                        ins = nc.tensor.transpose(PS[0:w.dk, b, T + t * P:T + (t + 1) * P], w.k[:, t, :], ID)
                    ins.then_inc(S("qk_ps"), 1)

                def scores(i):
                    u, w, b = r.ub + i, units[i], i % 2
                    pe.wait_ge(S("qk"), 2 * (u + 1))
                    if u >= 2:
                        pe.wait_ge(S("logits"), u - 1)
                    fox = w.kind == "fox"
                    for t, (c0, c1) in enumerate(BLK):
                        ins = mm(PS[:, 2 + b, c0:c1], QK[0:w.dk, b, t * P:(t + 1) * P], QK[0:w.dk, b, T:T + c1 - c0],
                                 start=True, stop=not fox)
                        if fox:
                            ins = mm(PS[:, 2 + b, c0:c1], bc(ID[0:8, w.h:w.h + 1], (8, P)), NCT[0:8, 0:c1 - c0],
                                     start=False, stop=True)
                    ins.then_inc(S("scores"), 1)

                def probs(i):
                    u, b = r.ub + i, i % 2
                    pe.wait_ge(S("p"), 2 * (u + 1))
                    if u >= 2:
                        pe.wait_ge(S("pt"), u - 1)
                    for c in range(3):
                        ins = nc.tensor.transpose(PS[:, 4 + b, c * P:(c + 1) * P], PB[:, b, c * P:(c + 1) * P], ID)
                    ins.then_inc(S("pt_ps"), 1)

                def values(i):
                    u, w, b = r.ub + i, units[i], i % 2
                    pe.wait_ge(S("pt"), u + 1)
                    if u >= 2:
                        pe.wait_ge(S("o"), u - 1)
                    mm(PS[:, 6 + b, 0:HD], PT[:, b, 0:P], w.v[:, 0, :], start=True, stop=True)
                    mm(PS[:, 6 + b, HD:2 * HD], PT[:, b, P:2 * P], w.v[:, 0, :], start=True, stop=False)
                    mm(PS[:, 6 + b, HD:2 * HD], PT[:, b, 2 * P:3 * P], w.v[:, 1, :], start=False, stop=True)\
                        .then_inc(S("o_ps"), 1)

                n = len(units)
                for i in range(n + 3):
                    if i < n:
                        transposed(i)
                    if 0 <= i - 1 < n:
                        scores(i - 1)
                    if 0 <= i - 2 < n:
                        probs(i - 2)
                    if 0 <= i - 3 < n:
                        values(i - 3)

            def forget_gates(r):
                pe.wait_ge(S("small_load"), 16 * N_SMALL)
                pe.wait_ge(S("tm_even"), 1)
                for k in range(KD):
                    ins = mm(PS[0:8, 3, 0:T], WF[:, k, :], XT[:, k, :], start=k == 0, stop=k == KD - 1)
                ins.then_inc(S("w_used"), 1)

            def even(r):
                trn(r.u, X)
                pe.wait_ge(S("xt"), 8 * (r.u + 1))
                project(r, "tm_even")
                pe.wait_ge(S("tm_even"), 2)
                columns()
                pe.wait_ge(S("ct"), 1)
                pe.wait_ge(S("cols"), ROW_TILES)
                for t in range(TT):
                    ins = nc.tensor.transpose(PS[:, 4, 8 * t:8 * t + 8], CT[0:8, t * P:(t + 1) * P], ID[0:8, 0:8])
                ins.then_inc(S("ct_ps"), 1)
                pe.wait_ge(S("ctok"), 1)
                pe.wait_ge(S("tm_even"), 3)
                attention(r, units_of("even"))
                trn(r.u + 1, XN)
                pe.wait_ge(S("xt"), 8 * (r.u + 2))
                out_rows(r)

            def odd(r):
                trn(r.u, X)
                pe.wait_ge(S("xt"), 8 * (r.u + 1))
                project(r, "tm_odd")
                pe.wait_ge(S("tm_odd"), 2)
                for h in range(5):
                    for t in range(TT):
                        ins = nc.tensor.transpose(PS[0:HD, h // 2, (h % 2) * T + t * P:(h % 2) * T + (t + 1) * P],
                                                  TMO[:, t, 640 + HD * h:640 + HD * (h + 1)], ID)
                ins.then_inc(S("qi_ps"), 1)
                pe.wait_ge(S("qit"), 3)
                for h in range(4):
                    for t, (c0, c1) in enumerate(BLK):
                        ins = mm(PS[:, 4 + h, c0:c1], QIT[0:HD, h, t * P:(t + 1) * P], QIT[0:HD, 4, 0:c1 - c0],
                                 start=True, stop=True)
                    ins.then_inc(S("dots"), 1)
                pe.wait_ge(S("cqn"), 1)
                for c in range(3):
                    for t in range(TT):
                        ins = nc.tensor.transpose(PS[:, c, t * P:(t + 1) * P], CQN[:, t, c, :], ID)
                ins.then_inc(S("cqt_ps"), 1)
                pe.wait_ge(S("cqt"), 3)
                pe.wait_ge(S("rank_load"), 32)
                pe.wait_ge(S("dsa"), 1)
                for t in range(TT):
                    for c0, c1 in ((0, 512), (512, 768)):
                        for k in range(2):
                            ins = mm(PS[:, 4 + 2 * t + c0 // 512, 0:c1 - c0], CQT[:, k, t * P:(t + 1) * P],
                                     WUQ[:, k, c0:c1], start=k == 0, stop=k == 1)
                ins.then_inc(S("dq_ps"), 1)
                for t in range(TT):
                    for h in range(2):
                        ins = mm(PS[:, 2 * t + h, :], CQT[:, 2, t * P:(t + 1) * P], WUKV[:, 512 * h:512 * h + 512],
                                 start=True, stop=True)
                ins.then_inc(S("dkv_ps"), 1)
                pe.wait_ge(S("mla_ready"), 1)
                attention(r, units_of("odd"))
                trn(r.u + 1, XN)
                pe.wait_ge(S("xt"), 8 * (r.u + 2))
                out_rows(r)

            def hidden_layer(r, beside=None):
                def gate_up(i, j):
                    pe.wait_ge(S("lo_gu"), i * r.per + (r.cb + j + 1))
                    if past(i, j, 2):
                        pe.wait_ge(S("hidden"), i * r.per + (r.cb + j - 1))
                    b = j % 2
                    for m in range(2):
                        for k in range(KD):
                            if isinstance(i, int) and i == 0 and j == 0 and m == 0 and k % 2 == 0:
                                pe.wait_ge(S("x_low"), r.sb + k // 2 + 1)
                            w = slice((m * KD + k) * P, (m * KD + k + 1) * P)
                            for q, (w_, x_) in enumerate(((WGH, XTH), (WGH, XTL), (WGL, XTH))):
                                ins = mm(PS[:, 4 + b, m * T:(m + 1) * T], w_[:, b, w], x_[:, k, :],
                                         start=k == 0 and q == 0, stop=k == KD - 1 and q == 2)
                    ins.then_inc(S("gate_up"), 1)

                def down(i, j):
                    pe.wait_ge(S("lo_dn"), i * r.per + (r.cb + j + 1))
                    pe.wait_ge(S("hidden"), i * r.per + (r.cb + j + 1))
                    first = isinstance(i, int) and i == 0 and j == 0
                    last = not exists(r, i, j, 1)
                    b = j % 2
                    for t in range(TT):
                        for q, (h_, w_) in enumerate(((HTH, WDH), (HTH, WDL), (HTL, WDH))):
                            for h in range(2):
                                if last and t == 1 and q == 0 and h == 0:
                                    ins.then_inc(S("y0"), 1)
                                ins = mm(PSY[:, t, 512 * h:512 * h + 512], h_[:, b, t * P:(t + 1) * P],
                                         w_[:, b, 512 * h:512 * h + 512], start=first and q == 0,
                                         stop=last and q == 2, skip_group_check=True)
                    ins.then_inc(S("w_used"), 1)

                def mod_sums(i):
                    pe.wait_ge(S("mod_acc"), i * TURN + (r.me * MOE_G + TURN))
                    if not (isinstance(i, int) and i == 0 and r.me == 0):
                        pe.wait_ge(S("mod_out"), i + r.me * (MOE_G // TURN))
                    for m in range(AW // P):
                        ins = mm(PS[:, 6, m:m + 1], ADC[:, m * P:(m + 1) * P], ONES[:, 0:1], start=True, stop=True)
                    ins.then_inc(S("mod_ps"), 1)

                def step(i, j):
                    if exists(r, i, j, 1):
                        gate_up(i, j + 1)
                    if r.kind == "moe" and j == r.per - 1:
                        mod_sums(i)
                    down(i, j)

                gate_up(0, 0)
                if beside:
                    beside()
                run_turns(pe, CH * r.items, r.per, step)

            def gate_row(r):
                pe.wait_ge(S("diag"), r.v2 + 1)
                for j in range(2):
                    ins = mm(PS[:, 6 + j, :], ONES[:, 0:P],
                             DG[:, 4 * j:4 * j + 4, :].rearrange("p k d -> p (k d)"), start=True, stop=True)
                ins.then_inc(S("row_ps"), 1)

            def moe(r):
                trn(r.u, X)
                pe.wait_ge(S("xt"), 8 * (r.u + 1))
                pe.wait_ge(S("small_load"), 16 * N_SMALL)
                for t in range(TT):
                    for k in range(KD):
                        ins = mm(PS[:, 6, NE * t:NE * t + NE], XT[:, k, t * P:(t + 1) * P], RW[:, k, :],
                                 start=k == 0, stop=k == KD - 1)
                ins.then_inc(S("route_ps"), 1)

                def gates():
                    pe.wait_ge(S("gates"), r.me + 1)
                    for t in range(TT):
                        ins = nc.tensor.transpose(PS[0:NE, 7, t * P:(t + 1) * P], RT[:, 11, NE * t:NE * t + NE], ID)
                    ins.then_inc(S("gates_ps"), 1)
                    pe.wait_ge(S("gates_t"), r.me + 1)
                    for e in range(NE):
                        if e >= 4 and e % 2 == 0:
                            pe.wait_ge(S("gate_rows"), 8 * r.me + e // 2 - 1)
                        ins = mm(PS[:, 6 + (e // 2) % 2, (e % 2) * T:(e % 2 + 1) * T],
                                 bc(ID[0:NE, e:e + 1], (NE, P)), GT[0:NE, :], start=True, stop=True)
                        if e % 2 == 1:
                            ins.then_inc(S("rows_ps"), 1)
                    pe.wait_ge(S("gate_rows"), 8 * (r.me + 1))

                hidden_layer(r, gates)

            def ffn(r):
                trn(r.u, XN)
                hidden_layer(r, lambda: gate_row(r))

            def mod(r):
                pass

            def hyb(r):
                trn(r.u, XN)
                for f in range(37):
                    project_tile(r, f, 6)
                    if f == 1:
                        gate_row(r)
                    if f == LRU_AT:
                        pe.wait_ge(S("lru_load"), 32)
                        pe.wait_ge(S("conv"), 8)
                        pe.wait_ge(S("row"), r.v2 + 1)
                    if LRU_AT <= f < LRU_AT + 8:
                        i = f - LRU_AT
                        b = 6 + i % 2
                        if i >= 2:
                            pe.wait_ge(S("lru_gates"), 2 * (i - 1))
                        mm(PS[:, b, 0:T], HWA[:, i, :], XL[:, i, :], start=True, stop=True)
                        mm(PS[:, b, T:2 * T], HWX[:, i, :], XL[:, i, :], start=True, stop=True)\
                            .then_inc(S("lru_ps"), 1)
                pe.wait_ge(S("lru_gates"), 16)
                pe.wait_ge(S("tile_out"), EV_BASE["hyb"] + 37)
                pe.wait_ge(S("ssd_rows"), 1)
                for m, src in enumerate((AC, DTR)):
                    for t in range(TT):
                        ins = nc.tensor.transpose(PS[:, 1, 32 * m + 16 * t:32 * m + 16 * t + 16],
                                                  src[0:16, t * P:(t + 1) * P], ID[0:16, 0:16])
                ins.then_inc(S("acd_ps"), 1)
                pe.wait_ge(S("xbc"), 3)
                for t in range(TT):
                    for j in range(2):
                        for c in range(4):
                            ins = nc.tensor.transpose(PS[:, 4 + 2 * t + j, c * P:(c + 1) * P],
                                                      XBC[:, 4 * j + c, t * P:(t + 1) * P], ID)
                        ins.then_inc(S("xs_ps"), 1)
                for g in range(2):
                    mm(PS[:, 2 + g, 0:T], XBC[:, 8 + g, 0:P], XBC[:, 10 + g, :], start=True, stop=True)
                    mm(PS[:, 2 + g, T:MW], XBC[:, 8 + g, P:T], XBC[:, 10 + g, P:T], start=True, stop=True)\
                        .then_inc(S("cb_ps"), 1)
                pe.wait_ge(S("cbm"), 2)
                pe.wait_ge(S("xd"), 4)
                pe.wait_ge(S("acd"), 1)

                def spread(h):
                    if h >= 2:
                        pe.wait_ge(S("eh"), 2 * (h - 1))
                    b = 4 + h % 2
                    one = bc(ID[0:16, h:h + 1], (16, P))
                    tri = CON[:, C_CAUS:C_CAUS + P]
                    mm(PS[:, b, 0:P], tri, ID, start=True, stop=False)
                    mm(PS[:, b, 0:P], one, AC[0:16, 0:P], start=False, stop=True)
                    mm(PS[:, b, P:T], one, AC[0:16, P:T], start=True, stop=True)
                    mm(PS[:, b, T:MW], tri, ID, start=True, stop=False)
                    mm(PS[:, b, T:MW], one, AC[0:16, P:T], start=False, stop=True).then_inc(S("spread"), 1)

                def head(h):
                    pe.wait_ge(S("mt"), h + 1)
                    if h % 2 == 0 and h >= 4:
                        pe.wait_ge(S("ys"), h // 2 - 1)
                    o = 64 * (h % 2)
                    b = 6 + (h // 2) % 2
                    mm(PS[o:o + 64, b, 0:T], RG_XD[:, 0, 64 * h:64 * h + 64], EH[:, h % 2, 0:T],
                       start=True, stop=False)
                    mm(PS[o:o + 64, b, P:T], RG_XD[:, 1, 64 * h:64 * h + 64], EH[:, h % 2, T:MW],
                       start=False, stop=True).then_inc(S("head_ps"), 1)

                def squares(g):
                    pe.wait_ge(S("sq"), g + 1)
                    for j in range(4):
                        ins = mm(PS[:, 4, 0:T], ONES[:, 0:P], XBC[:, 4 * g + j, :], start=j == 0, stop=j == 3)
                    ins.then_inc(S("sq_ps"), 1)

                def lru_out(q):
                    out_piece(r, r.n_proj + q, 2 * q, r.sb + KD // 2)

                for h in range(18):
                    if h == 12:
                        pe.wait_ge(S("eh"), 2 * 11)
                        squares(0)
                        lru_out(2)
                        pe.wait_ge(S("sq_out"), 1)
                    if h < 16:
                        spread(h)
                    if h >= 2:
                        head(h - 2)
                    if h in (5, 8):
                        lru_out((h - 5) // 3)
                lru_out(3)
                squares(1)
                out_rows(r, 1)

            def mlstm(r):
                trn(r.u, XN)
                for f in range(32):
                    project_tile(r, f, 6)
                    if f == 1:
                        gate_row(r)
                pe.wait_ge(S("tile_out"), EV_BASE["mlstm"] + 32)
                pe.wait_ge(S("row"), r.v2 + 1)
                for h in range(4):
                    pe.wait_ge(S("bd"), h + 1)
                    pe.wait_ge(S("xc"), h + 1)
                    for w in range(3):
                        for j in range(4):
                            q = (h * 3 + w) * 4 + j
                            b = 2 + q % 4
                            if q >= 4:
                                pe.wait_ge(S("qkv1"), q - 3)
                            src = XM[:, 4 * h + j, 3:] if w == 2 else XC[:, 4 * h + j, :]
                            mm(PS[:, b, 0:T], BDS[h][w][:, j, :], src, start=True, stop=True).then_inc(S("qkv1_ps"), 1)
                            if q >= 2:
                                gates_add(q - 2)
                gates_add(46)
                gates_add(47)

                def gates_by_token():
                    pe.wait_ge(S("gtok_in"), 1)
                    for m in range(2):
                        for t in range(TT):
                            ins = nc.tensor.transpose(PS[:, 7, 8 * m + 4 * t:8 * m + 4 * t + 4],
                                                      MR[0:4, 2 + m, t * P:(t + 1) * P], ID[0:4, 0:4])
                    ins.then_inc(S("gtok_ps"), 1)
                    pe.wait_ge(S("gtok"), 1)

                def scores(h):
                    pe.wait_ge(S("bd"), 4 + h + 1)
                    for w in range(2):
                        for j in range(4):
                            q = w * 4 + j
                            if q >= 2:
                                pe.wait_ge(S("qk2"), 8 * h + q - 1)
                            mm(PS[:, q % 2, 0:T], BDS[4 + h][w][:, j, :], XC[:, 4 * h + j, :], start=True, stop=True)\
                                .then_inc(S("qk2_ps"), 1)
                    if h >= 2:
                        pe.wait_ge(S("ym_read"), h - 1)
                    for t in range(TT):
                        for j in range(4):
                            ins = mm(PS[:, 2 + t, j * P:(j + 1) * P], XM[:, 4 * h + j, 3 + t * P:3 + (t + 1) * P],
                                     BDS[4 + h][2][:, j, :], start=True, stop=True)
                        ins.then_inc(S("v2_ps"), 1)
                    if h:
                        pe.wait_ge(S("den_read"), h)
                    if h == 0:
                        gates_by_token()
                    one, tri = bc(ID[0:4, h:h + 1], (4, P)), CON[:, C_CAUS:C_CAUS + P]
                    mm(PS[:, 4, 0:P], tri, ID, start=True, stop=False)
                    mm(PS[:, 4, 0:P], one, MR[0:4, 1, 0:P], start=False, stop=True)
                    mm(PS[:, 4, P:T], one, MR[0:4, 1, P:T], start=True, stop=True)
                    mm(PS[:, 4, T:MW], tri, ID, start=True, stop=False)
                    mm(PS[:, 4, T:MW], one, MR[0:4, 1, P:T], start=False, stop=True).then_inc(S("mspread"), 1)
                    pe.wait_ge(S("qk2"), 8 * (h + 1))
                    for c, (s0, t0, t1) in enumerate(((0, 0, T), (P, P, T))):
                        for j in range(4):
                            ins = mm(PS[:, 5, 0 + c * T:c * T + t1 - t0], NQ[:, 4 + j, s0:s0 + P], NQ[:, j, t0:t1],
                                     start=j == 0, stop=j == 3)
                    ins.then_inc(S("kq_ps"), 1)

                def values(h):
                    pe.wait_ge(S("pm"), h + 1)
                    pe.wait_ge(S("v2"), 2 * (h + 1))
                    for t in range(TT):
                        for s in range(t + 1):
                            c0 = s * T if t == s else P
                            ins = mm(PS[:, 4, MW + t:MW + t + 1], PM[:, c0:c0 + P], ONES[:, 0:1],
                                     start=s == 0, stop=s == t)
                    for t in range(TT):
                        for s in range(t + 1):
                            c0 = s * T if t == s else P
                            ins = mm(PS[:, 6 + t, :], PM[:, c0:c0 + P], VM[:, s, :], start=s == 0, stop=s == t)
                    ins.then_inc(S("num_ps"), 1)

                def normed(h):
                    pe.wait_ge(S("hn"), h + 1)
                    pe.wait_ge(S("v2"), 2 * min(h + 2, 4))
                    b = NORMED_BANK[h]
                    for j in range(4):
                        for t in range(TT):
                            ins = nc.tensor.transpose(PS[:, b + j // 2, (j % 2) * T + t * P:(j % 2) * T + (t + 1) * P],
                                                      HN[:, t, j * P:(j + 1) * P], ID)
                    ins.then_inc(S("hn_ps"), 1)

                scores(0)
                for h in range(3):
                    values(h)
                    scores(h + 1)
                    normed(h)
                values(3)
                pe.wait_ge(S("ym_read"), 3)
                for q in range(4):
                    out_piece(r, r.n_proj + q, 2 * q, r.sb + KD // 2)
                    if q == 1:
                        pe.wait_ge(S("den_read"), 4)
                        normed(3)
                out_rows(r, 1)

            def gates_add(q):
                h, w, j = q // 12, q // 4 % 3, q % 4
                pe.wait_ge(S("qkv1"), q + 1)
                k = w * 16 + 4 * h + j
                at = 64 * (k // 8) + 4 * (k % 8)
                mm(PS[0:36, 6, 0:T], WGT[:, :, :, :, :].rearrange("p g m k e -> p (g m k e)")[:, at:at + 36], NQ[:, q % 8, :],
                   start=q == 0, stop=q == 47).then_inc(S("gadd"), 1)

            if plan[0].kind != "even":
                columns()
            for r in plan:
                {"even": even, "odd": odd, "moe": moe, "mod": mod, "ffn": ffn, "hyb": hyb, "mlstm": mlstm}[r.kind](r)

        BN = ST[:, 0:24].rearrange("p (t h s) -> p t h s", t=TT, h=2)
        MV = ST[:, 24:28].rearrange("p (t s) -> p t s", t=TT)
        VAR, SD, RSTD, SSQ = ST[:, 28:30], ST[:, 30:32], ST[:, 32:34], ST[:, 34:36]
        NM = ST[:, 36:40].rearrange("p (b t) -> p b t", b=2)
        SM = ST[:, 40:44].rearrange("p (b t) -> p b t", b=2)
        ES = ST[:, 44:48].rearrange("p (b t) -> p b t", b=2)
        RC = ST[:, 48:52].rearrange("p (b t) -> p b t", b=2)
        SSQ4 = ST[:, 52:56]
        CACT = ST[:, 56:64]
        NSINK = ST[:, 64:72]
        WI = ST[:, 72:80].rearrange("p (t h) -> p t h", t=TT)
        VAR4, SD4, RS4 = ST[:, 80:84], ST[:, 84:88], ST[:, 88:92]
        TICK = ST[0:1, 95:96]
        SPL = ST[:, 96:104]
        NSPL = ST[:, 104:112]
        SPA = [ST[:, 112 + 8 * i:120 + 8 * i] for i in range(5)]
        ENM = ST[:, 152:160].rearrange("p (t h) -> p t h", t=TT)
        GTOK = ST[:, 160:176].rearrange("p (m t h) -> p m t h", m=2, t=TT)
        DEN = ST[:, 176:178]
        M8 = ST[:, 178:186]
        M8B = ST[:, 104:112]

        @block.scalar
        def _(act):
            L = Lane(act, "act")
            c = L.c
            count = {"sqrt": 0, "sp": 0, "tile": 0, "ssq": 0}

            f = nc.scalar.activation

            def root(out_, in_):
                count["sqrt"] += 1
                act.wait_ge(S("var"), count["sqrt"])
                f(out_, in_, ACT.Sqrt).then_inc(S("sd"), 1)

            def softplus_exp(e, a_):
                count["sp"] += 1
                act.wait_ge(S("sp_a"), count["sp"])
                f(e, a_, ACT.Exp, scale=-1.0).then_inc(S("sp_e"), 1)

            def trn_out(r, u, mod=False, norm=False):
                for k in range(KD):
                    act.wait_ge(S("xt_ps"), 4 * u + k // 2 + 1)
                    src = PS[:, 4 + k // 2, (k % 2) * T:(k % 2 + 1) * T]
                    if mod:
                        i = r.layer * 3 + r.sub
                        f(XT[:, k, :], src, ACT.Identity, scale=MODA[:, i, k:k + 1],
                          bias=MOD[:, r.layer, r.sub * 24 + k:r.sub * 24 + k + 1]).then_inc(S("xt"), 1)
                    elif norm and r is not plan[0]:
                        n = {"moe0": 0, "odd": 1, "moe1": 2}[r.name] * KD + k
                        f(XT[:, k, :], src, ACT.Identity, scale=col("ln_g", n), bias=col("ln_b", n))\
                            .then_inc(S("xt"), 1)
                    else:
                        f(XT[:, k, :], src, ACT.Copy).then_inc(S("xt"), 1)

            def squares(r):
                for t in range(TT):
                    act.wait_ge(S("xres"), TT * r.v2 + t + 1)
                    f(XN[:, t, :], X[:, t, :], ACT.Square, accum_out=SSQ[:, t:t + 1]).then_inc(S("ssq"), 1)
                root(SD, VAR)
                act.wait_ge(S("rstd"), r.v2 + 1)
                f(XN[:, 1, :], X[:, 1, :], ACT.Copy, scale=RSTD[:, 1:2]).then_inc(S("xn1"), 1)

            def high(r, p):
                if p >= len(r.pieces):
                    return
                n = r.pieces[p][0]
                act.wait_ge(S(f"w_land{n % SLOTS}"), 48 * (n // SLOTS + 1))
                if p >= 2:
                    act.wait_ge(S("w_used"), r.used[p - 2])
                elif r.cb:
                    act.wait_ge(S("gate_up"), r.cb)
                raw, hi, _ = piece(r, p)
                f(hi, raw, ACT.Copy).then_inc(S("piece_hi"), 1)

            def prepare(r):
                if r.items:
                    split_high(r, 0, 0, True)
                else:
                    high(r, 0)
                    high(r, 1)

            def gate_row_out(r):
                act.wait_ge(S("row_ps"), r.v2 + 1)
                f(ROWB[:, 0, :], PS[:, 6:8, :].rearrange("p j n -> p (j n)"), ACT.Copy).then_inc(S("row"), 1)

            def attention(r, units):
                n = len(units)
                for i in range(n + 2):
                    if i < n:
                        u, w, b = r.ub + i, units[i], i % 2
                        act.wait_ge(S("qk_ps"), u + 1)
                        if u >= 2:
                            act.wait_ge(S("scores"), u - 1)
                        f(QK[0:w.dk, b, 0:T], PS[0:w.dk, b, 0:T], ACT.Copy, scale=w.scale).then_inc(S("qk"), 1)
                        f(QK[0:w.dk, b, T:2 * T], PS[0:w.dk, b, T:2 * T], ACT.Copy).then_inc(S("qk"), 1)
                    if i >= 2:
                        u, b = r.ub + i - 2, i % 2
                        act.wait_ge(S("pt_ps"), u + 1)
                        if u >= 2:
                            act.wait_ge(S("o_ps"), u - 1)
                        f(PT[:, b, :], PS[:, 4 + b, 0:MW], ACT.Copy).then_inc(S("pt"), 1)
                    if 1 <= i <= n:
                        u, w, b = r.ub + i - 1, units[i - 1], (i - 1) % 2
                        act.wait_ge(S("nm"), u + 1)
                        if u >= 2:
                            act.wait_ge(S("pt_ps"), u - 1)
                        if w.kind == "window":
                            c(f(ES[:, b, :], NM[:, b, :], ACT.Exp, bias=SINK[:, w.h:w.h + 1]))
                        for t, (c0, c1) in enumerate(BLK):
                            f(PB[:, b, c0:c1], LG[:, b, c0:c1], ACT.Exp, bias=NM[:, b, t:t + 1],
                              accum_out=SM[:, b, t:t + 1]).then_inc(S("p"), 1)

            def even(r):
                trn_out(r, r.u)
                prepare(r)
                for i in range(3):
                    for p in range(3 * i, 3 * i + 3):
                        high(r, p + 2)
                    act.wait_ge(S("w_used"), r.used[3 * i + 2])
                    f(TM[:, :, PW * i:PW * (i + 1)],
                      PS[:, 4 * (i % 2):4 * (i % 2) + 4, :].rearrange("p (t h) n -> p t (h n)", t=TT)[:, :, 0:PW],
                      ACT.Copy).then_inc(S("tm_even"), 1)
                    if i == 1:
                        softplus_exp(SPW[0:8, 2, :], SPW[0:8, 1, :])
                attention(r, units_of("even"))
                trn_out(r, r.u + 1)
                for p in range(r.n_proj, len(r.pieces)):
                    high(r, p + 2)
                prepare(AFTER[r.name])
                root(SD, VAR)

            def odd(r):
                trn_out(r, r.u, norm=True)
                for i, w in enumerate((PW, ODD_IN - PW)):
                    for p in range(3 * i, 3 * i + 3):
                        high(r, p + 2)
                    act.wait_ge(S("w_used"), r.used[3 * i + 2])
                    f(TMO[:, :, PW * i:PW * i + w],
                      PS[:, 4 * i:4 * i + 4, :].rearrange("p (t h) n -> p t (h n)", t=TT)[:, :, 0:w],
                      ACT.Copy).then_inc(S("tm_odd"), 1)
                act.wait_ge(S("tm_odd"), 2)
                for m, (c0, c1) in enumerate(((964, 1220), (1220, 1348))):
                    for t in range(TT):
                        c(f(XN[:, 0, 0:c1 - c0], TMO[:, t, c0:c1], ACT.Square,
                            accum_out=SSQ4[:, 2 * m + t:2 * m + t + 1]))
                f(ST[0:1, 94:95], SSQ4[0:1, 0:1], ACT.Copy).then_inc(S("ssq4"), 1)
                act.wait_ge(S("qi_ps"), 1)
                for b in range(3):
                    m = 2 if b < 2 else 1
                    f(QIT[0:HD, 2 * b:2 * b + m, :],
                      PS[0:HD, b, 0:m * T].rearrange("p (m t) -> p m t", m=m), ACT.Copy).then_inc(S("qit"), 1)
                root(SD4, VAR4)
                act.wait_ge(S("cqt_ps"), 1)
                for k in range(3):
                    g = col("odd_q_norm", k) if k < 2 else col("odd_kv_norm")
                    f(CQT[:, k, :], PS[:, k, 0:T], ACT.Copy, scale=g).then_inc(S("cqt"), 1)
                act.wait_ge(S("dq_ps"), 1)
                f(DQ.rearrange("p t h d -> p t (h d)"),
                  PS[:, 4:8, :].rearrange("p (t h) n -> p t (h n)", t=TT)[:, :, 0:768], ACT.Copy).then_inc(S("dq"), 1)
                act.wait_ge(S("dkv_ps"), 1)
                f(DKV.rearrange("p t h d -> p t (h d)"),
                  PS[:, 0:4, :].rearrange("p (t h) n -> p t (h n)", t=TT), ACT.Copy).then_inc(S("dkv"), 1)
                attention(r, units_of("odd"))
                trn_out(r, r.u + 1)
                for p in range(r.n_proj, len(r.pieces)):
                    high(r, p + 2)
                prepare(AFTER[r.name])
                root(SD, VAR)

            def split_high(r, i, j, gate_up):
                s, b = (r.n + j // CH) % SLOTS, j % 2
                gu, dn = raw_slot(r, j)
                if gate_up:
                    act.wait_ge(S(f"w_land{s}"), land_count(r, i, j))
                    if past(i, j, 2):
                        act.wait_ge(S("gate_up"), i * r.per + (r.cb + j - 1))
                    elif r.before and r.before.items:
                        act.wait_ge(S("gate_up"), r.cb + j - 1)
                    elif r.before:
                        act.wait_ge(S("w_used"), r.before.used[j - 2])
                    f(WGH[:, b, :].rearrange("p (k f) -> p k f", f=P), gu, ACT.Copy).then_inc(S("hi_gu"), 1)
                else:
                    if past(i, j, 2):
                        act.wait_ge(S("w_used"), i * r.per + (r.wb + j - 1))
                    f(WDH[:, b, :], dn, ACT.Copy).then_inc(S("hi_dn"), 1)

            def hidden_start(r):
                split_high(r, 0, 1, True)
                if r.wb:
                    act.wait_ge(S("w_used"), r.wb)
                split_high(r, 0, 0, False)

            def hidden_layer(r):
                def step(i, j):
                    act.wait_ge(S("gate_up"), i * r.per + (r.cb + j + 1))
                    if past(i, j, 2):
                        act.wait_ge(S("hidden"), i * r.per + (r.cb + j - 1))
                    f(SG[:, j % 2, :], PS[:, 4 + j % 2, 0:T], ACT.Silu).then_inc(S("silu"), 1)
                    if exists(r, i, j, 2):
                        split_high(r, i, j + 2, True)
                    if exists(r, i, j, 1):
                        split_high(r, i, j + 1, False)

                run_turns(act, CH * r.items, r.per, step)
                if r.name in AFTER:
                    prepare(AFTER[r.name])

            def moe(r):
                if r.me == 0:
                    act.wait_ge(S("cols"), ROW_TILES)
                    f(CACT, col("c_2", 0, KD), ACT.Silu).then_inc(S("c_act"), 1)
                hidden_start(r)
                trn_out(r, r.u, norm=True)
                act.wait_ge(S("route_ps"), r.me + 1)
                f(RT[:, 0, :], PS[:, 6, 0:TT * NE], ACT.Sigmoid).then_inc(S("aff"), 1)
                act.wait_ge(S("gates_ps"), r.me + 1)
                f(GT[0:NE, :], PS[0:NE, 7, 0:T], ACT.Copy).then_inc(S("gates_t"), 1)
                for k in range(8):
                    act.wait_ge(S("rows_ps"), 8 * r.me + k + 1)
                    f(GB[:, 2 * k:2 * k + 2, :], PS[:, 6 + k % 2, :].rearrange("p (e t) -> p e t", e=2),
                      ACT.Copy).then_inc(S("gate_rows"), 1)
                hidden_layer(r)
                root(SD, VAR)

            def ffn(r):
                squares(r)
                hidden_start(r)
                trn_out(r, r.u, True)
                gate_row_out(r)
                hidden_layer(r)

            def mod(r):
                pass

            def tap(r, f_, raw, banks, dst, w, b, n, i):
                act.wait_ge(S("w_used"), r.wb + f_ + 1)
                f(dst, PS[:, f_ % banks, 0:T], ACT.Identity, scale=col(w, 3 * n + i), bias=col(b, i))\
                    .then_inc(S("tap_out"), 1)
                f(raw, PS[:, f_ % banks, 0:T], ACT.Copy).then_inc(S("tile_out"), 1)

            def tile_out(r, f_, dst, banks):
                act.wait_ge(S("w_used"), r.wb + f_ + 1)
                f(dst, PS[:, f_ % banks, 0:T], ACT.Copy).then_inc(S("tile_out"), 1)

            def hyb(r):
                squares(r)
                trn_out(r, r.u, True)
                gate_row_out(r)

                act.wait_ge(S("pads"), 1)
                conv = 0
                for f_, k in enumerate(HYB_TILES):
                    p = TILE_OF["hyb"][f_][0]
                    if f_ + 1 == len(HYB_TILES) or TILE_OF["hyb"][f_ + 1][0] != p:
                        high(r, p + 2)
                    if k < 8:
                        dst = GA[:, k, :]
                    elif 16 <= k < 24:
                        dst = ZH[:, k - 16, :]
                    elif k < 36:
                        dst = RAW[:, k % 2, 3:]
                        if conv >= 2:
                            act.wait_ge(S("conv"), conv - 1)
                        conv += 1
                    if 8 <= k < 16:
                        tap(r, f_, dst, 6, XL[:, k - 8, :], "lru_conv_w_2", "lru_conv_b_2", 8, k - 8)
                    elif 24 <= k < 36:
                        tap(r, f_, dst, 6, XBC[:, k - 24, :], "ssd_conv_w_2", "ssd_conv_b_2", 12, k - 24)
                    elif k == 36:
                        act.wait_ge(S("w_used"), r.wb + f_ + 1)
                        act.wait_ge(S("small_load"), 16 * N_SMALL)
                        f(SPH[4], PS[0:16, f_ % 6, 0:T], ACT.Identity, bias=BF[0:16, 1:2]).then_inc(S("tile_out"), 1)
                    else:
                        tile_out(r, f_, dst, 6)
                    if f_ == 8:
                        softplus_exp(SPA[1], SPA[0])
                    if f_ == STEP_AT:
                        f(BF[0:16, 5:6], BF[0:16, 2:3], ACT.Exp).then_inc(S("a_exp"), 1)
                        softplus_exp(SPH[1], SPH[0])
                    if LRU_AT <= f_ < LRU_AT + 8:
                        lru_gates(f_ - LRU_AT)
                    if f_ == LRU_AT + 12:
                        root(RG, RG)
                    if k == 1:
                        f(ZH, ZH, ACT.Silu).then_inc(S("zsilu"), 1)
                        act.wait_ge(S("conv"), 20)
                    if k in (3, 5, 7):
                        xbc = XBC[:, 4 * (k // 2 - 1):4 * (k // 2), :]
                        f(xbc, xbc, ACT.Silu).then_inc(S("xbc"), 1)
                for q in range(4):
                    act.wait_ge(S("gelu_step"), 3 * q + 3)
                    f(H2[:, 2 * q:2 * q + 2, :], H2[:, 2 * q:2 * q + 2, :], ACT.Tanh, scale=0.7978845608028654)\
                        .then_inc(S("gelu_tanh"), 1)
                for h in range(16):
                    act.wait_ge(S("spread"), h + 1)
                    if h >= 2:
                        act.wait_ge(S("head_ps"), h - 1)
                    for t, (c0, c1) in enumerate(((0, T), (T, MW))):
                        f(EH[:, h % 2, c0:c1], PS[:, 4 + h % 2, c0:c1], ACT.Exp,
                          bias=ACD[:, 16 * t + h:16 * t + h + 1]).then_inc(S("eh"), 1)
                    if h in (7, 10):
                        high(r, r.n_proj + h // 3)
                    if h == 14:
                        high(r, r.n_proj + 4)
                root(H2_RS[:, 0, :], H2_RS[:, 0, :])
                high(r, r.n_proj + 5)
                root(H2_RS[:, 1, :], H2_RS[:, 1, :])
                for p in range(r.n_proj + 4, len(r.pieces)):
                    high(r, p + 2)
                prepare(AFTER[r.name])

            def lru_gates(i):
                act.wait_ge(S("lru_ps"), i + 1)
                b = 6 + i % 2
                f(RG[:, i, :], PS[:, b, 0:T], ACT.Sigmoid, bias=col("lru_ba_2", i)).then_inc(S("lru_gates"), 1)
                f(IG[:, i, :], PS[:, b, T:2 * T], ACT.Sigmoid, bias=col("lru_bx_2", i)).then_inc(S("lru_gates"), 1)
                if i == 3:
                    act.wait_ge(S("spl"), 1)
                if i % 4 == 3:
                    act.wait_ge(S("lru_gates"), 2 * i + 2)
                    for m in range(i - 3, i + 1):
                        f(H1[:, m, :], RG[:, m, :], ACT.Exp, scale=NSPL[:, m:m + 1])
                        f(RG[:, m, :], RG[:, m, :], ACT.Tanh, scale=SPL[:, m:m + 1]).then_inc(S("lru_at"), 1)

            def mlstm(r):
                squares(r)
                trn_out(r, r.u, True)
                gate_row_out(r)
                for f_ in range(32):
                    if f_ % 2 == 1:
                        high(r, (f_ + 1) // 2 + 1)
                    if f_ < 16:
                        tap(r, f_, XM[:, f_, 3:], 6, XC[:, f_, :], "mlstm_conv_w_2", "mlstm_conv_b_2", 16, f_)
                    else:
                        tile_out(r, f_, ZM[:, f_ - 16, :], 6)
                    if f_ in (21, 24, 27, 30):
                        h = (f_ - 21) // 3
                        act.wait_ge(S("mconv"), 4 * h + 4)
                        f(XC[:, 4 * h:4 * h + 4, :], XC[:, 4 * h:4 * h + 4, :], ACT.Silu).then_inc(S("xc"), 1)
                for q in range(48):
                    act.wait_ge(S("qkv1_ps"), q + 1)
                    if q >= 8:
                        act.wait_ge(S("gadd"), q - 7)
                    f(NQ[:, q % 8, :], PS[:, 2 + q % 4, 0:T], ACT.Copy).then_inc(S("qkv1"), 1)
                act.wait_ge(S("gadd"), 48)
                f(SPX[4], PS[32:36, 6, 0:T], ACT.Copy).then_inc(S("f_row"), 1)
                softplus_exp(SPX[1], SPX[0])
                for h in range(4):
                    if h == 0:
                        act.wait_ge(S("gadd"), 48)
                    else:
                        act.wait_ge(S("kq_ps"), h)
                        act.wait_ge(S("num_ps"), h)
                    for q in range(8):
                        act.wait_ge(S("qk2_ps"), 8 * h + q + 1)
                        f(NQ[:, q, :], PS[:, q % 2, 0:T], ACT.Copy).then_inc(S("qk2"), 1)
                    if h:
                        root(SD, VAR)
                    for t in range(TT):
                        act.wait_ge(S("v2_ps"), 2 * h + t + 1)
                        if h == 0:
                            act.wait_ge(S("gadd"), 48)
                        f(VM[:, t, :], PS[:, 2 + t, :], ACT.Copy).then_inc(S("v2"), 1)
                    if h == 0:
                        act.wait_ge(S("gtok"), 1)
                        f(ENM, GTOK[:, 1, :, :], ACT.Exp, scale=-1.0).then_inc(S("enm"), 1)
                    act.wait_ge(S("mspread"), h + 1)
                    for t, (c0, c1) in enumerate(((0, T), (T, MW))):
                        f(EM[:, c0:c1], PS[:, 4, c0:c1], ACT.Exp, bias=GTOK[:, 0, t, h:h + 1]).then_inc(S("em_exp"), 1)
                    if h == 0:
                        f(ZM, ZM, ACT.Silu).then_inc(S("zm"), 1)
                root(SD, VAR)
                for p in range(r.n_proj, len(r.pieces)):
                    high(r, p + 2)
                prepare(AFTER[r.name])

            def final():
                for t in range(TT):
                    act.wait_ge(S("xres"), TT * v2_end + t + 1)
                    f(XN[:, t, :], X[:, t, :], ACT.Square, accum_out=SSQ[:, t:t + 1]).then_inc(S("ssq"), 1)
                root(SD, VAR)

            act.dma_start(CON[:, :], a["const"]).then_inc(S("con_load"), 16)
            for r in plan:
                {"even": even, "odd": odd, "moe": moe, "mod": mod, "ffn": ffn, "hyb": hyb, "mlstm": mlstm}[r.kind](r)
            if FINAL:
                final()

        @block.vector
        def _(dve):
            L = Lane(dve, "dve")
            c = L.c
            V = nc.vector
            count, marks = {"var": 0, "sp": 0, "ssq": 0, "ln": 0}, [0]

            def mark():
                marks[0] += 1
                return V.memset(MARKS[0:1, marks[0]:marks[0] + 1], 0.0)

            def ts(out_, in_, s1, s2=None, o1=ALU.mult, o2=None):
                return V.tensor_scalar(out_, in_, s1, s2, o1, o2) if o2 is not None else \
                    V.tensor_scalar(out_, in_, s1, s2, o1)

            def tt(out_, x_, y_, op=ALU.mult):
                return V.tensor_tensor(out_, x_, y_, op)

            def stt(out_, x_, s, y_, o1, o2):
                return V.scalar_tensor_tensor(out=out_, in0=x_, scalar=s, in1=y_, op0=o1, op1=o2)

            def root(rstd, sd):
                count["var"] += 1
                mark().then_inc(S("var"), 1)
                dve.wait_ge(S("sd"), count["var"])
                c(V.reciprocal(rstd, sd))

            def softplus(out_, x_, a_, e, d, w):
                count["sp"] += 1
                c(ts(a_, x_, -1.0))
                c(tt(a_, a_, x_, ALU.max))
                mark().then_inc(S("sp_a"), 1)
                dve.wait_ge(S("sp_e"), count["sp"])
                c(ts(d, e, 2.0, None, ALU.add))
                c(V.reciprocal(d, d))
                c(tt(e, e, d))
                c(tt(w, e, e))
                c(ts(d, w, 1.0 / 17))
                for k in range(7, 0, -1):
                    c(stt(d, d, 1.0 / (2 * k + 1), w, ALU.add, ALU.mult))
                c(stt(d, d, 1.0, e, ALU.add, ALU.mult))
                c(ts(w, x_, 0.0, None, ALU.max))
                c(stt(out_, d, 2.0, w, ALU.mult, ALU.add))

            def low(r, p):
                if p >= len(r.pieces):
                    return
                dve.wait_ge(S("piece_hi"), r.pb + p + 1)
                raw, hi, lo = piece(r, p)
                tt(lo, raw, hi.bitcast(F32), ALU.subtract).then_inc(S("piece_lo"), 1)

            def first_low(r, m):
                if r.items:
                    split_low(r, 0, m, True)
                else:
                    low(r, m)

            def split_tiles(n, k0, src):
                V.tensor_copy(XTH[:, k0:k0 + 2, :], src).then_inc(S("x_high"), 1)
                dve.wait_ge(S("x_high"), n + 1)
                tt(XTL[:, k0:k0 + 2, :], src, XTH[:, k0:k0 + 2, :].bitcast(F32), ALU.subtract).then_inc(S("x_low"), 1)

            def residual_norm(r):
                if r.ln:
                    dve.wait_ge(S("x_ready"), r.ln)
                for t in range(TT):
                    if t == 0:
                        dve.wait_ge(S("y0"), work.index(r) + 1)
                    else:
                        dve.wait_ge(S("w_used"), r.we)
                    c(stt(X[:, t, :], X[:, t, :], ALPHA, PSY[:, t, :], ALU.mult, ALU.add))
                    V.bn_stats(BN[:, t, 0, :], X[:, t, 0:512])
                    c(V.bn_stats(BN[:, t, 1, :], X[:, t, 512:1024]))
                    c(V.bn_aggr(MV[:, t, :], BN[:, t, :, :]))
                c(ts(VAR, MV[:, :, 1], LN_EPS, None, ALU.add))
                root(RSTD, SD)
                for t in range(TT):
                    ts(X[:, t, :], X[:, t, :], MV[:, t, 0:1], RSTD[:, t:t + 1], ALU.subtract, ALU.mult)\
                        .then_inc(S(f"normed{t}"), 1)
                for t in range(TT):
                    dve.wait_ge(S(f"normed{t}"), r.ln + 1)
                if r.scaled_by_pool:
                    return
                dve.wait_ge(S("ln_load"), 32 * (r.ln + 1))
                for t in range(TT):
                    c(tt(X[:, t, :], X[:, t, :], ROWB[:, 0, :]))
                    tt(X[:, t, :], X[:, t, :], ROWB[:, 1, :], ALU.add).then_inc(S("xres"), 1)
                dve.wait_ge(S("xres"), TT)
                mark().then_inc(S("x_ready"), 1)

            def squares():
                count["ssq"] += 2
                dve.wait_ge(S("ssq"), count["ssq"])
                c(ts(VAR, SSQ, 1.0 / D, EPS, ALU.mult, ALU.add))
                root(RSTD, SD)

            def begin(r):
                squares()
                mark().then_inc(S("rstd"), 1)
                ts(XN[:, 0, :], X[:, 0, :], RSTD[:, 0:1]).then_inc(S("xn0"), 1)
                first_low(r, 0)

            def diagonals(r):
                i = r.layer * 3 + r.sub
                c(tt(DG, bc(ID.unsqueeze(1), (P, KD, P)), bc(MODG[:, i, :].unsqueeze(2), (P, KD, P))))
                mark().then_inc(S("diag"), 1)

            def residual_gate(r):
                dve.wait_ge(S("row"), r.v2 + 1)
                for t in range(TT):
                    if t == 0:
                        dve.wait_ge(S("y0"), work.index(r) + 1)
                    else:
                        dve.wait_ge(S("w_used"), r.we)
                    c(tt(XN[:, t, :], PSY[:, t, :], ROWB[:, 0, :]))
                    tt(X[:, t, :], X[:, t, :], XN[:, t, :], ALU.add).then_inc(S("xres"), 1)
                dve.wait_ge(S("xres"), TT * (r.v2 + 2))

            def attention(r, units, beside=None):
                n = len(units)
                for i in range(n + 2):
                    if i >= 2:
                        u, w, b = r.ub + i - 2, units[i - 2], i % 2
                        dve.wait_ge(S("p"), 2 * (u + 1))
                        if w.kind == "window":
                            c(tt(SM[:, b, :], SM[:, b, :], ES[:, b, :], ALU.add))
                        c(V.reciprocal(RC[:, b, :], SM[:, b, :]))
                    if i < n:
                        u, w, b = r.ub + i, units[i], i % 2
                        dve.wait_ge(S("scores"), u + 1)
                        if u >= 2:
                            dve.wait_ge(S("p"), 2 * (u - 1))
                        s, lg = PS[:, 2 + b, 0:MW], LG[:, b, :]
                        slope = 2.0 ** -(w.h + 1)
                        if w.kind == "window":
                            stt(lg, CON[:, C_NEGW:C_NEGW + MW], slope, s, ALU.mult, ALU.add).then_inc(S("logits"), 1)
                        elif w.kind == "dsa":
                            stt(lg, CON[:, C_NEGC:C_NEGC + MW], slope, s, ALU.mult, ALU.add).then_inc(S("logits"), 1)
                            dve.wait_ge(S("logits"), u + 1)
                            c(tt(lg, lg, SELM, ALU.add))
                        elif w.kind == "mla":
                            tt(lg, s, CON[:, C_CAUS:C_CAUS + MW], ALU.add).then_inc(S("logits"), 1)
                        else:
                            for t, (c0, c1) in enumerate(BLK):
                                ins = stt(lg[:, c0:c1], s[:, c0:c1], CTOK[:, t, w.h:w.h + 1],
                                          CON[:, C_CAUS + c0:C_CAUS + c1], ALU.add, ALU.add)
                                if t == 0:
                                    c(ins)
                            ins.then_inc(S("logits"), 1)
                        dve.wait_ge(S("logits"), u + 1)
                        for t, (c0, c1) in enumerate(BLK):
                            ins = V.tensor_reduce(NM[:, b, t:t + 1], lg[:, c0:c1], AX.X, ALU.max, negate=True)
                            if t == 0 or w.kind == "window":
                                c(ins)
                        if w.kind == "window":
                            ins = ts(NM[:, b, :], NM[:, b, :], NSINK[:, w.h:w.h + 1], None, ALU.min)
                        ins.then_inc(S("nm"), 1)
                    if beside:
                        beside(i)
                    if i >= 2:
                        u, w, b = r.ub + i - 2, units[i - 2], i % 2
                        dve.wait_ge(S("o_ps"), u + 1)
                        tt(XN[:, :, w.at:w.at + HD], PS[:, 6 + b, 0:2 * HD].rearrange("p (t d) -> p t d", t=TT),
                           bc(RC[:, b, :].unsqueeze(2), (P, TT, HD))).then_inc(S("o"), 1)
                dve.wait_ge(S("o"), r.ub + n)

            def columns():
                for t in range(ROW_TILES):
                    m = min(P, NROWS - t * P)
                    dve.wait_ge(S("cols_ps"), t + 1)
                    V.tensor_copy(COL[:, t * P:t * P + m], PS[:, 4 + t, 0:m]).then_inc(S("cols"), 1)
                dve.wait_ge(S("cols"), ROW_TILES)
                mark().then_inc(S("cols_done"), 1)

            def even(r):
                dve.wait_ge(S("x_load"), 32)
                for t in range(TT):
                    mark().then_inc(S(f"xn{t}"), 1)
                first_low(r, 0)
                split_x(r)
                first_low(r, 1)
                for p in range(6):
                    low(r, p + 2)
                dve.wait_ge(S("w_used"), r.forget_used)
                dve.wait_ge(S("small_load"), 16 * N_SMALL)
                c(ts(NSINK, SINK[:, :], -1.0))
                ts(SPW[0:8, 0, :], PS[0:8, 3, 0:T], -1.0, BF[0:8, 0:1], ALU.mult, ALU.subtract).then_inc(S("forget"), 1)
                dve.wait_ge(S("forget"), 1)
                softplus(SPW[0:8, 5, :], *[SPW[0:8, k, :] for k in range(5)])
                c(V.tensor_tensor_scan(NCT[0:8, :], ONES[0:8, :], SPW[0:8, 5, :], 0.0, ALU.mult, ALU.add))
                ts(CT[0:8, :], NCT[0:8, :], -1.0).then_inc(S("ct"), 1)
                for p in range(6, r.n_proj):
                    low(r, p + 2)
                columns()
                dve.wait_ge(S("ct_ps"), 1)
                V.tensor_copy(CTOK.rearrange("p t h -> p (t h)"), PS[:, 4, 0:16]).then_inc(S("ctok"), 1)
                dve.wait_ge(S("ctok"), 1)
                attention(r, units_of("even"))
                for t in range(TT):
                    mark().then_inc(S(f"xn{t}"), 1)
                split_x(r, True)
                for p in range(r.n_proj, len(r.pieces)):
                    low(r, p + 2)
                residual_norm(r)

            def rope(dst1, dst2, x1, x2, cos, sin, s4):
                for s_, (x_, y_) in zip(s4, ((x1, cos), (x2, sin), (x1, sin), (x2, cos))):
                    c(tt(s_, x_, y_))
                c(tt(dst1, s4[0], s4[1], ALU.subtract))
                c(tt(dst2, s4[2], s4[3], ALU.add))

            def odd(r):
                for t in range(TT):
                    mark().then_inc(S(f"xn{t}"), 1)
                first_low(r, 0)
                split_x(r)
                first_low(r, 1)
                for p in range(r.n_proj):
                    low(r, p + 2)
                dve.wait_ge(S("ssq4"), 1)
                c(ts(VAR4[:, 0:2], SSQ4[:, 0:2], 1.0 / 256, EPS, ALU.mult, ALU.add))
                c(ts(VAR4[:, 2:4], SSQ4[:, 2:4], 1.0 / 128, EPS, ALU.mult, ALU.add))
                root(RS4, SD4)
                for t in range(TT):
                    c(ts(CQN[:, t, 0:2, :].rearrange("p k d -> p (k d)"), TMO[:, t, 964:1220], RS4[:, t:t + 1]))
                    c(ts(CQN[:, t, 2, :], TMO[:, t, 1220:1348], RS4[:, 2 + t:3 + t]))
                mark().then_inc(S("cqn"), 1)
                c(ts(WI, TMO[:, :, 960:964], 1.0 / 16))
                for h in range(4):
                    dve.wait_ge(S("dots"), h + 1)
                    for t, (c0, c1) in enumerate(BLK):
                        dst = SCR if h == 0 else TMPS
                        c(ts(dst[:, c0:c1], PS[:, 4 + h, c0:c1], 0.0, WI[:, t, h:h + 1], ALU.max, ALU.mult))
                    if h:
                        c(tt(SCR, SCR, TMPS, ALU.add))
                c(tt(SCR, SCR, CON[:, C_CAUS:C_CAUS + MW], ALU.add))
                mark().then_inc(S("dsa"), 1)
                dve.wait_ge(S("dq"), 1)
                s4 = [SELM[:, 128 * i:128 * i + 128] for i in range(3)] + [TMPS[:, 0:128]]
                for t in range(TT):
                    cos = CON[:, C_COS + 16 * t:C_COS + 16 * t + 16]
                    sin = CON[:, C_SIN + 16 * t:C_SIN + 16 * t + 16]
                    rope(DQ[:, t, :, 64:80], DQ[:, t, :, 80:96], DQ[:, t, :, 64:80], DQ[:, t, :, 80:96],
                         bc(cos.unsqueeze(1), (P, 8, 16)), bc(sin.unsqueeze(1), (P, 8, 16)),
                         [s_.rearrange("p (h d) -> p h d", h=8) for s_ in s4])
                    rope(TMPS[:, 128:144], TMPS[:, 144:160], TMO[:, t, 1348:1364], TMO[:, t, 1364:1380], cos, sin,
                         [s_[:, 0:16] for s_ in s4])
                    c(V.tensor_copy(DK[:, t, :, 64:96], bc(TMPS[:, 128:160].unsqueeze(1), (P, 8, 32))))
                dve.wait_ge(S("dkv"), 1)
                c(V.tensor_copy(DK[:, 0, :, 0:64], DKV[:, 0, :, 0:64]))
                c(V.tensor_copy(DK[:, 1, :, 0:64], DKV[:, 1, :, 0:64]))
                mark().then_inc(S("mla_ready"), 1)

                def select(i):
                    if i < 8:
                        for b, (c0, c1) in enumerate(BLK):
                            m8 = M8[:, 0:8] if b == 0 else M8B
                            c(V.max(m8, SCR[:, c0:c1]))
                            c(V.match_replace(SCR[:, c0:c1], m8, SCR[:, c0:c1], -3.0e38))
                    if i == 7:
                        c(ts(SELM, SCR, -2.0e38, None, ALU.is_le))
                        c(ts(SELM, SELM, 1.0, -NEG, ALU.subtract, ALU.mult))

                attention(r, units_of("odd"), select)
                for t in range(TT):
                    mark().then_inc(S(f"xn{t}"), 1)
                split_x(r, True)
                for p in range(r.n_proj, len(r.pieces)):
                    low(r, p + 2)
                residual_norm(r)

            def first_of(dst, x_, m, tie, n, tmp):
                c(V.tensor_reduce(m, x_, AX.X, ALU.max))
                c(tt(tmp, x_, bc(m.unsqueeze(2), (P, TT, n)), ALU.is_equal))
                c(tt(tmp, tmp, bc(tie.unsqueeze(1), (P, TT, n))))
                c(V.tensor_reduce(m, tmp, AX.X, ALU.max))
                c(tt(dst, tmp, bc(m.unsqueeze(2), (P, TT, n)), ALU.is_equal))

            def route(r):
                v = [RT[:, k, :].rearrange("p (t e) -> p t e", t=TT) for k in range(12)]
                aff, sel, one1, one2, tmp, w = v[0], v[1], v[2], v[3], v[4], v[5]
                grp, gone, gtmp = v[6][:, :, 0:4], v[7][:, :, 0:4], v[8][:, :, 0:4]
                m = RT[:, 9, 0:2]
                dve.wait_ge(S("aff"), r.me + 1)
                dve.wait_ge(S("small_load"), 16 * N_SMALL)
                c(tt(sel, aff, bc(RB[:, :].unsqueeze(1), (P, TT, NE)), ALU.add))
                q = sel.rearrange("p t (g e) -> p t g e", g=4)
                for k, (i, j) in enumerate(((0, 1), (0, 2), (0, 3), (1, 2), (1, 3), (2, 3))):
                    c(tt(RP[:, :, :, k], q[:, :, :, i], q[:, :, :, j], ALU.add))
                c(V.tensor_reduce(grp, RP, AX.X, ALU.max))
                first_of(gone, grp, m, CON[:, C_TIE:C_TIE + 4], 4, gtmp)
                c(ts(gone, gone, 1.0, -NEG, ALU.subtract, ALU.mult))
                for t in range(TT):
                    c(tt(sel[:, t, :].rearrange("p (g e) -> p g e", g=4), sel[:, t, :].rearrange("p (g e) -> p g e", g=4),
                         bc(gone[:, t, :].unsqueeze(2), (P, 4, 4)), ALU.add))
                first_of(one1, sel, m, CON[:, C_TIE:C_TIE + NE], NE, tmp)
                c(stt(sel, one1, 10 * NEG, sel, ALU.mult, ALU.add))
                first_of(one2, sel, m, CON[:, C_TIE:C_TIE + NE], NE, tmp)
                c(tt(one1, one1, one2, ALU.add))
                c(tt(w, one1, aff))
                c(V.tensor_reduce(m, w, AX.X, ALU.add))
                c(V.reciprocal(m, m))
                c(tt(v[11], w, bc(m.unsqueeze(2), (P, TT, NE))))
                mark().then_inc(S("gates"), 1)

            def split_low(r, i, j, gate_up):
                b = j % 2
                gu, dn = raw_slot(r, j)
                if gate_up:
                    dve.wait_ge(S("hi_gu"), i * r.per + (r.cb + j + 1))
                    high = WGH[:, b, :].bitcast(F32).rearrange("p (k f) -> p k f", f=P)
                    tt(WGL[:, b, :].rearrange("p (k f) -> p k f", f=P), gu, high, ALU.subtract).then_inc(S("lo_gu"), 1)
                else:
                    dve.wait_ge(S("hi_dn"), i * r.per + (r.cb + j + 1))
                    tt(WDL[:, b, :], dn, WDH[:, b, :].bitcast(F32), ALU.subtract).then_inc(S("lo_dn"), 1)

            def hidden_layer(r):
                gated = r.kind == "moe"
                n_steps = 3 if gated else 2

                def hidden(i, j):
                    step = [0]

                    def then(ins):
                        step[0] += 1
                        ins.then_inc(S("hid_step"), 1)
                        dve.wait_ge(S("hid_step"), i * (n_steps * r.per) + (r.hs + n_steps * j + step[0]))

                    b = j % 2
                    dve.wait_ge(S("silu"), i * r.per + (r.cb + j + 1))
                    if past(i, j, 2):
                        dve.wait_ge(S("w_used"), i * r.per + (r.wb + j - 1))
                    if gated:
                        e = bass.ds(i * (r.per // 4) + j // 4, 1)
                        then(tt(SG[:, b, :], SG[:, b, :], GB[:, e, :].rearrange("p a t -> p (a t)")))
                    then(tt(HR[:, b, :], SG[:, b, :], PS[:, 4 + b, T:2 * T]))
                    then(V.tensor_copy(HTH[:, b, :], HR[:, b, :]))
                    tt(HTL[:, b, :], HR[:, b, :], HTH[:, b, :].bitcast(F32), ALU.subtract).then_inc(S("hidden"), 1)

                def mod_products(i, m):
                    n = r.me * MOE_G + m
                    dve.wait_ge(S(f"mod_land{m % 2}"), i * (16 * TURN // 2) + 16 * (n // 2 + 1))
                    if m == 0:
                        if past(i, m, 1):
                            dve.wait_ge(S("mod_ps"), i + r.me * (MOE_G // TURN))
                        elif r.me:
                            dve.wait_ge(S("mod_ps"), r.me * (MOE_G // TURN))
                        ts(ADC, ADW[:, 0, :], CACT[:, 0:1]).then_inc(S("mod_acc"), 1)
                    else:
                        dve.wait_ge(S("mod_acc"), i * TURN + n)
                        stt(ADC, ADW[:, m % 2, :], CACT[:, m:m + 1], ADC, ALU.mult, ALU.add).then_inc(S("mod_acc"), 1)

                def mod_out(i):
                    n = r.me * (MOE_G // TURN)
                    dve.wait_ge(S("mod_ps"), i + (n + 1))
                    w = AW // P
                    at = bass.ds(i * w, w)
                    tt(MOD[:, r.layer, at], PS[:, 6, 0:w], col("ada_b_2", 72 * r.layer, 72)[:, at], ALU.add)\
                        .then_inc(S("mod_out"), 1)

                def step(i, j):
                    hidden(i, j)
                    if exists(r, i, j, 2):
                        split_low(r, i, j + 2, True)
                    if exists(r, i, j, 1):
                        split_low(r, i, j + 1, False)
                    if gated and j % 2 == 0:
                        mod_products(i, j // 2)
                    if gated and j == r.per - 1:
                        mod_out(i)

                run_turns(dve, CH * r.items, r.per, step)

            def hidden_start(r):
                split_low(r, 0, 0, False)

            def split_x(r, again=False):
                for k in range(0, KD, 2):
                    dve.wait_ge(S("xt"), 8 * (r.u + again) + k + 2)
                    split_tiles(r.sb + KD // 2 * again + k // 2, k, XT[:, k:k + 2, :])

            def moe(r):
                for t in range(TT):
                    mark().then_inc(S(f"xn{t}"), 1)
                first_low(r, 0)
                split_x(r)
                first_low(r, 1)
                hidden_start(r)
                route(r)
                dve.wait_ge(S("gate_rows"), 8 * (r.me + 1))
                dve.wait_ge(S("c_act"), 1)
                hidden_layer(r)
                if r.me:
                    modulation()
                residual_norm(r)

            def ffn(r):
                begin(r)
                split_x(r)
                first_low(r, 1)
                diagonals(r)
                hidden_start(r)
                hidden_layer(r)
                residual_gate(r)

            def mod(r):
                pass

            def modulation():
                dve.wait_ge(S("mod_out"), 2 * (MOE_G // TURN))
                for l in range(2):
                    for s in range(3):
                        i = 3 * l + s
                        c(stt(MODA[:, i, :], MOD[:, l, 24 * s + 8:24 * s + 16], 1.0, col("norm_g_2", 8 * i, 8),
                              ALU.add, ALU.mult))
                        c(ts(MODG[:, i, :], MOD[:, l, 24 * s + 16:24 * s + 24], 1.0, 1.0 if s == 1 else 0.5,
                             ALU.add, ALU.mult))

            def conv4(dst, x_, w, b, n, i, sem):
                for k in (2, 1):
                    c(stt(dst, x_[:, k:k + T], col(w, k * n + i), dst, ALU.mult, ALU.add))
                stt(dst, x_[:, 0:T], col(w, i), dst, ALU.mult, ALU.add).then_inc(S(sem), 1)

            def hyb(r):
                begin(r)
                c(V.memset(RAW[:, :, 0:3], 0.0))
                mark().then_inc(S("pads"), 1)
                split_x(r)
                first_low(r, 1)
                diagonals(r)
                for f_, k in enumerate(HYB_TILES):
                    p = TILE_OF["hyb"][f_][0]
                    if f_ + 1 == len(HYB_TILES) or TILE_OF["hyb"][f_ + 1][0] != p:
                        low(r, p + 2)
                    if 8 <= k < 16:
                        dve.wait_ge(S("tile_out"), EV_BASE["hyb"] + f_ + 1)
                        conv4(XL[:, k - 8, :], RAW[:, k % 2, :], "lru_conv_w_2", "lru_conv_b_2", 8, k - 8, "conv")
                    if 24 <= k < 36:
                        dve.wait_ge(S("tile_out"), EV_BASE["hyb"] + f_ + 1)
                        conv4(XBC[:, k - 24, :], RAW[:, k % 2, :], "ssd_conv_w_2", "ssd_conv_b_2", 12, k - 24, "conv")
                    if f_ == 8:
                        c(ts(SPA[4], col("lru_lambda_2", 0, 8), -1.0))
                        softplus(SPL, SPA[4], SPA[0], SPA[1], SPA[2], SPA[3])
                        c(ts(SPL, SPL, 8.0))
                        c(ts(NSPL, SPL, -1.0))
                        mark().then_inc(S("spl"), 1)
                    if f_ == STEP_AT:
                        dve.wait_ge(S("row_ps"), r.v2 + 1)
                        dve.wait_ge(S("a_exp"), 1)
                        c(ts(BF[0:16, 5:6], BF[0:16, 5:6], -1.0))
                        dve.wait_ge(S("tile_out"), EV_BASE["hyb"] + DT_AT + 1)
                        softplus(DTR[0:16, :], SPH[4], *SPH[0:4])
                        c(ts(SPH[4], DTR[0:16, :], BF[0:16, 5:6]))
                        c(V.tensor_tensor_scan(AC[0:16, :], ONES[0:16, :], SPH[4], 0.0, ALU.mult, ALU.add))
                        mark().then_inc(S("ssd_rows"), 1)
                    if f_ == LRU_AT + 10:
                        dve.wait_ge(S("a_squared"), 1)
                        c(stt(RG, H2, 1.0, RG, ALU.add, ALU.mult))
                        count["var"] += 1
                        mark().then_inc(S("var"), 1)
                        mark().then_inc(S("h2_free"), 1)
                    if f_ == LRU_AT + 13:
                        dve.wait_ge(S("gated_in"), 1)
                        dve.wait_ge(S("sd"), count["var"])
                        c(tt(IG[:, :, :], IG[:, :, :], RG))
                    if f_ in (LRU_AT + 14, LRU_AT + 16):
                        for i in range(0, 4) if f_ == LRU_AT + 14 else range(4, 8):
                            c(V.tensor_tensor_scan(XL[:, i, :], H1[:, i, :], IG[:, i, :], 0.0, ALU.mult, ALU.add))
                def gelu(q):
                    k = 2 * q
                    dve.wait_ge(S("gelu_tanh"), q + 1)
                    g, h_ = GA[:, k:k + 2, :], H2[:, k:k + 2, :]
                    c(stt(h_, h_, 1.0, g, ALU.add, ALU.mult))
                    c(stt(g, h_, 0.5, XL[:, k:k + 2, :], ALU.mult, ALU.mult))
                    split_tiles(r.sb + KD // 2 + q, k, g)

                dve.wait_ge(S("acd_ps"), 1)
                c(ts(ACD[:, 0:32], PS[:, 1, 0:32], -1.0))
                V.tensor_copy(ACD[:, 32:64], PS[:, 1, 32:64]).then_inc(S("acd"), 1)
                dve.wait_ge(S("acd"), 1)
                for t in range(TT):
                    for j in range(2):
                        dve.wait_ge(S("xs_ps"), 2 * t + j + 1)
                        tt(XN[:, t, 512 * j:512 * j + 512].rearrange("p (h d) -> p h d", h=8),
                           PS[:, 4 + 2 * t + j, :].rearrange("p (h d) -> p h d", h=8),
                           bc(ACD[:, 32 + 16 * t + 8 * j:32 + 16 * t + 8 * j + 8].unsqueeze(2), (P, 8, 64)))\
                            .then_inc(S("xd"), 1)
                for g in range(2):
                    dve.wait_ge(S("cb_ps"), g + 1)
                    tt(CBM[:, g, :], PS[:, 2 + g, 0:MW], CON[:, C_TRIT:C_TRIT + MW]).then_inc(S("cbm"), 1)
                dve.wait_ge(S("cbm"), 2)

                def ys(k):
                    dve.wait_ge(S("head_ps"), 2 * k + 2)
                    stt(XBC[:, k, :], XBC[:, k, :], SSDD[:, k:k + 1], PS[:, 6 + k % 2, 0:T], ALU.mult, ALU.add)\
                        .then_inc(S("ys"), 1)

                def gated(g):
                    dve.wait_ge(S("ys"), 4 * (g + 1))
                    dve.wait_ge(S("zsilu"), 1)
                    z, y = ZH[:, 4 * g:4 * g + 4, :], XBC[:, 4 * g:4 * g + 4, :]
                    c(tt(z, z, y))
                    tt(y, z, z).then_inc(S("sq"), 1)

                def mean_square(g):
                    dve.wait_ge(S("sq_ps"), g + 1)
                    ts(H2_RS[:, g, :], PS[:, 4, 0:T], 1.0 / 512, EPS, ALU.mult, ALU.add).then_inc(S("sq_out"), 1)
                    dve.wait_ge(S("sq_out"), g + 1)

                for h in range(17):
                    if h < 16:
                        dve.wait_ge(S("eh"), 2 * (h + 1))
                        tt(EH[:, h % 2, :], EH[:, h % 2, :], CBM[:, h // 8, :]).then_inc(S("mt"), 1)
                    if h in (2, 4, 6, 8):
                        gelu(h // 2 - 1)
                    if h in (7, 10):
                        low(r, r.n_proj + h // 3)
                    if h >= 3 and h % 2 == 1:
                        ys((h - 3) // 2)
                    if h == 9:
                        gated(0)
                    if h == 11:
                        mean_square(0)
                    if h == 14:
                        low(r, r.n_proj + 4)
                ys(7)
                gated(1)

                def normed(g):
                    root(H2_RS[:, g, :], H2_RS[:, g, :])
                    for k in range(4 * g, 4 * g + 4):
                        c(stt(ZH[:, k, :], ZH[:, k, :], col("ssd_norm_g_2", k), H2_RS[:, g, :], ALU.mult, ALU.mult))
                        if k % 2 == 1:
                            dve.wait_ge(S("w_used"), r.used[r.n_proj + k // 2])
                            split_tiles(r.sb + KD + k // 2, k - 1, ZH[:, k - 1:k + 1, :])

                normed(0)
                mean_square(1)
                low(r, r.n_proj + 5)
                normed(1)
                low(r, r.n_proj + 6)
                low(r, r.n_proj + 7)
                residual_gate(r)

            def mlstm(r):
                begin(r)
                c(V.memset(XM[:, :, 0:3], 0.0))
                split_x(r)
                first_low(r, 1)
                diagonals(r)
                for k in range(16):
                    if k % 2 == 0:
                        low(r, k // 2 + 2)
                    dve.wait_ge(S("tile_out"), EV_BASE["mlstm"] + k + 1)
                    conv4(XC[:, k, :], XM[:, k, :], "mlstm_conv_w_2", "mlstm_conv_b_2", 16, k, "mconv")
                dve.wait_ge(S("mconv"), 16)

                for p in range(10, r.n_proj + 2):
                    low(r, p)
                dve.wait_ge(S("gadd"), 48)
                F_, NMR, G_, MR_ = (MR[0:4, k, :] for k in range(4))
                x_ = SPX[4]
                dve.wait_ge(S("f_row"), 1)
                c(ts(x_, x_, -1.0, BF[0:4, 4:5], ALU.mult, ALU.subtract))
                softplus(SPX[5], x_, *SPX[0:4])
                c(ts(SPX[5], SPX[5], -1.0))
                c(V.tensor_tensor_scan(F_, ONES[0:4, :], SPX[5], 0.0, ALU.mult, ALU.add))
                c(stt(G_, PS[0:4, 6, 0:T], BF[0:4, 3:4], F_, ALU.add, ALU.subtract))
                c(V.tensor_tensor_scan(x_, ONES[0:4, :], G_, 0.0, ALU.mult, ALU.max))
                c(tt(MR_, F_, x_, ALU.add))
                c(ts(NMR, x_, -1.0))
                mark().then_inc(S("gtok_in"), 1)
                dve.wait_ge(S("gtok_ps"), 1)
                V.tensor_copy(GTOK.rearrange("p m t h -> p (m t h)"), PS[:, 7, 0:16]).then_inc(S("gtok"), 1)
                dve.wait_ge(S("gtok"), 1)

                def probs(h):
                    dve.wait_ge(S("em_exp"), 2 * (h + 1))
                    dve.wait_ge(S("kq_ps"), h + 1)
                    stt(PM, PS[:, 5, 0:MW], 512 ** -0.5, EM, ALU.mult, ALU.mult).then_inc(S("pm"), 1)

                def out_split(q):
                    low(r, r.n_proj + q + 2)
                    dve.wait_ge(S("w_used"), r.used[r.n_proj + q])
                    split_tiles(r.sb + KD + q, 2 * q, ZM[:, KD + 2 * q:KD + 2 * q + 2, :])

                probs(0)
                for h in range(4):
                    dve.wait_ge(S("num_ps"), h + 1)
                    dve.wait_ge(S("enm"), 1)
                    den = PS[:, 4, MW:MW + 2]
                    c(ts(DEN, den, -1.0))
                    tt(DEN, DEN, den, ALU.max).then_inc(S("den_read"), 1)
                    dve.wait_ge(S("den_read"), h + 1)
                    c(tt(DEN, DEN, ENM[:, :, h], ALU.max))
                    c(V.reciprocal(DEN, DEN))
                    for t in range(TT):
                        c(ts(HN[:, t, :], PS[:, 6 + t, :], DEN[:, t:t + 1]))
                        c(V.bn_stats(BN[:, t, 0, :], HN[:, t, :]))
                        c(V.bn_aggr(MV[:, t, :], BN[:, t, 0, :]))
                    c(ts(VAR, MV[:, :, 1], EPS, None, ALU.add))
                    root(RSTD, SD)
                    for t in range(TT):
                        c(ts(HN[:, t, :], HN[:, t, :], MV[:, t, 0:1], RSTD[:, t:t + 1], ALU.subtract, ALU.mult))
                    mark().then_inc(S("hn"), 1)
                    if h < 3:
                        probs(h + 1)
                    if h == 3:
                        out_split(0)
                    dve.wait_ge(S("hn_ps"), h + 1)
                    dve.wait_ge(S("zm"), 1)
                    for j in range(4):
                        k = 4 * h + j
                        c(ts(XC[:, k, :], XC[:, k, :], col("mlstm_skip_2", k)))
                        c(stt(XC[:, k, :], PS[:, NORMED_BANK[h] + j // 2, (j % 2) * T:(j % 2 + 1) * T],
                              col("mlstm_norm_g_2", k),
                              XC[:, k, :], ALU.mult, ALU.add))
                        c(tt(ZM[:, k, :], ZM[:, k, :], XC[:, k, :]))
                    mark().then_inc(S("ym_read"), 1)
                    if h == 2:
                        for k in range(0, KD, 2):
                            split_tiles(r.sb + KD // 2 + k // 2, k, ZM[:, k:k + 2, :])
                for q in range(1, 4):
                    out_split(q)
                low(r, r.n_proj + 6)
                low(r, r.n_proj + 7)
                residual_gate(r)

            def final():
                squares()
                dve.wait_ge(S("fin_load"), 16)
                for t in range(TT):
                    c(ts(XN[:, t, :], X[:, t, :], RSTD[:, t:t + 1]))
                    c(tt(XN[:, t, :], XN[:, t, :], ROWB[:, 1, :]))
                mark().then_inc(S("final"), 1)

            c(V.memset(ONES[:, :], 1.0))
            dve.wait_ge(S("con_load"), 16)
            if plan[0].kind != "even":
                columns()
            for r in plan:
                {"even": even, "odd": odd, "moe": moe, "mod": mod, "ffn": ffn, "hyb": hyb, "mlstm": mlstm}[r.kind](r)
            if FINAL:
                final()
            else:
                for t in range(TT):
                    c(V.tensor_copy(XN[:, t, :], X[:, t, :]))
                mark().then_inc(S("final"), 1)


def kernel(**inputs):
    import concourse.bacc as bacc
    from concourse.bass_utils import run_bass_kernel_spmd

    nc = bacc.Bacc("TRN2", target_bir_lowering=False, num_devices=1)
    arrays = {name: np.ascontiguousarray(x) for name, x in inputs.items()}
    arrays["const"] = constants()
    aps = {name: nc.dram_tensor(f"in_{name}", x.shape, mybir.dt.from_np(x.dtype), kind="ExternalInput").ap()
           for name, x in arrays.items()}
    out = nc.dram_tensor("out", (1, T, D), F32, kind="ExternalOutput").ap()
    program(nc, aps, out)
    r = run_bass_kernel_spmd(nc, [{f"in_{name}": x for name, x in arrays.items()}], core_ids=[0])
    return r.results[0]["out"]
```
